# Optimizing a Trainium2 kernel written in Bass

```python
import jax, jax.numpy as jnp
from jax import lax
import numpy as np

D_MODEL = 1024
BATCH = 1
SEQ = 1024
DEPTH = 1

CHUNK = 64
PLE_DIM = 256
EPS = 1e-6

A_HEADS = 8
A_HEAD_DIM = 64
A_WIDTH = A_HEADS * A_HEAD_DIM
A_LOOKBACK = 8
A_BAND = A_LOOKBACK + 1
REL_CLIP = 128
N_REL = 2 * REL_CLIP + 1

B_HEADS = 4
B_KEY_DIM = 128
B_VAL_DIM = 128
B_QK_WIDTH = B_HEADS * B_KEY_DIM
B_V_WIDTH = B_HEADS * B_VAL_DIM
CONV_WIDTH = 4
B_CONV_CH = 2 * B_QK_WIDTH + B_V_WIDTH

D_FF = ((8 * D_MODEL // 3 + 255) // 256) * 256

N_BRANCH = 2
SPLIT_A = 3 * A_WIDTH
SPLIT_CONV = SPLIT_A + B_CONV_CH
SPLIT_Z = SPLIT_CONV + B_V_WIDTH
SPLIT_BETA = SPLIT_Z + B_HEADS
SPLIT_DECAY = SPLIT_BETA + B_HEADS
D_IN = SPLIT_DECAY + N_BRANCH * D_MODEL

kernel_name = "hybrid_chunked_attn_gated_deltanet_block"

def rmsnorm(x, g):
    xf = x.astype(jnp.float32)
    y = xf * lax.rsqrt(jnp.mean(xf * xf, axis=-1, keepdims=True) + EPS)
    return (y * g.astype(jnp.float32)).astype(x.dtype)

def l2norm(x):
    return x * lax.rsqrt(jnp.sum(x * x, axis=-1, keepdims=True) + EPS)

def causal_depthwise_conv(x, w):
    s = x.shape[1]
    k = w.shape[0]
    xp = jnp.pad(x, ((0, 0), (k - 1, 0), (0, 0)))
    out = xp[:, 0:s] * w[0]
    for i in range(1, k):
        out = out + xp[:, i:i + s] * w[i]
    return out

def chunked_band_attention(q, k, v, rel_bias):
    b, s, h, d = q.shape
    nc = s // CHUNK
    qc = q.reshape(b, nc, CHUNK, h, d) * (d ** -0.5)
    pad = ((0, 0), (A_LOOKBACK, 0), (0, 0), (0, 0), (0, 0))
    kc = jnp.pad(k.reshape(b, nc, CHUNK, h, d), pad)
    vc = jnp.pad(v.reshape(b, nc, CHUNK, h, d), pad)
    scores = jnp.stack(
        [jnp.einsum('bnqhd,bnkhd->bhnqk', qc, kc[:, j:j + nc]) for j in range(A_BAND)],
        axis=4)
    scores = scores.reshape(b, h, nc, CHUNK, A_BAND * CHUNK).astype(jnp.float32)
    qi = jnp.arange(CHUNK)
    kj = jnp.arange(A_BAND * CHUNK)
    rel = (A_LOOKBACK * CHUNK + qi[:, None]) - kj[None, :]
    idx = jnp.clip(rel, -REL_CLIP, REL_CLIP) + REL_CLIP
    bias = rel_bias[:, idx].astype(jnp.float32)
    valid = (jnp.arange(nc)[:, None] + jnp.arange(A_BAND)[None, :]) >= A_LOOKBACK
    valid = jnp.repeat(valid, CHUNK, axis=1)
    scores = jnp.where(valid[None, None, :, None, :], scores + bias[None, :, None], -1e30)
    probs = jax.nn.softmax(scores, axis=-1).astype(v.dtype)
    probs = probs.reshape(b, h, nc, CHUNK, A_BAND, CHUNK)
    out = jnp.einsum('bhnqk,bnkhd->bnqhd', probs[:, :, :, :, 0], vc[:, 0:nc])
    for j in range(1, A_BAND):
        out = out + jnp.einsum('bhnqk,bnkhd->bnqhd', probs[:, :, :, :, j], vc[:, j:j + nc])
    return out.reshape(b, s, h * d)

def gated_delta_rule(q, k, v, g, beta):
    out_dtype = v.dtype
    f32 = jnp.float32
    b, s, h, dk = q.shape
    dv = v.shape[-1]
    nc = s // CHUNK
    L = CHUNK

    def to_chunks(t):
        return jnp.moveaxis(t.reshape((b, nc, L, h) + t.shape[3:]), 3, 1)

    q = to_chunks(l2norm(q.astype(f32)) * (dk ** -0.5))
    k = to_chunks(l2norm(k.astype(f32)))
    v = to_chunks(v.astype(f32))
    g = to_chunks(g.astype(f32))
    beta = to_chunks(beta.astype(f32))

    gc = jnp.cumsum(g, axis=-1)
    ti = jnp.arange(L)
    tri_incl = ti[:, None] >= ti[None, :]
    tri_strict = ti[:, None] > ti[None, :]
    diff = gc[..., :, None] - gc[..., None, :]
    decay = jnp.exp(jnp.where(tri_incl, diff, -jnp.inf))
    kk = jnp.einsum('bhnid,bhnjd->bhnij', k, k)
    a_mat = jnp.where(tri_strict, beta[..., :, None] * kk * decay, 0.0)
    eye = jnp.eye(L, dtype=f32)
    rhs = jnp.concatenate([beta[..., None] * v,
                           (beta * jnp.exp(gc))[..., None] * k], axis=-1)
    sol = lax.linalg.triangular_solve(eye + a_mat, rhs, left_side=True,
                                      lower=True, unit_diagonal=True)
    u, wk = sol[..., :dv], sol[..., dv:]
    pqk = jnp.einsum('bhnid,bhnjd->bhnij', q, k) * decay
    gamma = jnp.exp(gc)
    g_last = gc[..., -1]
    kdec = k * jnp.exp(g_last[..., None] - gc)[..., None]

    def front(t):
        return jnp.moveaxis(t, 2, 0)

    xs = (front(u), front(wk), front(q), front(pqk), front(gamma), front(kdec), front(g_last))

    def step(state, inp):
        u_c, wk_c, q_c, p_c, gam_c, kd_c, gl_c = inp
        w = u_c - jnp.einsum('bhld,bhvd->bhlv', wk_c, state)
        o = gam_c[..., None] * jnp.einsum('bhld,bhvd->bhlv', q_c, state) \
            + jnp.einsum('bhts,bhsv->bhtv', p_c, w)
        state = jnp.exp(gl_c)[..., None, None] * state + jnp.einsum('bhlv,bhld->bhvd', w, kd_c)
        return state, o

    s0 = jnp.zeros((b, h, dv, dk), f32)
    _, o = lax.scan(step, s0, xs)
    o = jnp.transpose(o, (1, 0, 3, 2, 4)).reshape(b, s, h, dv)
    return o.astype(out_dtype)

def setup_inputs(seed: int = 0) -> dict:
    key = jax.random.key(seed)
    ks = jax.random.split(key, 24)
    f32 = jnp.float32

    def nrm(k, shape, scale):
        return jax.random.normal(k, shape, f32) * scale

    def gain(k, shape):
        return 1.0 + 0.1 * jax.random.normal(k, shape, f32)

    x = jax.random.normal(ks[0], (BATCH, SEQ, D_MODEL), f32)
    p = jax.random.normal(ks[1], (DEPTH, BATCH, SEQ, PLE_DIM), f32)
    g_mix = gain(ks[2], (DEPTH, D_MODEL))
    w_in = nrm(ks[3], (DEPTH, D_MODEL, D_IN), D_MODEL ** -0.5)
    conv_w = nrm(ks[4], (DEPTH, CONV_WIDTH, B_CONV_CH), CONV_WIDTH ** -0.5)
    a_log = jnp.log(jax.random.uniform(ks[5], (DEPTH, B_HEADS), f32, 1.0, 16.0))
    dt = jnp.exp(jax.random.uniform(ks[6], (DEPTH, B_HEADS), f32,
                                    np.log(1e-3), np.log(1e-1)))
    dt_bias = dt + jnp.log(-jnp.expm1(-dt))
    rel_bias = nrm(ks[7], (DEPTH, A_HEADS, N_REL), 0.1)
    w_onorm = gain(ks[8], (DEPTH, B_VAL_DIM))
    w_branch_a = nrm(ks[9], (DEPTH, A_WIDTH, D_MODEL), A_WIDTH ** -0.5)
    w_branch_b = nrm(ks[10], (DEPTH, B_V_WIDTH, D_MODEL), B_V_WIDTH ** -0.5)
    w_out = nrm(ks[11], (DEPTH, D_MODEL, D_MODEL), D_MODEL ** -0.5)
    g_ffn = gain(ks[12], (DEPTH, D_MODEL))
    w_gate_up = nrm(ks[13], (DEPTH, D_MODEL, 2 * D_FF), D_MODEL ** -0.5)
    w_down = nrm(ks[14], (DEPTH, D_FF, D_MODEL), D_FF ** -0.5)
    g_ple = gain(ks[15], (DEPTH, D_MODEL))
    w_ple_gate = nrm(ks[16], (DEPTH, D_MODEL, D_MODEL), D_MODEL ** -0.5)
    w_ple_proj = nrm(ks[17], (DEPTH, PLE_DIM, D_MODEL), PLE_DIM ** -0.5)
    g_final = gain(ks[18], (D_MODEL,))
    return {"x": x, "p": p, "g_mix": g_mix, "w_in": w_in, "conv_w": conv_w,
            "a_log": a_log, "dt_bias": dt_bias, "rel_bias": rel_bias, "w_onorm": w_onorm,
            "w_branch_a": w_branch_a, "w_branch_b": w_branch_b, "w_out": w_out,
            "g_ffn": g_ffn, "w_gate_up": w_gate_up, "w_down": w_down,
            "g_ple": g_ple, "w_ple_gate": w_ple_gate, "w_ple_proj": w_ple_proj,
            "g_final": g_final}

def reference(x, p, g_mix, w_in, conv_w, a_log, dt_bias, rel_bias, w_onorm,
              w_branch_a, w_branch_b, w_out, g_ffn, w_gate_up, w_down,
              g_ple, w_ple_gate, w_ple_proj, g_final):
    b, s, _ = x.shape
    for i in range(DEPTH):
        h = rmsnorm(x, g_mix[i])
        proj = h @ w_in[i]
        qkv_a = proj[..., :SPLIT_A]
        conv_in = proj[..., SPLIT_A:SPLIT_CONV]
        z = proj[..., SPLIT_CONV:SPLIT_Z]
        beta_raw = proj[..., SPLIT_Z:SPLIT_BETA]
        decay_raw = proj[..., SPLIT_BETA:SPLIT_DECAY]
        gates = proj[..., SPLIT_DECAY:]

        q_a = qkv_a[..., :A_WIDTH].reshape(b, s, A_HEADS, A_HEAD_DIM)
        k_a = qkv_a[..., A_WIDTH:2 * A_WIDTH].reshape(b, s, A_HEADS, A_HEAD_DIM)
        v_a = qkv_a[..., 2 * A_WIDTH:].reshape(b, s, A_HEADS, A_HEAD_DIM)
        y_a = chunked_band_attention(q_a, k_a, v_a, rel_bias[i])

        c = jax.nn.silu(causal_depthwise_conv(conv_in, conv_w[i]))
        q_b = c[..., :B_QK_WIDTH].reshape(b, s, B_HEADS, B_KEY_DIM)
        k_b = c[..., B_QK_WIDTH:2 * B_QK_WIDTH].reshape(b, s, B_HEADS, B_KEY_DIM)
        v_b = c[..., 2 * B_QK_WIDTH:].reshape(b, s, B_HEADS, B_VAL_DIM)
        beta = jax.nn.sigmoid(beta_raw)
        g = -jnp.exp(a_log[i]) * jax.nn.softplus(decay_raw + dt_bias[i])
        o_b = gated_delta_rule(q_b, k_b, v_b, g, beta)
        o_b = rmsnorm(o_b, w_onorm[i]) * jax.nn.silu(z.reshape(b, s, B_HEADS, B_VAL_DIM))
        y_b = o_b.reshape(b, s, B_V_WIDTH)

        gate_a = jax.nn.sigmoid(gates[..., :D_MODEL])
        gate_b = jax.nn.sigmoid(gates[..., D_MODEL:])
        merged = gate_a * (y_a @ w_branch_a[i]) + gate_b * (y_b @ w_branch_b[i])
        x = x + merged @ w_out[i]

        h = rmsnorm(x, g_ffn[i])
        gu = h @ w_gate_up[i]
        x = x + (jax.nn.silu(gu[..., :D_FF]) * gu[..., D_FF:]) @ w_down[i]

        ple_gate = jax.nn.sigmoid(rmsnorm(x, g_ple[i]) @ w_ple_gate[i])
        x = x + ple_gate * (p[i] @ w_ple_proj[i])
    return rmsnorm(x, g_final)


_drawn_inputs = setup_inputs


def setup_inputs(seed=0):
    import zlib

    import numpy as np

    out = dict(_drawn_inputs(seed))
    spreads = {}
    factors = {'rel_bias': 8.0, 'g_ple': 3.601}
    for name, (base, spread) in spreads.items():
        noise = np.random.default_rng([zlib.crc32(name.encode()), seed]).standard_normal(out[name].shape)
        drawn = base * np.exp(spread * noise) if base else spread * noise
        out[name] = __import__('jax').numpy.asarray(drawn.astype(out[name].dtype))
    for name, factor in factors.items():
        out[name] = (out[name] * factor).astype(out[name].dtype)
    return out
```

```python
import numpy as np
import concourse.bass as bass
from concourse import mybir
from contextlib import ExitStack

S, D, P = 1024, 1024, 128
KT = D // P
HALF = 512
TOK_TILES = S // P
CHUNK = 64
A_HEADS, A_DIM, LOOKBACK, REL_CLIP = 8, 64, 8, 128
PAIRS = A_HEADS // 2
WINDOW = 5 * P
B_HEADS, B_DIM = 4, 128
CONV = 4
D_FF = 2816
GROUPS = D_FF // (2 * P)
EPS = 1e-6
NEG = -1e30

C_IDENT, C_ONES, C_CUM, C_CHUNK, C_MASK, C_LEVEL = 0, 128, 256, 384, 512, 640
LEVELS = (1, 2, 4, 8, 16, 32)
C_EPS = C_LEVEL + 128 * len(LEVELS)
C_QKS = C_EPS + 1
N_CONST = C_QKS + 12
P_GMIX, P_GFFN, P_GPLE, P_GFIN, P_CONV = 0, 8, 16, 24, 32
P_ONORM = P_CONV + 12 * CONV
P_ALOG, P_DTB = P_ONORM + 1, P_ONORM + 5
P_WBD = P_ONORM + 9
N_PARAM = P_WBD + 64

BLK_B, BLK_A, BLK_Z, BLK_M = 0, 12, 24, 28
BLK_O = BLK_M + 3 * 8
BLK_F = BLK_O + 8
BLK_PP = BLK_F + 6 * GROUPS
BLK_PG = BLK_PP + 2
N_BLK = BLK_PG + 8
JOB_B, JOB_A, JOB_Z, JOB_M = 0, 12, 24, 28
JOB_O = JOB_M + 4 * 8
JOB_F = JOB_O + 8
JOB_T = JOB_F + 4 + 12 * (GROUPS - 1)
JOB_P = JOB_T + 8


def ffn_jobs(i):
    if isinstance(i, int) and i == 0:
        return [JOB_F + c for c in range(4)], []
    base = JOB_F + 4 + (i - 1) * 12
    return [base + 3 * c for c in range(4)], [base + 3 * (n // 2) + 1 + n % 2 for n in range(8)]


def hybrid_block(nc, x_t, p_t, blocks, consts_d, params_d, bias_d, out_t):
    f32, f32r = mybir.dt.float32, mybir.dt.float32r
    ALU, ACT, AX = mybir.AluOpType, mybir.ActivationFunctionType, mybir.AxisListType
    ds = bass.ds

    ctx = ExitStack()
    with ctx:
        BASE = 16512
        K = 1024

        def at(name, shape, dt, offset):
            return nc.alloc_sbuf_tensor_at(name, shape, dt, offset=BASE + offset)

        def sem(name):
            return ctx.enter_context(nc.semaphore(name))

        h_hi = at("h_hi", [P, 8, S], f32r, 0)
        h_lo = at("h_lo", [P, 8, S], f32r, 32 * K)
        mg_hi = at("mg_hi", [P, 8, S], f32r, 0)
        mg_lo = at("mg_lo", [P, 8, S], f32r, 32 * K)
        hid_hi = [at(f"hid_hi{g}", [P, 2, S], f32r, 32 * K * g) for g in range(2)]
        hid_lo = [at(f"hid_lo{g}", [P, 2, S], f32r, 32 * K * g + 8 * K) for g in range(2)]
        dw_hi = [at(f"dw_hi{g}", [P, 2, S], f32r, 32 * K * g + 16 * K) for g in range(2)]
        dw_lo = [at(f"dw_lo{g}", [P, 2, S], f32r, 32 * K * g + 24 * K) for g in range(2)]
        out_sb = at("out_sb", [P, 8, S], f32, 0)
        ya_hi = at("ya_hi", [P, 4, S], f32r, 64 * K)
        ya_lo = at("ya_lo", [P, 4, S], f32r, 80 * K)
        yb_hi = at("yb_hi", [P, 4, S], f32r, 96 * K)
        yb_lo = at("yb_lo", [P, 4, S], f32r, 112 * K)
        h2_hi = at("h2_hi", [P, 8, S], f32r, 64 * K)
        h2_lo = at("h2_lo", [P, 8, S], f32r, 96 * K)
        mixb = at("mixb", [P, 12, S], f32, 96 * K)
        x_sb = at("x_sb", [P, 8, S], f32, 128 * K)
        merged = at("merged", [P, 8, S], f32, 128 * K)
        raw = [at(f"raw{s}", [P, 1024], f32, 160 * K + 4 * K * s) for s in range(2)]
        w_hi = [at(f"w_hi{s}", [P, 8, P], f32r, 168 * K + 8 * K * s) for s in range(2)]
        w_lo = [at(f"w_lo{s}", [P, 8, P], f32r, 172 * K + 8 * K * s) for s in range(2)]
        consts = at("consts", [P, N_CONST], f32, 184 * K)
        params = at("params", [P, N_PARAM], f32, 190 * K)
        rstd = at("rstd", [P, S], f32, 191 * K)
        tmp = [at(f"tmp{n}", [P, HALF], f32, 195 * K + 2 * K * n) for n in range(6)]
        small = 207 * K
        off = [small]

        def tiny(name, n, dt=f32):
            off[0] += 32
            return at(name, [P, n], dt, off[0] - 32)

        nmax = tiny("nmax", 4)
        psum_row = tiny("psum_row", 4)
        rsum = tiny("rsum", 4)
        rstd_tok = tiny("rstd_tok", 8)

        neg_a = tiny("neg_a", 4)
        assert off[0] <= 212848
        sq = [at(f"sq{n}", [P, S], f32, 64 * K + 4 * K * n) for n in range(2)]
        sumsq = at("sumsq", [P, S], f32, 72 * K)
        sumsq2 = at("sumsq2", [P, S], f32, 203 * K)
        convin = at("convin", [P, S + 4], f32, 76 * K)
        conv = [at(f"conv{n}", [P, S], f32, 81 * K + 4 * K * n) for n in range(2)]
        lnb = at("lnb", [P, S], f32, 89 * K)
        inv_l2 = at("inv_l2", [P, S], f32, 64 * K)
        sqv = at("sqv", [P, S], f32, 68 * K)
        spots = [64 * K + 2 * K * n for n in range(16)] + [144 * K + 2 * K * n for n in range(8)]
        spot = iter(spots)

        def four(name):
            return at(name, [P, 4, P], f32, next(spot))

        (kn, vn, gb, gamb, dtmp, decT, pT_, aT, qg, gk, kdec, vtok, T, TT, Ns, nwk, w_, state) = (
            four(n) for n in "kn vn gb gamb dtmp decT pT aT qg gk kdec vtok T TT Ns nwk w state".split())
        aoff = [four(f"aoff{b}") for b in LEVELS[1:]]
        gates8 = at("gates8", [P, 8, 8], f32, 93 * K)
        sp_a = at("sp_a", [P, 8, 4], f32, 93 * K + 256)
        sp_b = at("sp_b", [P, 8, 4], f32, 93 * K + 384)
        beta = at("beta", [P, 32], f32, 203 * K)
        g_log = at("g_log", [P, 32], f32, 203 * K + 128)
        neg_gc = at("neg_gc", [P, 32], f32, 203 * K + 256)
        gam = at("gam", [P, 32], f32, 203 * K + 384)
        kds = at("kds", [P, 32], f32, 203 * K + 512)
        gdiff = at("gdiff", [P, 32], f32, 203 * K + 640)
        wbd_hi = at("wbd_hi", [P, 64], f32r, 204 * K)
        wbd_lo = at("wbd_lo", [P, 64], f32r, 204 * K + 256)
        qa = at("qa", [P, S], f32, 144 * K)
        ka = at("ka", [P, S], f32, 148 * K)
        va = at("va", [P, S], f32, 152 * K)
        va_tok = at("va_tok", [P, 8, P], f32, 156 * K)
        biast = [at(f"biast{n}", [P, WINDOW], f32, 96 * K + 2560 * n) for n in range(2)]
        sc = [at(f"sc{n}", [P, WINDOW], f32, 102 * K + 2560 * n) for n in range(2)]
        pr = [at(f"pr{n}", [P, WINDOW], f32, 107 * K + 2560 * n) for n in range(2)]
        prT = [at(f"prT{n}", [P, WINDOW], f32, 112 * K + 2560 * n) for n in range(2)]
        ytok = [at(f"ytok{n}", [P, P], f32, 118 * K + 512 * n) for n in range(2)]
        osq = at("osq", [P, S], f32, 144 * K)
        oln = at("oln", [P, S], f32, 148 * K)
        oinv = at("oinv", [P, S], f32, 152 * K)
        p_raw = at("p_raw", [P, 2, S], f32, 40 * K)

        ident = consts[:, C_IDENT:C_IDENT + P]
        ones = consts[:, C_ONES:C_ONES + P]
        cum = consts[:, C_CUM:C_CUM + P]
        chunk_ones = consts[:, C_CHUNK:C_CHUNK + P]
        decay_mask = consts[:, C_MASK:C_MASK + P]
        level = [consts[:, C_LEVEL + P * n:C_LEVEL + P * (n + 1)] for n in range(len(LEVELS))]
        eps_col = consts[:, C_EPS:C_EPS + 1]

        def heads(a):
            return a.unsqueeze(1).to_broadcast([P, 4, P])

        acc = [ctx.enter_context(nc.psum_tensor(f"acc{n}", [P, HALF], f32)) for n in range(2)]
        pair_a = ctx.enter_context(nc.psum_tensor("pair_a", [P, 1024], f32))
        pair_b = ctx.enter_context(nc.psum_tensor("pair_b", [P, 1024], f32))
        one = [ctx.enter_context(nc.psum_tensor(f"one{n}", [P, HALF], f32)) for n in range(2)]

        def bank(n):
            t = (pair_a, pair_a, pair_b, pair_b, one[0], one[1])[n]
            c = (0, HALF, 0, HALF, 0, 0)[n]
            return t[:, c:c + HALF]

        def bank4(n):
            return bank(n).rearrange("p (h i) -> p h i", h=4)

        def sems(names):
            return [sem(n) for n in names.split()]

        smalls_loaded, hi_made, lo_made, acc_ready = sems("smalls_loaded hi_made lo_made acc_ready")
        x_loaded = [sem(f"x_loaded{k}") for k in range(8)]
        raw_loaded = [sem(f"raw_loaded{s}") for s in range(2)]
        acc_read = [sem(f"acc_read{s}") for s in range(2)]
        norm_hi, norm_lo, sq_made, sq_added, stat_ready, rstd_ready = sems(
            "norm_hi norm_lo sq_made sq_added stat_ready rstd_ready")
        sq0_made, sq0_added, tok_stat, tok_rstd = sems("sq0_made sq0_added tok_stat tok_rstd")
        conv_done, silu_done, l2_sq, l2_sum, l2_ln, l2_inv, l2_done = sems(
            "conv_done silu_done l2_sq l2_sum l2_ln l2_inv l2_done")
        wbd_split, bd_ready, bd_scaled, bd_exp, bd_sum, bd_ln, neg_a_made, g_made, gc_ready, gc_read, gc_made = sems(
            "wbd_split bd_ready bd_scaled bd_exp bd_sum bd_ln neg_a_made g_made gc_ready gc_read gc_made")
        (tiles_in, gb_made, gcb_ready, kk_ready, tok_ready, gamb_made, dtmp_made, dec_made, aT_made, vtok_made,
         keys_made, tt0_made, t0_ready, t0_made, aoff_made, n_ready, n_made, tn_ready, t_updated, wk_ready, nwk_made,
         wv_ready, w_made, o_ready, ds_ready, state_made, o_made, state_init) = sems(
            "tiles_in gb_made gcb_ready kk_ready tok_ready gamb_made dtmp_made dec_made aT_made vtok_made "
            "keys_made tt0_made t0_ready t0_made aoff_made n_ready n_made tn_ready t_updated wk_ready nwk_made "
            "wv_ready w_made o_ready ds_ready state_made o_made state_init")
        bias_loaded = sems("bias_loaded0 bias_loaded1")
        (qkv_made, vt_ready, vt_made, sc_ready, sc_read, max_made, pr_made, prT_ready, prT_made, oa_ready, ya_norm,
         yT_ready, yT_hi, yT_lo) = sems(
            "qkv_made vt_ready vt_made sc_ready sc_read max_made pr_made prT_ready prT_made oa_ready ya_norm "
            "yT_ready yT_hi yT_lo")
        o_sq, o_sum, o_ln, o_inv, o_normed, z_silu, yb_made, yb_h, yb_l = sems(
            "o_sq o_sum o_ln o_inv o_normed z_silu yb_made yb_h yb_l")
        gate_sig, merged_made, mg_h, mg_l = sems("gate_sig merged_made mg_h mg_l")
        f_silu, f_scaled, f_hi, f_lo = sems("f_silu f_scaled f_hi f_lo")
        p_loaded, p_hi, p_lo, pg_sig, x4_made, out_made, out_stored = sems(
            "p_loaded p_hi p_lo pg_sig x4_made out_made out_stored")

        class Num:

            def __init__(self, reg, step, base):
                self.reg, self.step, self.base = reg, step, base

            def __add__(self, n):
                return Num(self.reg, self.step, self.base + n)

            @property
            def parity(self):
                return self.base % 2

            @property
            def value(self):
                return self.base if self.reg is None else self.reg * self.step + self.base

            @property
            def turn(self):
                return self.base // 2 if self.reg is None else self.reg * (self.step // 2) + self.base // 2

        def num(n):
            return Num(None, 0, n)

        def lin(reg, step, base):
            return base if reg is None else reg * step + base

        def flat(t):
            return t[:, :, :].rearrange("p a b -> p (a b)")

        def half_of(h):
            return slice(h * HALF, (h + 1) * HALF)

        def settle(eng):
            eng.wait_ge(smalls_loaded, 32)

        def split_hi(act, n, dst, free):
            act.wait_ge(raw_loaded[n.parity], (n.turn + 1) * 16)
            if free is not None:
                act.wait_ge(acc_ready, free)
            nc.scalar.activation(dst, raw[n.parity][:, :], ACT.Copy).then_inc(hi_made, 1)

        def split_lo(pool, n, dst, hi):
            pool.wait_ge(hi_made, (n + 1).value)
            nc.gpsimd.tensor_tensor(dst, raw[n.parity][:, :], hi.bitcast(f32), ALU.subtract).then_inc(lo_made, 1)

        def fetch_hi(act, n, s, free):
            split_hi(act, n, flat(w_hi[s % 2]), free)

        def fetch_lo(pool, n, s):
            split_lo(pool, n, flat(w_lo[s % 2]), flat(w_hi[s % 2]))

        def fetch_down_hi(act, n, g, free):
            for r in range(2):
                split_hi(act, n + r, dw_hi[g][:, r, :], free)

        def fetch_down_lo(pool, n, g):
            for r in range(2):
                split_lo(pool, n + r, dw_lo[g][:, r, :], dw_hi[g][:, r, :])

        def project(pe, job, w, src, ks, block_no=None, source_wait=None):
            if block_no is not None:
                pe.wait_ge(lo_made, (block_no + 1).value)
            for half in range(2):
                if not (isinstance(job, int) and job == 0):
                    pe.wait_ge(acc_read[half], job)
                for n, (kw, kx) in enumerate(ks):
                    if source_wait is not None and half == 0:
                        source_wait(n)
                    for a, b in ((0, 0), (0, 1), (1, 0)):
                        last = nc.tensor.matmul(acc[half][:, :], w[a](kw), src[b][:, kx, half_of(half)],
                                                start=(n == 0 and a == b), stop=(n == len(ks) - 1 and a == 1))
                last.then_inc(acc_ready, 1)

        def ring(s):
            return (lambda k: w_hi[s % 2][:, k, :]), (lambda k: w_lo[s % 2][:, k, :])

        def down_w(g, j):
            return (lambda r: dw_hi[g][:, r, j * P:(j + 1) * P]), (lambda r: dw_lo[g][:, r, j * P:(j + 1) * P])

        ALL = [(k, k) for k in range(8)]
        hx, h2x, mgx = (h_hi, h_lo), (h2_hi, h2_lo), (mg_hi, mg_lo)

        def job_done(eng, job, half):
            eng.wait_ge(acc_ready, job * 2 + (half + 1))

        def evacuated(eng, job, half):
            eng.wait_ge(acc_read[half], job + 1)

        def stat_sum(pe, ss):
            for half in range(2):
                last = nc.tensor.matmul(pair_a[:, half_of(half)], ones, ss[:, half_of(half)], start=True, stop=True)
            last.then_inc(stat_ready, 1)

        def stat_rstd(act, n, scratch):
            act.wait_ge(stat_ready, n)
            nc.scalar.activation(scratch[:, :], pair_a[:, :], ACT.Ln, bias=eps_col, scale=1.0 / D)
            act.drain()
            nc.scalar.activation(rstd[:, :], scratch[:, :], ACT.Exp, scale=-0.5).then_inc(rstd_ready, 1)

        def residual_hi(act, job, j, half, gcol, count):
            act.wait_ge(acc_read[half], job + 1)
            nc.scalar.activation(h2_hi[:, j, half_of(half)], x_sb[:, j, half_of(half)], ACT.Copy,
                                 scale=params[:, gcol + j:gcol + j + 1]).then_inc(norm_hi, 1)
            squares(act, j, half, count)

        def squares(act, j, half, count):
            c = count + 2 * j + half
            if c >= 2:
                act.wait_ge(sq_added, c - 1)
            nc.scalar.activation(tmp[half][:, :], x_sb[:, j, half_of(half)], ACT.Square).then_inc(sq_made, 1)

        def residual_lo(dve, j, half, gcol, count):
            dve.wait_ge(norm_hi, count + 2 * j + half + 1)
            nc.vector.scalar_tensor_tensor(h2_lo[:, j, half_of(half)], x_sb[:, j, half_of(half)],
                                           params[:, gcol + j:gcol + j + 1],
                                           h2_hi[:, j, half_of(half)].bitcast(f32), ALU.mult, ALU.subtract
                                           ).then_inc(norm_lo, 1)

        def add_squares(pool, j, half, count):
            c = count + 2 * j + half
            pool.wait_ge(sq_made, c + 1)
            if j == 0:
                nc.gpsimd.tensor_copy(sumsq2[:, half_of(half)], tmp[half][:, :]).then_inc(sq_added, 1)
            else:
                pool.wait_ge(sq_added, c - 1)
                nc.gpsimd.tensor_tensor(sumsq2[:, half_of(half)], sumsq2[:, half_of(half)], tmp[half][:, :],
                                        ALU.add).then_inc(sq_added, 1)

        block = ctx.enter_context(nc.Block())

        @block.sync
        def _(sp):
            sp.dma_start(consts[:, :], consts_d).then_inc(smalls_loaded, 16)
            sp.dma_start(params[:, :], params_d).then_inc(smalls_loaded, 16)
            for s in range(2):
                sp.dma_start(raw[s][:, :], blocks[s]).then_inc(raw_loaded[s], 16)
            with sp.Fori(1, N_BLK // 2) as i:
                for s in range(2):
                    sp.wait_ge(lo_made, i * 2 + (s - 1))
                    src = blocks[ds(i * 2 + s, 1)].rearrange("a p n -> (a p) n")
                    sp.dma_start(raw[s][:, :], src).then_inc(raw_loaded[s], 16)
            for j in range(8):
                sp.wait_ge(out_made, j + 1)
                sp.dma_start(out_t[j], out_sb[:, j, :]).then_inc(out_stored, 16)
            sp.wait_ge(out_stored, 16 * 8)

        @block.gpsimd
        def _(pool):
            g = nc.gpsimd
            fetch_lo(pool, num(0), 0)
            with pool.Fori(0, 6) as i:
                fetch_lo(pool, Num(i, 2, 1), 1)
                fetch_lo(pool, Num(i, 2, 2), 0)
            with pool.Fori(0, TOK_TILES) as t:
                pool.wait_ge(aT_made, t + 1)
                for n in range(5):
                    g.tensor_tensor(aoff[n][:, :, :], aT[:, :, :], heads(level[n + 1]), ALU.mult
                                    ).then_inc(aoff_made, 1)
            with pool.Fori(0, 2) as i:
                for q in range(2):
                    for c in range(3):
                        fetch_lo(pool, Num(i, 6, BLK_A + 3 * q + c + 1), 3 * q + c + 1)
                        if c == 0:
                            for hh in range(2):
                                src = bias_d[ds(i * 4 + (2 * q + hh), 1)].rearrange("a p n -> (a p) n")
                                pool.dma_start(biast[hh][:, :], src).then_inc(bias_loaded[hh], 16)
            for c in range(4):
                fetch_lo(pool, num(BLK_Z + c + 1), c + 1)
            with pool.Fori(0, 4) as i:
                for c in range(6):
                    fetch_lo(pool, Num(i, 6, BLK_M + c + 1), c + 1)
            for j in range(8):
                fetch_lo(pool, num(BLK_O + j + 1), j + 1)
                for half in range(2):
                    add_squares(pool, j, half, 0)

            def group(i, reg, gpar, step, last=False):
                n = Num(reg, 6 * step, BLK_F + 6 * i)
                for c in range(4):
                    if c < 3:
                        fetch_lo(pool, n + (c + 1), c + 1)
                    else:
                        fetch_down_lo(pool, n + 4, gpar)
                        if not last:
                            fetch_lo(pool, n + 6, 0)
                    if c % 2 == 0:
                        for half in range(2):
                            pool.wait_ge(f_silu, lin(reg, 4 * step, 4 * i + c + half + 1))
                            g.tensor_tensor(tmp[half][:, :], tmp[half][:, :], rstd[:, half_of(half)],
                                            ALU.mult).then_inc(f_scaled, 1)

            group(0, None, 0, 0)
            with pool.Fori(0, 4) as i:
                group(1, i, 1, 2)
                group(2, i, 0, 2)
            group(9, None, 1, 0)
            group(10, None, 0, 0, last=True)
            pool.wait_ge(acc_ready, 2 * JOB_T)
            pool.dma_start(p_raw[:, :, :], p_t.rearrange("k p n -> p k n")).then_inc(p_loaded, 16)
            fetch_down_lo(pool, num(BLK_PP), 1)
            fetch_lo(pool, num(BLK_PG), 0)
            for j in range(8):
                for half in range(2):
                    add_squares(pool, j, half, 16)
            for j in range(8):
                if j < 7:
                    fetch_lo(pool, num(BLK_PG + j + 1), j + 1)
                for half in range(2):
                    add_squares(pool, j, half, 32)

        @block.scalar
        def _(act):
            A = nc.scalar.activation
            for k in range(8):
                act.dma_start(x_sb[:, k, :], x_t[k]).then_inc(x_loaded[k], 16)
            act.wait_ge(smalls_loaded, 32)
            for k in range(8):
                act.wait_ge(x_loaded[k], 16)
                A(h_hi[:, k, :], x_sb[:, k, :], ACT.Copy, scale=params[:, P_GMIX + k:P_GMIX + k + 1]
                  ).then_inc(norm_hi, 1)
                if k >= 2:
                    act.wait_ge(sq0_added, k - 1)
                A(sq[k % 2][:, :], x_sb[:, k, :], ACT.Square).then_inc(sq0_made, 1)
                if k == 0:
                    fetch_hi(act, num(0), 0, None)
                if k == 1:
                    fetch_hi(act, num(1), 1, None)
            stat_rstd(act, 1, lnb)
            act.wait_ge(tok_stat, 1)
            A(rstd_tok[:, :], one[1][:, 0:8], ACT.Ln, bias=eps_col, scale=1.0 / D)
            act.drain()
            A(rstd_tok[:, :], rstd_tok[:, :], ACT.Exp, scale=-0.5).then_inc(tok_rstd, 1)
            A(neg_a[:, :], params[:, P_ALOG:P_ALOG + 4], ACT.Exp).then_inc(neg_a_made, 1)

            def l2_inverse(idx):
                act.wait_ge(l2_sum, idx + 1)
                A(lnb[:, :], pair_b[:, :], ACT.Ln, bias=eps_col).then_inc(l2_ln, 1)
                act.drain()
                if not (isinstance(idx, int) and idx == 0):
                    act.wait_ge(l2_done, idx)
                A(inv_l2[:, :], lnb[:, :], ACT.Exp, scale=-0.5).then_inc(l2_inv, 1)

            def conv_step(n, c, sq_job, inverse_prev):
                j = n.value
                if not (isinstance(j, int) and j == 0):
                    fetch_hi(act, n + 1, c + 1, j * 2)
                act.wait_ge(conv_done, j + 1)
                settle(act)
                A(mixb[:, j, :], conv[c][:, :], ACT.Silu).then_inc(silu_done, 1)
                if inverse_prev:
                    l2_inverse((n + -5).value)
                if sq_job:
                    act.drain()
                    A(sqv[:, :], mixb[:, j, :], ACT.Square).then_inc(l2_sq, 1)

            for j in range(2):
                conv_step(num(j), j, False, False)
            conv_step(num(2), 0, False, False)
            conv_step(num(3), 1, False, False)
            conv_step(num(4), 0, True, False)
            conv_step(num(5), 1, True, True)
            with act.Fori(3, 6) as i:
                conv_step(Num(i, 2, 0), 0, True, True)
                conv_step(Num(i, 2, 1), 1, True, True)
            l2_inverse(7)
            act.wait_ge(bd_scaled, 1)
            A(sp_a[:, :, :], gates8[:, :, 0:4], ACT.Exp, scale=-1.0)
            A(sp_b[:, :, :], gates8[:, :, 4:8], ACT.Exp, scale=-1.0)
            act.drain()
            A(sp_b[:, :, :], sp_b[:, :, :], ACT.Ln, bias=1.0).then_inc(bd_ln, 1)
            act.wait_ge(gc_ready, 1)
            A(gam[:, :], one[1][:, 0:32], ACT.Exp)
            A(neg_gc[:, :], one[1][:, 0:32], ACT.Copy, scale=-1.0).then_inc(gc_read, 1)
            act.wait_ge(gc_made, 1)
            A(kds[:, :], gdiff[:, :], ACT.Exp).then_inc(gc_read, 1)

            act.wait_ge(l2_done, 8)
            with act.Fori(0, TOK_TILES) as t:
                tok = ds(t * P, P)
                settle(act)
                A(kn[:, :, :], mixb[:, 4:8, tok], ACT.Copy).then_inc(tiles_in, 1)
                A(vn[:, :, :], mixb[:, 0:4, tok], ACT.Copy).then_inc(tiles_in, 1)
                act.wait_ge(gcb_ready, t + 1)
                A(gamb[:, :, :], bank4(0), ACT.Exp).then_inc(gamb_made, 1)
                act.wait_ge(dtmp_made, t + 1)
                settle(act)
                for h in range(4):
                    last = A(decT[:, h, :], dtmp[:, h, :], ACT.Exp, bias=neg_gc[:, ds(t * 4 + h, 1)])
                last.then_inc(dec_made, 1)
                act.wait_ge(tok_ready, t + 1)
                A(vtok[:, :, :], bank4(4), ACT.Copy).then_inc(vtok_made, 1)
                act.wait_ge(t0_ready, t + 1)
                A(T[:, :, :], bank4(5), ACT.Copy).then_inc(t0_made, 1)
                for n in range(5):
                    act.wait_ge(n_ready, t * 5 + (n + 1))
                    A(Ns[:, :, :], bank4(0), ACT.Copy).then_inc(n_made, 1)
                act.wait_ge(wk_ready, t + 1)
                A(nwk[:, :, :], bank4(3), ACT.Copy, scale=-1.0).then_inc(nwk_made, 1)
                act.wait_ge(o_ready, t + 1)
                settle(act)
                A(mixb[:, 8:12, tok], bank4(5), ACT.Copy).then_inc(o_made, 1)

            with act.Fori(0, 2) as i:
                for q in range(2):
                    p = i * 2 + q
                    for c in range(3):
                        n = Num(i, 6, BLK_A + 3 * q + c)
                        fetch_hi(act, n + 1, 3 * q + c + 1, n.value * 2)
                    act.wait_ge(vt_ready, p + 1)
                    A(flat(va_tok), pair_b[:, :], ACT.Copy).then_inc(vt_made, 1)
                    for u in range(19):
                        b, base = u % 2, p * 16
                        if u < 16:
                            width = P * min(u // 2 + 1, 5)
                            act.wait_ge(max_made, base + (u + 1))
                            if u >= 2:
                                act.wait_ge(prT_ready, base + (u - 1))
                            A(pr[b][:, :width], sc[b][:, :width], ACT.Exp, bias=nmax[:, b:b + 1],
                              accum_out=psum_row[:, u % 4:u % 4 + 1]).then_inc(pr_made, 1)
                        if 1 <= u < 17:
                            width = P * min((u - 1) // 2 + 1, 5)
                            act.wait_ge(prT_ready, base + u)
                            if u >= 3:
                                act.wait_ge(oa_ready, base + (u - 2))
                            A(prT[1 - b][:, :width], pair_b[:, :width], ACT.Copy).then_inc(prT_made, 1)
                        if u >= 4 and u % 2 == 0:
                            tt = (u - 4) // 2
                            act.wait_ge(yT_ready, p * 8 + (tt + 1))
                            settle(act)
                            A(ya_hi[:, p, tt * P:(tt + 1) * P], one[1][:, P:2 * P], ACT.Copy).then_inc(yT_hi, 1)

            for c in range(4):
                n = BLK_Z + c
                fetch_hi(act, num(n + 1), c + 1, n * 2)
                if c:
                    act.wait_ge(o_sum, c)
                A(osq[:, :], mixb[:, 8 + c, :], ACT.Square).then_inc(o_sq, 1)
                for half in range(2):
                    evacuated(act, JOB_Z + c, half)
                    A(tmp[half][:, :], tmp[half][:, :], ACT.Silu).then_inc(z_silu, 1)
                act.wait_ge(o_sum, c + 1)
                A(oln[:, :], pair_a[:, :], ACT.Ln, bias=eps_col, scale=1.0 / B_DIM).then_inc(o_ln, 1)
                act.drain()
                if c:
                    act.wait_ge(o_normed, c)
                A(oinv[:, :], oln[:, :], ACT.Exp, scale=-0.5).then_inc(o_inv, 1)
                for half in range(2):
                    act.wait_ge(yb_made, 2 * c + half + 1)
                    A(yb_hi[:, c, half_of(half)], tmp[2 + half][:, :], ACT.Copy).then_inc(yb_h, 1)

            with act.Fori(0, 4) as i:
                for q in range(2):
                    n = Num(i, 6, BLK_M + 3 * q)
                    job = i * 8 + (JOB_M + 4 * q)
                    fetch_hi(act, n + 1, 3 * q + 1, job * 2)
                    for half in range(2):
                        evacuated(act, job, half)
                        A(tmp[half][:, :], tmp[half][:, :], ACT.Sigmoid).then_inc(gate_sig, 1)
                    fetch_hi(act, n + 2, 3 * q + 2, job * 2 + 2)
                    for half in range(2):
                        evacuated(act, job + 1, half)
                        A(tmp[2 + half][:, :], tmp[2 + half][:, :], ACT.Sigmoid).then_inc(gate_sig, 1)
                    fetch_hi(act, n + 3, 3 * q + 3, job * 2 + 4)
            for k in range(8):
                act.wait_ge(merged_made, 2 * k + 2)
                A(mg_hi[:, k, :], merged[:, k, :], ACT.Copy).then_inc(mg_h, 1)
            for k in range(8):
                act.wait_ge(mg_l, k + 1)
                act.dma_start(x_sb[:, k, :], x_t[k]).then_inc(x_loaded[k], 16)

            for j in range(8):
                n = BLK_O + j
                fetch_hi(act, num(n + 1), j + 1, 2 * (JOB_O + j))
                for half in range(2):
                    residual_hi(act, JOB_O + j, j, half, P_GFFN, 0)
            stat_rstd(act, 2, sumsq2)

            def group(i, reg, gpar, step, last=False):
                n = Num(reg, 6 * step, BLK_F + 6 * i)
                if reg is None:
                    jobs = ffn_jobs(i)[0]
                    before = ffn_jobs(i - 1)[0] if i else [0, 0, 0, JOB_O + 7]
                    down_free = 2 * (ffn_jobs(i - 1)[0][3] + 3) if i > 1 else 2 * JOB_F
                else:
                    jobs = [reg * (12 * step) + v for v in ffn_jobs(i)[0]]
                    before = [None, None, None, reg * (12 * step) + (ffn_jobs(i)[0][0] - 3)]
                    down_free = reg * (24 * step) + 2 * ffn_jobs(i)[0][0]
                for c in range(4):
                    free = before[3] if c == 0 else jobs[c - 1]
                    if c < 3:
                        fetch_hi(act, n + (c + 1), c + 1, (free + 1) * 2)
                    else:
                        fetch_down_hi(act, n + 4, gpar, down_free)
                        if not last:
                            fetch_hi(act, n + 6, 0, (free + 1) * 2)
                    for half in range(2):
                        if c % 2 == 0:
                            evacuated(act, jobs[c], half)
                            A(tmp[half][:, :], tmp[half][:, :], ACT.Silu).then_inc(f_silu, 1)
                        else:
                            evacuated(act, jobs[c], half)
                            A(hid_hi[gpar][:, c // 2, half_of(half)], tmp[2 + half][:, :], ACT.Copy
                              ).then_inc(f_hi, 1)

            group(0, None, 0, 0)
            with act.Fori(0, 4) as i:
                group(1, i, 1, 2)
                group(2, i, 0, 2)
            group(9, None, 1, 0)
            group(10, None, 0, 0, last=True)
            fetch_down_hi(act, num(BLK_PP), 1, 2 * JOB_T)
            fetch_hi(act, num(BLK_PG), 0, 2 * JOB_T)
            act.wait_ge(p_loaded, 16)
            for k in range(2):
                A(hid_hi[1][:, k, :], p_raw[:, k, :], ACT.Copy).then_inc(p_hi, 1)
            for j in range(8):
                for half in range(2):
                    residual_hi(act, JOB_T + j, j, half, P_GPLE, 16)
            stat_rstd(act, 3, sumsq2)

            for j in range(8):
                if j < 7:
                    fetch_hi(act, num(BLK_PG + j + 1), j + 1, 2 * (JOB_P + 2 * (j - 1) + 1) if j else 2 * JOB_T)
                for half in range(2):
                    evacuated(act, JOB_P + 2 * j, half)
                    A(tmp[2 + half][:, :], tmp[2 + half][:, :], ACT.Sigmoid).then_inc(pg_sig, 1)
                for half in range(2):
                    act.wait_ge(x4_made, 2 * j + half + 1)
                    squares(act, j, half, 32)
            stat_rstd(act, 4, sumsq2)

        @block.vector
        def _(dve):
            V = nc.vector
            TTs, STT, TS = V.tensor_tensor, V.scalar_tensor_tensor, V.tensor_scalar
            dve.wait_ge(smalls_loaded, 32)
            V.tensor_copy(wbd_hi[:, :], params[:, P_WBD:P_WBD + 64])
            V.memset(convin[:, 0:4], 0.0)
            dve.drain()
            TTs(wbd_lo[:, :], params[:, P_WBD:P_WBD + 64], wbd_hi[:, :].bitcast(f32), ALU.subtract).then_inc(wbd_split, 1)
            for k in range(8):
                dve.wait_ge(norm_hi, k + 1)
                STT(h_lo[:, k, :], x_sb[:, k, :], params[:, P_GMIX + k:P_GMIX + k + 1],
                    h_hi[:, k, :].bitcast(f32), ALU.mult, ALU.subtract).then_inc(norm_lo, 1)
                if k:
                    dve.wait_ge(sq0_added, k)
                dve.wait_ge(sq0_made, k + 1)
                if k == 0:
                    V.tensor_copy(sumsq[:, :], sq[0][:, :]).then_inc(sq0_added, 1)
                else:
                    TTs(sumsq[:, :], sumsq[:, :], sq[k % 2][:, :], ALU.add).then_inc(sq0_added, 1)

            def l2_scale(idx, job):
                dve.wait_ge(l2_inv, idx + 1)
                STT(mixb[:, job, :], mixb[:, job, :], consts[:, ds(C_QKS + job, 1)] if not isinstance(job, int)
                    else consts[:, C_QKS + job:C_QKS + job + 1], inv_l2[:, :], ALU.mult, ALU.mult).then_inc(l2_done, 1)

            def conv_step(n, c, scale_prev):
                j = n.value
                dve.drain()
                for half in range(2):
                    job_done(dve, j, half)
                    TTs(convin[:, 3 + half * HALF:3 + (half + 1) * HALF], acc[half][:, :], rstd[:, half_of(half)],
                        ALU.mult).then_inc(acc_read[half], 1)
                for w in range(CONV):
                    col = P_CONV + w + (j * CONV)
                    tap = params[:, col:col + 1] if isinstance(col, int) else params[:, ds(col, 1)]
                    dve.drain()
                    if w == 0:
                        if not (isinstance(j, int) and j < 2):
                            dve.wait_ge(silu_done, (n + -1).value)
                        last = TS(conv[c][:, :], convin[:, 0:S], tap, None, ALU.mult)
                    else:
                        last = STT(conv[c][:, :], convin[:, w:w + S], tap, conv[c][:, :], ALU.mult, ALU.add)
                last.then_inc(conv_done, 1)
                if scale_prev:
                    l2_scale((n + -5).value, (n + -1).value)

            dve.wait_ge(rstd_ready, 1)
            for j in range(6):
                conv_step(num(j), j % 2, j == 5)
            with dve.Fori(3, 6) as i:
                conv_step(Num(i, 2, 0), 0, True)
                conv_step(Num(i, 2, 1), 1, True)
            dve.drain()
            dve.wait_ge(bd_ready, 1)
            dve.wait_ge(tok_rstd, 1)
            TTs(gates8[:, :, :], one[0][:, 0:64].rearrange("p (t c) -> p t c", t=8),
                rstd_tok[:, :].unsqueeze(2).to_broadcast([P, 8, 8]), ALU.mult)
            dve.drain()
            TTs(gates8[:, :, 4:8], gates8[:, :, 4:8],
                params[:, P_DTB:P_DTB + 4].unsqueeze(1).to_broadcast([P, 8, 4]), ALU.add)
            dve.drain()
            g4 = g_log[:, :].rearrange("p (t c) -> p t c", t=8)
            b4 = beta[:, :].rearrange("p (t c) -> p t c", t=8)
            TS(g4, gates8[:, :, 4:8], 0.0, None, ALU.max)
            TS(b4, gates8[:, :, 4:8], -1.0, None, ALU.mult)
            dve.drain()
            TTs(gates8[:, :, 4:8], gates8[:, :, 4:8], b4, ALU.max).then_inc(bd_scaled, 1)
            dve.wait_ge(bd_ln, 1)
            TS(b4, sp_a[:, :, :], 1.0, None, ALU.add)
            TTs(g4, g4, sp_b[:, :, :], ALU.add)
            dve.drain()
            V.reciprocal(beta[:, :], beta[:, :])
            dve.wait_ge(neg_a_made, 1)
            STT(g4, g4, -1.0, neg_a[:, :].unsqueeze(1).to_broadcast([P, 8, 4]), ALU.mult, ALU.mult).then_inc(g_made, 1)
            dve.wait_ge(gc_ready, 1)
            dve.wait_ge(gc_read, 1)
            V.tensor_copy(gdiff[:, :], one[1][:, 32:64])
            dve.drain()
            TTs(gdiff[:, :], gdiff[:, :], one[1][:, 0:32], ALU.subtract).then_inc(gc_made, 1)
            l2_scale(7, 11)
            V.memset(state[:, :, :], 0.0).then_inc(state_init, 1)
            dve.wait_ge(gc_read, 2)

            with dve.Fori(0, TOK_TILES) as t:
                tok = ds(t * P, P)

                def column(a):
                    return a[:, ds(t * 4, 4)].unsqueeze(2).to_broadcast([P, 4, P])

                TTs(gb[:, :, :], heads(ones), column(g_log), ALU.mult).then_inc(gb_made, 1)
                dve.wait_ge(gcb_ready, t + 1)
                dve.wait_ge(gamb_made, t + 1)
                TTs(dtmp[:, :, :], bank4(0), heads(decay_mask), ALU.add).then_inc(dtmp_made, 1)
                TTs(qg[:, :, :], mixb[:, 8:12, tok], gamb[:, :, :], ALU.mult)
                dve.wait_ge(dec_made, t + 1)
                dve.wait_ge(kk_ready, t + 1)
                for h in range(4):
                    last = STT(aT[:, h, :], decT[:, h, :], beta[:, ds(t * 4 + h, 1)], bank4(1)[:, h, :],
                               ALU.mult, ALU.mult)
                last.then_inc(aT_made, 1)
                dve.drain()
                TTs(TT[:, :, :], aT[:, :, :], heads(level[0]), ALU.mult)
                dve.drain()
                TTs(TT[:, :, :], heads(ident), TT[:, :, :], ALU.subtract).then_inc(tt0_made, 1)
                TTs(pT_[:, :, :], bank4(2), decT[:, :, :], ALU.mult)
                dve.wait_ge(tok_ready, t + 1)
                TTs(gk[:, :, :], bank4(3), column(gam), ALU.mult)
                TTs(kdec[:, :, :], bank4(3), column(kds), ALU.mult).then_inc(keys_made, 1)
                dve.wait_ge(t0_made, t + 1)
                for n in range(5):
                    dve.wait_ge(tn_ready, t * 5 + (n + 1))
                    if n < 4:
                        TTs(T[:, :, :], T[:, :, :], bank4(1), ALU.subtract)
                    TTs(TT[:, :, :], TT[:, :, :], bank4(2), ALU.subtract).then_inc(t_updated, 1)
                for c in range(2):
                    r = slice(c * CHUNK, (c + 1) * CHUNK)
                    dve.wait_ge(wv_ready, t * 2 + (c + 1))
                    TTs(w_[r, :, :], bank4(4)[r, :, :],
                        beta[r, ds(t * 4, 4)].unsqueeze(2).to_broadcast([CHUNK, 4, P]), ALU.mult).then_inc(w_made, 1)
                    dve.wait_ge(ds_ready, t * 2 + (c + 1))
                    end = (c + 1) * CHUNK - 1
                    for h in range(4):
                        last = STT(state[:, h, :], state[:, h, :], gamb[:, h, end:end + 1], bank4(0)[:, h, :],
                                   ALU.mult, ALU.add)
                    last.then_inc(state_made, 1)

            with dve.Fori(0, 2) as i:
                for q in range(2):
                    p = i * 2 + q
                    dve.drain()
                    for c, dst in enumerate((qa, ka, va)):
                        job = i * 6 + (JOB_A + 3 * q + c)
                        for half in range(2):
                            job_done(dve, job, half)
                            STT(dst[:, half_of(half)], acc[half][:, :], A_DIM ** -0.5 if c == 0 else 1.0,
                                rstd[:, half_of(half)], ALU.mult, ALU.mult).then_inc(acc_read[half], 1)
                    dve.drain()
                    for hh in range(2):
                        dve.wait_ge(bias_loaded[hh], (p + 1) * 16)
                    for u in range(19):
                        b, base = u % 2, p * 16
                        if u < 16:
                            width = P * min(u // 2 + 1, 5)
                            dve.wait_ge(sc_ready, base + (u + 1))
                            if u >= 2:
                                dve.wait_ge(pr_made, base + (u - 1))
                            TTs(sc[b][:, :width], pair_a[:, :width], biast[u % 2][:, WINDOW - width:], ALU.add
                                ).then_inc(sc_read, 1)
                            dve.drain()
                            V.tensor_reduce(nmax[:, b:b + 1], sc[b][:, :width], AX.X, ALU.max, negate=True
                                            ).then_inc(max_made, 1)
                        if 2 <= u < 18:
                            v, vb = u - 2, u % 2
                            tt = v // 2
                            dve.wait_ge(oa_ready, base + (v + 1))
                            V.reciprocal(rsum[:, vb:vb + 1], psum_row[:, v % 4:v % 4 + 1])
                            dve.drain()
                            if tt >= 2:
                                dve.wait_ge(yT_ready, p * 8 + (tt - 1))
                            TS(ytok[tt % 2][:, (v % 2) * 64:(v % 2) * 64 + 64], one[vb][:, 0:64], rsum[:, vb:vb + 1],
                               None, ALU.mult).then_inc(ya_norm, 1)
                        if u >= 4 and u % 2 == 0:
                            tt = (u - 4) // 2
                            dve.wait_ge(yT_hi, p * 8 + (tt + 1))
                            TTs(ya_lo[:, p, tt * P:(tt + 1) * P], one[1][:, P:2 * P],
                                ya_hi[:, p, tt * P:(tt + 1) * P].bitcast(f32), ALU.subtract).then_inc(yT_lo, 1)

            for c in range(4):
                for half in range(2):
                    dve.drain()
                    job_done(dve, JOB_Z + c, half)
                    TTs(tmp[half][:, :], acc[half][:, :], rstd[:, half_of(half)], ALU.mult).then_inc(acc_read[half], 1)
                dve.drain()
                dve.wait_ge(o_inv, c + 1)
                STT(mixb[:, 8 + c, :], mixb[:, 8 + c, :], params[:, P_ONORM:P_ONORM + 1], oinv[:, :], ALU.mult, ALU.mult
                    ).then_inc(o_normed, 1)
                dve.drain()
                for half in range(2):
                    dve.wait_ge(z_silu, 2 * c + half + 1)
                    if c:
                        dve.wait_ge(yb_h, 2 * (c - 1) + half + 1)
                    TTs(tmp[2 + half][:, :], tmp[half][:, :], mixb[:, 8 + c, half_of(half)], ALU.mult
                        ).then_inc(yb_made, 1)
                for half in range(2):
                    dve.wait_ge(yb_h, 2 * c + half + 1)
                    TTs(yb_lo[:, c, half_of(half)], tmp[2 + half][:, :], yb_hi[:, c, half_of(half)].bitcast(f32),
                        ALU.subtract).then_inc(yb_l, 1)

            with dve.Fori(0, 4) as i:
                for q in range(2):
                    j = i * 2 + q
                    job = i * 8 + (JOB_M + 4 * q)
                    dve.drain()
                    for c in range(4):
                        for half in range(2):
                            cols = half_of(half)
                            job_done(dve, job + c, half)
                            if c < 2:
                                TTs(tmp[2 * c + half][:, :], acc[half][:, :], rstd[:, cols], ALU.mult
                                    ).then_inc(acc_read[half], 1)
                            elif c == 2:
                                dve.wait_ge(gate_sig, i * 8 + (4 * q + half + 1))
                                TTs(merged[:, j, cols], acc[half][:, :], tmp[half][:, :], ALU.mult
                                    ).then_inc(acc_read[half], 1)
                            else:
                                dve.wait_ge(gate_sig, i * 8 + (4 * q + half + 3))
                                TTs(tmp[4 + half][:, :], acc[half][:, :], tmp[2 + half][:, :], ALU.mult
                                    ).then_inc(acc_read[half], 1)
                                dve.drain()
                                TTs(merged[:, j, cols], merged[:, j, cols], tmp[4 + half][:, :], ALU.add
                                    ).then_inc(merged_made, 1)
            for k in range(8):
                dve.wait_ge(mg_h, k + 1)
                TTs(mg_lo[:, k, :], merged[:, k, :], mg_hi[:, k, :].bitcast(f32), ALU.subtract).then_inc(mg_l, 1)

            def residual(job, j, half):
                job_done(dve, job, half)
                TTs(x_sb[:, j, half_of(half)], x_sb[:, j, half_of(half)], acc[half][:, :], ALU.add
                    ).then_inc(acc_read[half], 1)

            for j in range(8):
                dve.wait_ge(x_loaded[j], 32)
                for half in range(2):
                    residual(JOB_O + j, j, half)
                dve.drain()
                for half in range(2):
                    residual_lo(dve, j, half, P_GFFN, 8)

            def group(i, reg, gpar, step):
                shift = 12 * step
                jobs = [lin(reg, shift, v) for v in ffn_jobs(i)[0]]
                downs = [lin(reg, shift, v) for v in ffn_jobs(i)[1]]
                for c in range(4):
                    tile_ = c // 2
                    dve.drain()
                    for half in range(2):
                        job_done(dve, jobs[c], half)
                        if c % 2 == 0:
                            TTs(tmp[half][:, :], acc[half][:, :], rstd[:, half_of(half)], ALU.mult
                                ).then_inc(acc_read[half], 1)
                        else:
                            dve.wait_ge(f_scaled, lin(reg, 4 * step, 4 * i + 2 * tile_ + half + 1))
                            TTs(tmp[2 + half][:, :], acc[half][:, :], tmp[half][:, :], ALU.mult
                                ).then_inc(acc_read[half], 1)
                    if c % 2:
                        for half in range(2):
                            dve.wait_ge(f_hi, lin(reg, 4 * step, 4 * i + 2 * tile_ + half + 1))
                            TTs(hid_lo[gpar][:, tile_, half_of(half)], tmp[2 + half][:, :],
                                hid_hi[gpar][:, tile_, half_of(half)].bitcast(f32), ALU.subtract).then_inc(f_lo, 1)
                    for j in (2 * c, 2 * c + 1):
                        if downs:
                            for half in range(2):
                                residual(downs[j], j, half)

            dve.wait_ge(rstd_ready, 2)
            group(0, None, 0, 0)
            with dve.Fori(0, 4) as i:
                group(1, i, 1, 2)
                group(2, i, 0, 2)
            group(9, None, 1, 0)
            group(10, None, 0, 0)
            dve.drain()
            for j in range(8):
                for half in range(2):
                    residual(JOB_T + j, j, half)
                if j == 0:
                    for k in range(2):
                        dve.wait_ge(p_hi, k + 1)
                        TTs(hid_lo[1][:, k, :], p_raw[:, k, :], hid_hi[1][:, k, :].bitcast(f32), ALU.subtract
                            ).then_inc(p_lo, 1)
                dve.drain()
                for half in range(2):
                    residual_lo(dve, j, half, P_GPLE, 24)

            dve.wait_ge(rstd_ready, 3)
            for j in range(8):
                dve.drain()
                for half in range(2):
                    job_done(dve, JOB_P + 2 * j, half)
                    TTs(tmp[2 + half][:, :], acc[half][:, :], rstd[:, half_of(half)], ALU.mult
                        ).then_inc(acc_read[half], 1)
                for half in range(2):
                    job_done(dve, JOB_P + 2 * j + 1, half)
                    dve.wait_ge(pg_sig, 2 * j + half + 1)
                    TTs(tmp[2 + half][:, :], acc[half][:, :], tmp[2 + half][:, :], ALU.mult).then_inc(acc_read[half], 1)
                dve.drain()
                for half in range(2):
                    TTs(x_sb[:, j, half_of(half)], x_sb[:, j, half_of(half)], tmp[2 + half][:, :], ALU.add
                        ).then_inc(x4_made, 1)
            dve.wait_ge(rstd_ready, 4)
            for j in range(8):
                STT(out_sb[:, j, :], x_sb[:, j, :], params[:, P_GFIN + j:P_GFIN + j + 1], rstd[:, :],
                    ALU.mult, ALU.mult).then_inc(out_made, 1)

        @block.tensor
        def _(pe):
            mm, tr = nc.tensor.matmul, nc.tensor.transpose

            def l2_sums(idx):
                pe.wait_ge(l2_sq, idx + 1)
                if not (isinstance(idx, int) and idx == 0):
                    pe.wait_ge(l2_ln, idx)
                for half in range(2):
                    last = mm(pair_b[:, half_of(half)], ones, sqv[:, half_of(half)], start=True, stop=True)
                last.then_inc(l2_sum, 1)

            pe.wait_ge(smalls_loaded, 32)
            project(pe, 0, ring(0), hx, ALL, num(0), lambda n: pe.wait_ge(norm_lo, n + 1))
            pe.wait_ge(sq0_added, 8)
            stat_sum(pe, sumsq)
            for t in range(TOK_TILES):
                last = mm(one[1][:, t:t + 1], sumsq[:, t * P:(t + 1) * P], ones[:, 0:1], start=True, stop=True)
            last.then_inc(tok_stat, 1)
            pe.wait_ge(wbd_split, 1)
            for t in range(TOK_TILES):
                tokens = slice(t * P, (t + 1) * P)
                for k in range(8):
                    for a, b in ((h_hi, wbd_hi), (h_hi, wbd_lo), (h_lo, wbd_hi)):
                        last = mm(one[0][:, t * 8:(t + 1) * 8], a[:, k, tokens], b[:, k * 8:(k + 1) * 8],
                                  start=(k == 0 and a is h_hi and b is wbd_hi), stop=(k == 7 and a is h_lo))
            last.then_inc(bd_ready, 1)
            for j in range(1, 6):
                project(pe, j, ring(j), hx, ALL, num(j))
                if j == 5:
                    l2_sums(0)
            with pe.Fori(3, 6) as i:
                for c in range(2):
                    n = Num(i, 2, c)
                    project(pe, n.value, ring(c), hx, ALL, n)
                    l2_sums((n + -5).value)
            l2_sums(7)
            pe.wait_ge(g_made, 1)
            pe.wait_ge(tok_rstd, 1)
            mm(one[1][:, 0:32], cum, g_log[:, :], start=True, stop=True)
            mm(one[1][:, 32:64], chunk_ones, g_log[:, :], start=True, stop=True).then_inc(gc_ready, 1)
            pe.wait_ge(state_init, 1)
            pe.wait_ge(gc_made, 1)
            pe.wait_ge(gc_read, 2)
            with pe.Fori(0, TOK_TILES) as t:
                tok = ds(t * P, P)
                pe.wait_ge(gb_made, t + 1)
                for h in range(4):
                    last = mm(bank4(0)[:, h, :], gb[:, h, :], cum, start=True, stop=True)
                last.then_inc(gcb_ready, 1)
                pe.wait_ge(tiles_in, t * 2 + 2)
                for h in range(4):
                    mm(bank4(1)[:, h, :], kn[:, h, :], kn[:, h, :], start=True, stop=True)
                for h in range(4):
                    last = mm(bank4(2)[:, h, :], kn[:, h, :], mixb[:, 8 + h, tok], start=True, stop=True)
                last.then_inc(kk_ready, 1)
                for h in range(4):
                    tr(bank4(3)[:, h, :], kn[:, h, :], ident)
                for h in range(4):
                    last = tr(bank4(4)[:, h, :], vn[:, h, :], ident)
                last.then_inc(tok_ready, 1)
                pe.wait_ge(tt0_made, t + 1)
                for h in range(4):
                    last = tr(bank4(5)[:, h, :], TT[:, h, :], ident)
                last.then_inc(t0_ready, 1)
                pe.wait_ge(t0_made, t + 1)
                for n in range(5):
                    if n == 0:
                        pe.wait_ge(dtmp_made, t + 1)
                        pe.wait_ge(keys_made, t + 1)
                    else:
                        pe.wait_ge(t_updated, t * 5 + n)
                    pe.wait_ge(aoff_made, t * 5 + (n + 1))
                    for h in range(4):
                        last = mm(bank4(0)[:, h, :], aoff[n][:, h, :], T[:, h, :], start=True, stop=True)
                    last.then_inc(n_ready, 1)
                    pe.wait_ge(n_made, t * 5 + (n + 1))
                    for h in range(4):
                        if n < 4:
                            mm(bank4(1)[:, h, :], TT[:, h, :], Ns[:, h, :], start=True, stop=True)
                        last = mm(bank4(2)[:, h, :], Ns[:, h, :], TT[:, h, :], start=True, stop=True)
                    last.then_inc(tn_ready, 1)
                pe.wait_ge(t_updated, t * 5 + 5)
                for h in range(4):
                    last = mm(bank4(3)[:, h, :], gk[:, h, :], TT[:, h, :], start=True, stop=True)
                last.then_inc(wk_ready, 1)
                pe.wait_ge(nwk_made, t + 1)
                pe.wait_ge(vtok_made, t + 1)
                for c in range(2):
                    r = slice(c * CHUNK, (c + 1) * CHUNK)
                    if c:
                        pe.wait_ge(state_made, t * 2 + c)
                    for h in range(4):
                        mm(bank4(4)[r, h, :], TT[:, h, r], vtok[:, h, :], start=True, stop=False)
                        last = mm(bank4(4)[r, h, :], nwk[:, h, r], state[:, h, :], start=False, stop=True)
                    last.then_inc(wv_ready, 1)
                    pe.wait_ge(w_made, t * 2 + (c + 1))
                    for h in range(4):
                        mm(bank4(5)[:, h, r], state[:, h, :], qg[:, h, r], start=True, stop=False)
                        last = mm(bank4(5)[:, h, r], w_[r, h, :], pT_[r, h, r], start=False, stop=True)
                    if c:
                        last.then_inc(o_ready, 1)
                    for h in range(4):
                        last = mm(bank4(0)[:, h, :], kdec[r, h, :], w_[r, h, :], start=True, stop=True)
                    last.then_inc(ds_ready, 1)

            pe.wait_ge(o_made, 8)
            with pe.Fori(0, 2) as i:
                for q in range(2):
                    p = i * 2 + q
                    base = p * 16
                    for c in range(3):
                        n = Num(i, 6, BLK_A + 3 * q + c)
                        project(pe, n.value, ring(3 * q + c), hx, ALL, n)
                    for half in range(2):
                        pe.wait_ge(acc_read[half], (n + 1).value)
                    for tt in range(8):
                        last = tr(pair_b[:, tt * P:(tt + 1) * P], va[:, tt * P:(tt + 1) * P], ident)
                    last.then_inc(vt_ready, 1)
                    pe.wait_ge(vt_made, p + 1)
                    for u in range(19):
                        if u < 16:
                            tt, r = u // 2, slice(64 * (u % 2), 64 * (u % 2) + 64)
                            tiles = min(tt + 1, 5)
                            k0, width = (tt + 1 - tiles) * P, tiles * P
                            if u:
                                pe.wait_ge(sc_read, base + u)
                            for a in range(0, width, HALF):
                                e = min(width, a + HALF)
                                last = mm(pair_a[:, a:e], qa[r, tt * P:(tt + 1) * P], ka[r, k0 + a:k0 + e],
                                          start=True, stop=True)
                            last.then_inc(sc_ready, 1)
                        if 1 <= u < 17:
                            v = u - 1
                            tiles = min(v // 2 + 1, 5)
                            pe.wait_ge(pr_made, base + u)
                            if v:
                                pe.wait_ge(prT_made, base + v)
                            for kt in range(tiles):
                                last = tr(pair_b[:, kt * P:(kt + 1) * P], pr[v % 2][:, kt * P:(kt + 1) * P], ident)
                            last.then_inc(prT_ready, 1)
                        if u >= 4 and u % 2 == 0:
                            tt = (u - 4) // 2
                            pe.wait_ge(ya_norm, base + (2 * tt + 2))
                            tr(one[1][:, P:2 * P], ytok[tt % 2][:, :], ident).then_inc(yT_ready, 1)
                        if 2 <= u < 18:
                            v = u - 2
                            tt, r = v // 2, slice(64 * (v % 2), 64 * (v % 2) + 64)
                            tiles = min(tt + 1, 5)
                            pe.wait_ge(prT_made, base + (v + 1))
                            if v >= 2 and v % 2:
                                pe.wait_ge(yT_lo, p * 8 + tt)
                            elif v >= 2:
                                pe.wait_ge(ya_norm, base + (v - 1))
                            for kt in range(tiles):
                                last = mm(one[v % 2][:, 0:64], prT[v % 2][:, kt * P:(kt + 1) * P],
                                          va_tok[:, tt + 1 - tiles + kt, r], start=(kt == 0), stop=(kt == tiles - 1))
                            last.then_inc(oa_ready, 1)

            for c in range(4):
                project(pe, JOB_Z + c, ring(c), hx, ALL, num(BLK_Z + c))
                pe.wait_ge(o_sq, c + 1)
                if c:
                    pe.wait_ge(o_ln, c)
                for half in range(2):
                    last = mm(pair_a[:, half_of(half)], ones, osq[:, half_of(half)], start=True, stop=True)
                last.then_inc(o_sum, 1)

            with pe.Fori(0, 4) as i:
                for q in range(2):
                    n = Num(i, 6, BLK_M + 3 * q)
                    job = i * 8 + (JOB_M + 4 * q)
                    project(pe, job, ring(3 * q), hx, ALL, n)
                    project(pe, job + 1, ring(3 * q + 1), hx, ALL, n + 1)
                    pe.wait_ge(yT_lo, 32)
                    pe.wait_ge(yb_l, 8)
                    project(pe, job + 2, ring(3 * q + 2), (ya_hi, ya_lo), [(k, k) for k in range(4)], n + 2)
                    project(pe, job + 3, ring(3 * q + 2), (yb_hi, yb_lo), [(4 + k, k) for k in range(4)])
            for j in range(8):
                project(pe, JOB_O + j, ring(j), mgx, ALL, num(BLK_O + j),
                        (lambda n: pe.wait_ge(mg_l, n + 1)) if j == 0 else None)

            def group(i, reg, gpar, step):
                shift = 12 * step
                jobs = [lin(reg, shift, v) for v in ffn_jobs(i)[0]]
                downs = [lin(reg, shift, v) for v in ffn_jobs(i)[1]]
                n = Num(reg, 6 * step, BLK_F + 6 * i)
                for c in range(4):
                    wait = (lambda k: pe.wait_ge(norm_lo, 8 + 2 * k + 2)) if i == 0 and reg is None and c == 0 else None
                    project(pe, jobs[c], ring(c), h2x, ALL, n + c, wait)
                    if wait is not None:
                        pe.wait_ge(sq_added, 16)
                        stat_sum(pe, sumsq2)
                    if downs:
                        if c == 0:
                            pe.wait_ge(f_lo, lin(reg, 4 * step, 4 * i))
                        for j in (2 * c, 2 * c + 1):
                            project(pe, downs[j], down_w(1 - gpar, j), (hid_hi[1 - gpar], hid_lo[1 - gpar]),
                                    [(0, 0), (1, 1)])

            group(0, None, 0, 0)
            with pe.Fori(0, 4) as i:
                group(1, i, 1, 2)
                group(2, i, 0, 2)
            group(9, None, 1, 0)
            group(10, None, 0, 0)
            pe.wait_ge(f_lo, 4 * GROUPS)
            pe.wait_ge(lo_made, BLK_F + 6 * GROUPS)
            for j in range(8):
                project(pe, JOB_T + j, down_w(0, j), (hid_hi[0], hid_lo[0]), [(0, 0), (1, 1)])
            for j in range(8):
                project(pe, JOB_P + 2 * j, ring(j), h2x, ALL, num(BLK_PG + j),
                        (lambda k: pe.wait_ge(norm_lo, 24 + 2 * k + 2)) if j == 0 else None)
                if j == 0:
                    pe.wait_ge(sq_added, 32)
                    stat_sum(pe, sumsq2)
                    pe.wait_ge(p_lo, 2)
                project(pe, JOB_P + 2 * j + 1, down_w(1, j), (hid_hi[1], hid_lo[1]), [(0, 0), (1, 1)])
            pe.wait_ge(sq_added, 48)
            stat_sum(pe, sumsq2)


def constants():
    c = np.zeros((P, N_CONST), np.float32)
    j, i = np.arange(P)[:, None], np.arange(P)[None, :]
    same = j // CHUNK == i // CHUNK
    c[:, C_IDENT:C_IDENT + P] = j == i
    c[:, C_ONES:C_ONES + P] = 1.0
    c[:, C_CUM:C_CUM + P] = same & (j <= i)
    c[:, C_CHUNK:C_CHUNK + P] = same
    c[:, C_MASK:C_MASK + P] = np.where(same & (j <= i), 0.0, NEG)
    for n, b in enumerate(LEVELS):
        c[:, C_LEVEL + P * n:C_LEVEL + P * (n + 1)] = (j // (2 * b) == i // (2 * b)) & (i % (2 * b) >= b) & (j % (2 * b) < b)
    c[:, C_EPS] = EPS
    c[:, C_QKS:C_QKS + 8] = 1.0
    c[:, C_QKS + 8:C_QKS + 12] = B_DIM ** -0.5
    return c


def kernel(**inputs):
    import concourse.bacc as bacc
    from concourse.bass_utils import run_bass_kernel_spmd

    a = {k: np.asarray(v) for k, v in inputs.items()}
    f = np.float32
    w_in = a["w_in"][0]
    aw, qkv = A_HEADS * A_DIM, B_HEADS * B_DIM

    def col_blocks(w):
        k, n = w.shape[0] // P, w.shape[1] // P
        return w.reshape(k, P, n, P).transpose(2, 1, 0, 3).reshape(n, P, k * P)

    qa, ka, va = (col_blocks(w_in[:, aw * n:aw * (n + 1)]) for n in range(3))
    o = 3 * aw
    qb, kb, vb, z = (col_blocks(w_in[:, o + qkv * n:o + qkv * (n + 1)]) for n in range(4))
    o += 4 * qkv
    wbd = w_in[:, o:o + 8]
    ga, gb = col_blocks(w_in[:, o + 8:o + 8 + D]), col_blocks(w_in[:, o + 8 + D:o + 8 + 2 * D])
    wa, wb = col_blocks(a["w_branch_a"][0]), col_blocks(a["w_branch_b"][0])
    gate, up = col_blocks(a["w_gate_up"][0][:, :D_FF]), col_blocks(a["w_gate_up"][0][:, D_FF:])
    down = a["w_down"][0].reshape(D_FF // P, P, D)
    parts = [vb, kb, qb, np.stack([qa, ka, va], 1), z,
             np.stack([ga, gb, np.concatenate([wa, wb], 2)], 1), col_blocks(a["w_out"][0])]
    for g in range(GROUPS):
        parts += [gate[2 * g], up[2 * g], gate[2 * g + 1], up[2 * g + 1], down[2 * g], down[2 * g + 1]]
    parts += [a["w_ple_proj"][0].reshape(2, P, D), col_blocks(a["w_ple_gate"][0])]
    blocks = np.concatenate([x.reshape(-1, P, D) for x in parts]).astype(f, copy=False)
    assert blocks.shape[0] == N_BLK

    params = np.zeros((P, N_PARAM), f)
    for c, g in ((P_GMIX, a["g_mix"][0]), (P_GFFN, a["g_ffn"][0]), (P_GPLE, a["g_ple"][0]), (P_GFIN, a["g_final"])):
        params[:, c:c + 8] = g.reshape(8, P).T
    cw = a["conv_w"][0].reshape(CONV, 3, B_HEADS, P)[:, ::-1]
    params[:, P_CONV:P_CONV + 12 * CONV] = cw.reshape(CONV, 12, P).transpose(2, 1, 0).reshape(P, 48)
    params[:, P_ONORM] = a["w_onorm"][0]
    params[:, P_ALOG:P_ALOG + 4] = a["a_log"][0][None]
    params[:, P_DTB:P_DTB + 4] = a["dt_bias"][0][None]
    params[:, P_WBD:P_WBD + 64] = wbd.reshape(8, P, 8).transpose(1, 0, 2).reshape(P, 64)

    qi, kj = np.arange(P)[:, None], np.arange(WINDOW)[None, :]
    idx = np.clip(WINDOW - P + qi - kj, -REL_CLIP, REL_CLIP) + REL_CLIP
    chunks = kj // CHUNK - qi // CHUNK
    bias = np.where((chunks >= 0) & (chunks <= LOOKBACK), a["rel_bias"][0][:, idx], f(NEG)).astype(f, copy=False)

    x_t = np.ascontiguousarray(a["x"][0].T).reshape(8, P, S)
    p_t = np.ascontiguousarray(a["p"][0, 0].T).reshape(2, P, S)
    arrays = {"x_t": x_t, "p_t": p_t, "blocks": blocks, "consts": constants(), "params": params, "bias": bias}
    nc = bacc.Bacc("TRN2", target_bir_lowering=False, num_devices=1)
    aps = [nc.dram_tensor(n, v.shape, mybir.dt.float32, kind="ExternalInput").ap() for n, v in arrays.items()]
    aps.append(nc.dram_tensor("out_t", (8, P, S), mybir.dt.float32, kind="ExternalOutput").ap())
    hybrid_block(nc, *aps)
    r = run_bass_kernel_spmd(nc, [arrays], core_ids=[0])
    return np.ascontiguousarray(r.results[0]["out_t"].reshape(D, S).T).reshape(1, S, D)
```

```python
import numpy as np
import concourse.bass as bass
from concourse import mybir
from contextlib import ExitStack

S, D, P = 1024, 1024, 128
KT = D // P
HALF = 512
TOK_TILES = S // P
CHUNK = 64
A_HEADS, A_DIM, LOOKBACK, REL_CLIP = 8, 64, 8, 128
PAIRS = A_HEADS // 2
WINDOW = 5 * P
B_HEADS, B_DIM = 4, 128
CONV = 4
D_FF = 2816
GROUPS = D_FF // (2 * P)
EPS = 1e-6
NEG = -1e30

C_IDENT, C_ONES, C_CUM, C_CHUNK, C_MASK, C_LEVEL = 0, 128, 256, 384, 512, 640
LEVELS = (1, 2, 4, 8, 16, 32)
C_EPS = C_LEVEL + 128 * len(LEVELS)
C_QKS = C_EPS + 1
N_CONST = C_QKS + 12
P_GMIX, P_GFFN, P_GPLE, P_GFIN, P_CONV = 0, 8, 16, 24, 32
P_ONORM = P_CONV + 12 * CONV
P_ALOG, P_DTB = P_ONORM + 1, P_ONORM + 5
N_PARAM = P_ONORM + 9

BLK_A, BLK_G, BLK_M = 13, 29, 45
BLK_O = BLK_M + 8
BLK_F = BLK_O + 8
BLK_PP = BLK_F + 6 * GROUPS
BLK_PG = BLK_PP + 2
N_BLK = BLK_PG + 8
JOB_A, JOB_G, JOB_M = BLK_A, BLK_G, BLK_M
JOB_O = JOB_M + 2 * 8
FILL_B = (1, 2, 1) + (2, 2) * 5 + (2, 2, 2, 2)
FILL_A = (4, 4, 3, 3, 3, 3, 3, 3, 3, 3, 2, 2, 2, 2, 2, 2, 1, 1, 2)
JOB_F = JOB_O + 8
JOB_T = JOB_F + 4 + 12 * (GROUPS - 1)
JOB_P = JOB_T + 8


def ffn_jobs(i):
    if isinstance(i, int) and i == 0:
        return [JOB_F + c for c in range(4)], []
    base = JOB_F + 4 + (i - 1) * 12
    return [base + 3 * c for c in range(4)], [base + 3 * (n // 2) + 1 + n % 2 for n in range(8)]


def cuts(counts):
    ends = [sum(counts[:n + 1]) for n in range(len(counts))]
    return list(zip([0] + ends, ends))


def hybrid_block(nc, x_t, p_t, blocks, consts_d, params_d, bias_d, out_t, spill):
    f32, f32r = mybir.dt.float32, mybir.dt.float32r
    ALU, ACT, AX = mybir.AluOpType, mybir.ActivationFunctionType, mybir.AxisListType
    ds = bass.ds

    ctx = ExitStack()
    with ctx:
        BASE = 16512
        K = 1024

        def at(name, shape, dt, offset):
            return nc.alloc_sbuf_tensor_at(name, shape, dt, offset=BASE + offset)

        def sem(name):
            return ctx.enter_context(nc.semaphore(name))

        h_hi = at("h_hi", [P, 8, S], f32r, 0)
        h_lo = at("h_lo", [P, 8, S], f32r, 32 * K)
        mg_hi = at("mg_hi", [P, 8, S], f32r, 0)
        mg_lo = at("mg_lo", [P, 8, S], f32r, 32 * K)
        hid_hi = [at(f"hid_hi{g}", [P, 2, S], f32r, 32 * K * g) for g in range(2)]
        hid_lo = [at(f"hid_lo{g}", [P, 2, S], f32r, 32 * K * g + 8 * K) for g in range(2)]
        dw_hi = [at(f"dw_hi{g}", [P, 2, S], f32r, 32 * K * g + 16 * K) for g in range(2)]
        dw_lo = [at(f"dw_lo{g}", [P, 2, S], f32r, 32 * K * g + 24 * K) for g in range(2)]
        out_sb = at("out_sb", [P, 8, S], f32, 0)
        ya_hi = at("ya_hi", [P, 4, S], f32r, 64 * K)
        ya_lo = at("ya_lo", [P, 4, S], f32r, 80 * K)
        yb_hi = at("yb_hi", [P, 4, S], f32r, 96 * K)
        yb_lo = at("yb_lo", [P, 4, S], f32r, 112 * K)
        h2_hi = at("h2_hi", [P, 8, S], f32r, 64 * K)
        h2_lo = at("h2_lo", [P, 8, S], f32r, 96 * K)
        mixb = at("mixb", [P, 12, S], f32, 96 * K)
        x_sb = at("x_sb", [P, 8, S], f32, 128 * K)
        raw = [at(f"raw{s}", [P, 1024], f32, 160 * K + 4 * K * s) for s in range(2)]
        w_hi = [at(f"w_hi{s}", [P, 8, P], f32r, 168 * K + 8 * K * s) for s in range(2)]
        w_lo = [at(f"w_lo{s}", [P, 8, P], f32r, 172 * K + 8 * K * s) for s in range(2)]
        consts = at("consts", [P, N_CONST], f32, 184 * K)
        params = at("params", [P, N_PARAM], f32, 190 * K)
        rstd = at("rstd", [P, S], f32, 191 * K)
        tmp = [at(f"tmp{n}", [P, HALF], f32, 195 * K + 2 * K * n) for n in range(6)]
        small = 207 * K
        off = [small]

        def tiny(name, n, dt=f32):
            off[0] += 32
            return at(name, [P, n], dt, off[0] - 32)

        nmax = tiny("nmax", 4)
        psum_row = tiny("psum_row", 4)
        rsum = tiny("rsum", 4)

        neg_a = tiny("neg_a", 4)
        assert off[0] <= 212848
        sq = [at(f"sq{n}", [P, S], f32, 64 * K + 4 * K * n) for n in range(2)]
        sumsq = at("sumsq", [P, S], f32, 72 * K)
        sumsq2 = at("sumsq2", [P, S], f32, 203 * K)
        convin = at("convin", [P, S + 4], f32, 76 * K)
        conv = [at(f"conv{n}", [P, S], f32, 81 * K + 4 * K * n) for n in range(2)]
        lnb = at("lnb", [P, S], f32, 89 * K)
        inv_l2 = at("inv_l2", [P, S], f32, 64 * K)
        sqv = at("sqv", [P, S], f32, 68 * K)
        spots = [64 * K + 2 * K * n for n in range(16)] + [144 * K + 2 * K * n for n in range(8)]
        spot = iter(spots)

        def four(name):
            return at(name, [P, 4, P], f32, next(spot))

        (kn, vn, gb, gamb, dtmp, decT, pT_, aT, qg, gk, kdec, vtok, T, TT, Ns, nwk, w_, state) = (
            four(n) for n in "kn vn gb gamb dtmp decT pT aT qg gk kdec vtok T TT Ns nwk w state".split())
        aoff = [four(f"aoff{b}") for b in LEVELS[1:]]
        gates8 = at("gates8", [P, 8, 8], f32, 93 * K)
        sp_a = at("sp_a", [P, 8, 4], f32, 93 * K + 256)
        sp_b = at("sp_b", [P, 8, 4], f32, 93 * K + 384)
        beta = at("beta", [P, 32], f32, 203 * K)
        g_log = at("g_log", [P, 32], f32, 203 * K + 128)
        neg_gc = at("neg_gc", [P, 32], f32, 203 * K + 256)
        gam = at("gam", [P, 32], f32, 203 * K + 384)
        kds = at("kds", [P, 32], f32, 203 * K + 512)
        gdiff = at("gdiff", [P, 32], f32, 203 * K + 640)
        bd_rows = at("bd_rows", [8, S], f32, 195 * K)
        stage = [at(f"stage{n}", [P, S], f32, 195 * K + 4 * K * n) for n in range(2)]
        osq = [at(f"osq{n}", [P, S], f32, 64 * K + 4 * K * n) for n in range(2)]
        oln = at("oln", [P, S], f32, 72 * K)
        oinv = [at(f"oinv{n}", [P, S], f32, 76 * K + 4 * K * n) for n in range(2)]
        biast = [[at(f"biast{q}{n}", [P, WINDOW], f32, 96 * K + 2560 * (2 * q + n)) for n in range(2)] for q in range(2)]
        sc = [at(f"sc{n}", [P, WINDOW], f32, 106 * K + 2560 * n) for n in range(2)]
        pr = [at(f"pr{n}", [P, WINDOW], f32, 111 * K + 2560 * n) for n in range(2)]
        prT = [at(f"prT{n}", [P, WINDOW], f32, 116 * K + 2560 * n) for n in range(2)]
        ytok = [at(f"ytok{n}", [P, P], f32, 121 * K + 512 * n) for n in range(2)]
        qa = [at(f"qa{q}", [P, S], f32, o * K) for q, o in enumerate((144, 124))]
        ka = [at(f"ka{q}", [P, S], f32, o * K) for q, o in enumerate((148, 203))]
        va = at("va", [P, S], f32, 152 * K)
        va_tok = at("va_tok", [P, 8, P], f32, 156 * K)
        z_sb = [qa[0], ka[0], va, at("z3", [P, S], f32, 156 * K)]
        gate_sb = [[at(f"gate{q}{n}", [P, S], f32, (144 + 8 * q + 4 * n) * K) for n in range(2)] for q in range(2)]
        prod = [at(f"prod{n}", [P, S], f32, 195 * K + 4 * K * n) for n in range(2)]
        p_raw = at("p_raw", [P, 2, S], f32, 40 * K)

        ident = consts[:, C_IDENT:C_IDENT + P]
        ones = consts[:, C_ONES:C_ONES + P]
        cum = consts[:, C_CUM:C_CUM + P]
        chunk_ones = consts[:, C_CHUNK:C_CHUNK + P]
        decay_mask = consts[:, C_MASK:C_MASK + P]
        level = [consts[:, C_LEVEL + P * n:C_LEVEL + P * (n + 1)] for n in range(len(LEVELS))]
        eps_col = consts[:, C_EPS:C_EPS + 1]

        def heads(a):
            return a.unsqueeze(1).to_broadcast([P, 4, P])

        acc = [ctx.enter_context(nc.psum_tensor(f"acc{n}", [P, HALF], f32)) for n in range(2)]
        pair_a = ctx.enter_context(nc.psum_tensor("pair_a", [P, 1024], f32))
        pair_b = ctx.enter_context(nc.psum_tensor("pair_b", [P, 1024], f32))
        one = [ctx.enter_context(nc.psum_tensor(f"one{n}", [P, HALF], f32)) for n in range(2)]

        def bank(n):
            t = (pair_a, pair_a, pair_b, pair_b, one[0], one[1])[n]
            c = (0, HALF, 0, HALF, 0, 0)[n]
            return t[:, c:c + HALF]

        def bank4(n):
            return bank(n).rearrange("p (h i) -> p h i", h=4)

        def sems(names):
            return [sem(n) for n in names.split()]

        smalls_loaded, hi_made, lo_made, acc_ready = sems("smalls_loaded hi_made lo_made acc_ready")
        x_loaded = [sem(f"x_loaded{k}") for k in range(8)]
        raw_loaded = [sem(f"raw_loaded{s}") for s in range(2)]
        acc_read = [sem(f"acc_read{s}") for s in range(2)]
        norm_hi, norm_lo, sq_made, sq_added, stat_ready, rstd_ready = sems(
            "norm_hi norm_lo sq_made sq_added stat_ready rstd_ready")
        sq0_made, sq0_added = sems("sq0_made sq0_added")
        conv_done, silu_done, l2_sq, l2_sum, l2_ln, l2_inv, l2_done = sems(
            "conv_done silu_done l2_sq l2_sum l2_ln l2_inv l2_done")
        bd_ready, bd_scaled, bd_ln, neg_a_made, g_made, gc_ready, gc_read, gc_made = sems(
            "bd_ready bd_scaled bd_ln neg_a_made g_made gc_ready gc_read gc_made")
        (tiles_in, gb_made, gcb_ready, kk_ready, tok_ready, gamb_made, dtmp_made, dec_made, aT_made, vtok_made,
         keys_made, tt0_made, t0_ready, t0_made, aoff_made, n_ready, n_made, tn_ready, t_updated, wk_ready, nwk_made,
         wv_ready, w_made, o_ready, ds_ready, state_made, o_made, state_init) = sems(
            "tiles_in gb_made gcb_ready kk_ready tok_ready gamb_made dtmp_made dec_made aT_made vtok_made "
            "keys_made tt0_made t0_ready t0_made aoff_made n_ready n_made tn_ready t_updated wk_ready nwk_made "
            "wv_ready w_made o_ready ds_ready state_made o_made state_init")
        bias_loaded = sems("bias_loaded0 bias_loaded1")
        spilled = [sem(f"spilled{s}") for s in range(2)]
        gates_loaded = [sem(f"gates_loaded{s}") for s in range(2)]
        (qkv_loaded, z_loaded, vt_ready, vt_made, sc_ready, sc_read, max_made, pr_made, prT_ready, prT_made, oa_ready, ya_norm,
         yT_ready, yT_hi, yT_lo) = sems(
            "qkv_loaded z_loaded vt_ready vt_made sc_ready sc_read max_made pr_made prT_ready prT_made oa_ready ya_norm "
            "yT_ready yT_hi yT_lo")
        norm_o_done = sem("norm_o_done")
        o_sq, o_sum, o_ln, o_inv, o_normed, z_silu, yb_made, yb_h, yb_l = sems(
            "o_sq o_sum o_ln o_inv o_normed z_silu yb_made yb_h yb_l")
        gate_sig, merged_made, mg_h, mg_l = sems("gate_sig merged_made mg_h mg_l")
        f_silu, f_scaled, f_hi, f_lo = sems("f_silu f_scaled f_hi f_lo")
        p_loaded, p_hi, p_lo, pg_sig, x4_made, out_made, out_stored = sems(
            "p_loaded p_hi p_lo pg_sig x4_made out_made out_stored")

        class Num:

            def __init__(self, reg, step, base):
                self.reg, self.step, self.base = reg, step, base

            def __add__(self, n):
                return Num(self.reg, self.step, self.base + n)

            @property
            def parity(self):
                return self.base % 2

            @property
            def value(self):
                return self.base if self.reg is None else self.reg * self.step + self.base

            @property
            def turn(self):
                return self.base // 2 if self.reg is None else self.reg * (self.step // 2) + self.base // 2

        def num(n):
            return Num(None, 0, n)

        def lin(reg, step, base):
            return base if reg is None else reg * step + base

        def flat(t):
            return t[:, :, :].rearrange("p a b -> p (a b)")

        def half_of(h):
            return slice(h * HALF, (h + 1) * HALF)

        def settle(eng):
            eng.wait_ge(smalls_loaded, 32)

        def split_hi(act, n, dst, free):
            act.wait_ge(raw_loaded[n.parity], (n.turn + 1) * 16)
            if free is not None:
                act.wait_ge(acc_ready, free)
            nc.scalar.activation(dst, raw[n.parity][:, :], ACT.Copy).then_inc(hi_made, 1)

        def split_lo(pool, n, dst, hi):
            pool.wait_ge(hi_made, (n + 1).value)
            nc.gpsimd.tensor_tensor(dst, raw[n.parity][:, :], hi.bitcast(f32), ALU.subtract).then_inc(lo_made, 1)

        def fetch_hi(act, n, free):
            split_hi(act, n, flat(w_hi[n.parity]), free)

        def fetch_lo(pool, n):
            split_lo(pool, n, flat(w_lo[n.parity]), flat(w_hi[n.parity]))

        def fetch_down_hi(act, n, g, free):
            for r in range(2):
                split_hi(act, n + r, dw_hi[g][:, r, :], free)

        def fetch_down_lo(pool, n, g):
            for r in range(2):
                split_lo(pool, n + r, dw_lo[g][:, r, :], dw_hi[g][:, r, :])

        def project(pe, job, w, src, ks, block_no=None, source_wait=None):
            if block_no is not None:
                pe.wait_ge(lo_made, (block_no + 1).value)
            for half in range(2):
                if not (isinstance(job, int) and job == 0):
                    pe.wait_ge(acc_read[half], job)
                for n, (kw, kx) in enumerate(ks):
                    if source_wait is not None and half == 0:
                        source_wait(n)
                    for a, b in ((0, 0), (0, 1), (1, 0)):
                        last = nc.tensor.matmul(acc[half][:, :], w[a](kw), src[b][:, kx, half_of(half)],
                                                start=(n == 0 and a == b), stop=(n == len(ks) - 1 and a == 1))
                last.then_inc(acc_ready, 1)

        def fill(pe, jobs, cut):
            for s in range(*cut):
                n, half, k = jobs[s // 16], s % 16 // 8, s % 8
                if s % 16 == 0:
                    pe.wait_ge(lo_made, (n + 1).value)
                if k == 0:
                    pe.wait_ge(acc_read[half], n.value)
                for a, b in ((w_hi, h_hi), (w_hi, h_lo), (w_lo, h_hi)):
                    last = nc.tensor.matmul(acc[half][:, :], a[n.parity][:, k, :], b[:, k, half_of(half)],
                                            start=(k == 0 and b is h_hi and a is w_hi), stop=(k == 7 and a is w_lo))
                if k == 7:
                    last.then_inc(acc_ready, 1)

        def spills(jobs):
            return jobs * 16 + 16

        def stage_out(dve, n, half):
            dve.wait_ge(spilled[n.parity], spills((n + -JOB_A).turn))
            job_done(dve, n.value, half)
            nc.vector.tensor_tensor(stage[n.parity][:, half_of(half)], acc[half][:, :], rstd[:, half_of(half)],
                                    ALU.mult).then_inc(acc_read[half], 1)

        def ring(n):
            return (lambda k: w_hi[n.parity][:, k, :]), (lambda k: w_lo[n.parity][:, k, :])

        def down_w(g, j):
            return (lambda r: dw_hi[g][:, r, j * P:(j + 1) * P]), (lambda r: dw_lo[g][:, r, j * P:(j + 1) * P])

        ALL = [(k, k) for k in range(8)]
        hx, h2x, mgx = (h_hi, h_lo), (h2_hi, h2_lo), (mg_hi, mg_lo)

        def job_done(eng, job, half):
            eng.wait_ge(acc_ready, job * 2 + (half + 1))

        def evacuated(eng, job, half):
            eng.wait_ge(acc_read[half], job + 1)

        def stat_sum(pe, ss):
            for half in range(2):
                last = nc.tensor.matmul(pair_a[:, half_of(half)], ones, ss[:, half_of(half)], start=True, stop=True)
            last.then_inc(stat_ready, 1)

        def stat_rstd(act, n, scratch):
            act.wait_ge(stat_ready, n)
            nc.scalar.activation(scratch[:, :], pair_a[:, :], ACT.Ln, bias=eps_col, scale=1.0 / D)
            act.drain()
            nc.scalar.activation(rstd[:, :], scratch[:, :], ACT.Exp, scale=-0.5).then_inc(rstd_ready, 1)

        def residual_hi(act, job, j, half, gcol, count):
            act.wait_ge(acc_read[half], job + 1)
            nc.scalar.activation(h2_hi[:, j, half_of(half)], x_sb[:, j, half_of(half)], ACT.Copy,
                                 scale=params[:, gcol + j:gcol + j + 1]).then_inc(norm_hi, 1)
            squares(act, j, half, count)

        def squares(act, j, half, count):
            c = count + 2 * j + half
            if c >= 2:
                act.wait_ge(sq_added, c - 1)
            nc.scalar.activation(tmp[half][:, :], x_sb[:, j, half_of(half)], ACT.Square).then_inc(sq_made, 1)

        def residual_lo(dve, j, half, gcol, count):
            dve.wait_ge(norm_hi, count + 2 * j + half + 1)
            nc.vector.scalar_tensor_tensor(h2_lo[:, j, half_of(half)], x_sb[:, j, half_of(half)],
                                           params[:, gcol + j:gcol + j + 1],
                                           h2_hi[:, j, half_of(half)].bitcast(f32), ALU.mult, ALU.subtract
                                           ).then_inc(norm_lo, 1)

        def add_squares(pool, j, half, count):
            c = count + 2 * j + half
            pool.wait_ge(sq_made, c + 1)
            if j == 0:
                nc.gpsimd.tensor_copy(sumsq2[:, half_of(half)], tmp[half][:, :]).then_inc(sq_added, 1)
            else:
                pool.wait_ge(sq_added, c - 1)
                nc.gpsimd.tensor_tensor(sumsq2[:, half_of(half)], sumsq2[:, half_of(half)], tmp[half][:, :],
                                        ALU.add).then_inc(sq_added, 1)

        fill_b, fill_a = cuts(FILL_B), cuts(FILL_A)
        FETCH_STEP = [max(0, [e > 16 * c for s, e in fill_a].index(True)) for c in range(3)]
        HALF_STEP = [[e >= 8 * (h + 1) for s, e in fill_a].index(True) for h in range(6)]
        HALF_LEVEL = [[e >= 8 * (h + 1) for s, e in fill_b].index(True) for h in range(4)]

        block = ctx.enter_context(nc.Block())

        @block.sync
        def _(sp):
            sp.dma_start(consts[:, :], consts_d).then_inc(smalls_loaded, 16)
            sp.dma_start(params[:, :], params_d).then_inc(smalls_loaded, 16)
            for s in range(2):
                sp.dma_start(raw[s][:, :], blocks[s]).then_inc(raw_loaded[s], 16)

            def load(i, s):
                sp.wait_ge(lo_made, i * 2 + (s - 1))
                src = blocks[ds(i * 2 + s, 1)].rearrange("a p n -> (a p) n")
                sp.dma_start(raw[s][:, :], src).then_inc(raw_loaded[s], 16)

            def store(n):
                for half in range(2):
                    sp.wait_ge(acc_read[half], (n + 1).value)
                dst = spill[ds((n + -JOB_A).value, 1)].rearrange("a p n -> (a p) n")
                sp.dma_start(dst, stage[n.parity][:, :]).then_inc(spilled[n.parity], 16)

            with sp.Fori(1, (JOB_A + 3) // 2) as i:
                load(i, 0)
                load(i, 1)
            with sp.Fori((JOB_A + 3) // 2, (JOB_M + 3) // 2) as i:
                for s in range(2):
                    load(i, s)
                    store(Num(i, 2, s - 3))
            with sp.Fori((JOB_M + 3) // 2, N_BLK // 2) as i:
                load(i, 0)
                load(i, 1)
            if N_BLK % 2:
                sp.wait_ge(lo_made, N_BLK - 2)
                sp.dma_start(raw[(N_BLK - 1) % 2][:, :], blocks[N_BLK - 1]).then_inc(raw_loaded[(N_BLK - 1) % 2], 16)
            for j in range(8):
                sp.wait_ge(out_made, j + 1)
                sp.dma_start(out_t[j], out_sb[:, j, :]).then_inc(out_stored, 16)
            sp.wait_ge(out_stored, 16 * 8)

        @block.gpsimd
        def _(pool):
            g = nc.gpsimd
            fetch_lo(pool, num(0))
            fetch_lo(pool, num(1))
            with pool.Fori(1, 7) as i:
                fetch_lo(pool, Num(i, 2, 0))
                fetch_lo(pool, Num(i, 2, 1))
            with pool.Fori(0, TOK_TILES) as t:
                n = Num(t, 2, BLK_A)
                pool.wait_ge(aT_made, t + 1)
                for m in range(5):
                    g.tensor_tensor(aoff[m][:, :, :], aT[:, :, :], heads(level[m + 1]), ALU.mult
                                    ).then_inc(aoff_made, 1)
                fetch_lo(pool, n + 1)
                fetch_lo(pool, n + 2)

            def load(dst, row, ready):
                settle(pool)
                src = spill[row] if isinstance(row, int) else spill[ds(row, 1)].rearrange("a p n -> (a p) n")
                pool.dma_start(dst[:, :], src).then_inc(ready, 16)

            for s in range(2):
                pool.wait_ge(spilled[s], spills(8))
            pool.wait_ge(o_made, 8)
            pool.wait_ge(state_made, 16)
            for c, dst in enumerate((qa[0], ka[0], va)):
                load(dst, c, qkv_loaded)
            fetch_lo(pool, num(BLK_G + 1))
            fetch_lo(pool, num(BLK_G + 2))
            with pool.Fori(0, 2) as i:
                for q in range(2):
                    p = i * 2 + q
                    if q == 0:
                        pool.wait_ge(norm_o_done, i + 1)
                        for r in range(2):
                            for hh in range(2):
                                src = bias_d[ds(i * 4 + (2 * r + hh), 1)].rearrange("a p n -> (a p) n")
                                settle(pool)
                                pool.dma_start(biast[r][hh][:, :], src).then_inc(bias_loaded[hh], 16)
                    pool.wait_ge(vt_ready, p + 1)
                    for c, dst in enumerate((qa[1 - q], ka[1 - q], va)):
                        load(dst, p * 3 + (3 + c), qkv_loaded)
                    for c in range(3):
                        fetch_lo(pool, Num(i, 6, BLK_G + 3 + 3 * q + c))
            pool.wait_ge(oa_ready, 64)
            load(z_sb[3], 15, z_loaded)
            fetch_lo(pool, num(BLK_G + 15))
            fetch_lo(pool, num(BLK_M))
            for q in range(2):
                pool.wait_ge(yb_made, 2 * q + 2)
                for c in range(2):
                    load(gate_sb[q][c], 16 + 2 * q + c, gates_loaded[q])
            for s in range(2):
                pool.wait_ge(spilled[s], spills(16))

            def merge(i, ahead):
                for q in range(2):
                    fetch_lo(pool, Num(i, 2, BLK_M + q + 1))
                    if ahead:
                        pool.wait_ge(acc_read[1], i * 4 + (JOB_M + 2 * q + 2))
                        for c in range(2):
                            load(gate_sb[q][c], i * 4 + (20 + 2 * q + c), gates_loaded[q])

            with pool.Fori(0, 3) as i:
                merge(i, True)
            for q in range(2):
                fetch_lo(pool, num(BLK_M + 6 + q + 1))
            for j in range(8):
                fetch_lo(pool, num(BLK_O + j + 1))
                for half in range(2):
                    add_squares(pool, j, half, 0)

            def group(i, reg, gpar, step, last=False):
                n = Num(reg, 6 * step, BLK_F + 6 * i)
                for c in range(4):
                    if c < 3:
                        fetch_lo(pool, n + (c + 1))
                    else:
                        fetch_down_lo(pool, n + 4, gpar)
                        if not last:
                            fetch_lo(pool, n + 6)
                    if c % 2 == 0:
                        for half in range(2):
                            pool.wait_ge(f_silu, lin(reg, 4 * step, 4 * i + c + half + 1))
                            g.tensor_tensor(tmp[half][:, :], tmp[half][:, :], rstd[:, half_of(half)],
                                            ALU.mult).then_inc(f_scaled, 1)

            group(0, None, 0, 0)
            with pool.Fori(0, 4) as i:
                group(1, i, 1, 2)
                group(2, i, 0, 2)
            group(9, None, 1, 0)
            group(10, None, 0, 0, last=True)
            pool.wait_ge(acc_ready, 2 * JOB_T)
            pool.dma_start(p_raw[:, :, :], p_t.rearrange("k p n -> p k n")).then_inc(p_loaded, 16)
            fetch_down_lo(pool, num(BLK_PP), 1)
            fetch_lo(pool, num(BLK_PG))
            for j in range(8):
                for half in range(2):
                    add_squares(pool, j, half, 16)
            for j in range(8):
                if j < 7:
                    fetch_lo(pool, num(BLK_PG + j + 1))
                for half in range(2):
                    add_squares(pool, j, half, 32)

        @block.scalar
        def _(act):
            A = nc.scalar.activation
            for k in range(8):
                act.dma_start(x_sb[:, k, :], x_t[k]).then_inc(x_loaded[k], 16)
            act.wait_ge(smalls_loaded, 32)
            for k in range(8):
                act.wait_ge(x_loaded[k], 16)
                A(h_hi[:, k, :], x_sb[:, k, :], ACT.Copy, scale=params[:, P_GMIX + k:P_GMIX + k + 1]
                  ).then_inc(norm_hi, 1)
                if k >= 2:
                    act.wait_ge(sq0_added, k - 1)
                A(sq[k % 2][:, :], x_sb[:, k, :], ACT.Square).then_inc(sq0_made, 1)
                if k == 0:
                    fetch_hi(act, num(0), None)
                if k == 1:
                    fetch_hi(act, num(1), None)
            stat_rstd(act, 1, lnb)
            A(neg_a[:, :], params[:, P_ALOG:P_ALOG + 4], ACT.Exp).then_inc(neg_a_made, 1)

            def l2_inverse(idx):
                act.wait_ge(l2_sum, idx + 1)
                A(lnb[:, :], pair_b[:, :], ACT.Ln, bias=eps_col).then_inc(l2_ln, 1)
                act.drain()
                if not (isinstance(idx, int) and idx == 0):
                    act.wait_ge(l2_done, idx)
                A(inv_l2[:, :], lnb[:, :], ACT.Exp, scale=-0.5).then_inc(l2_inv, 1)

            def conv_step(n, sq_job, inverse_prev):
                j = n.value
                fetch_hi(act, n + 1, j * 2)
                act.wait_ge(conv_done, j)
                settle(act)
                A(mixb[:, (n + -1).value, :], conv[n.parity][:, :], ACT.Silu).then_inc(silu_done, 1)
                if inverse_prev:
                    l2_inverse((n + -6).value)
                if sq_job:
                    act.drain()
                    A(sqv[:, :], mixb[:, (n + -1).value, :], ACT.Square).then_inc(l2_sq, 1)

            for j in range(1, 7):
                conv_step(num(j), j > 4, j == 6)
            with act.Fori(3, 6) as i:
                conv_step(Num(i, 2, 1), True, True)
                conv_step(Num(i, 2, 2), True, True)
            l2_inverse(7)
            act.wait_ge(bd_scaled, 1)
            A(sp_a[:, :, :], gates8[:, :, 0:4], ACT.Exp, scale=-1.0)
            A(sp_b[:, :, :], gates8[:, :, 4:8], ACT.Exp, scale=-1.0)
            act.drain()
            A(sp_b[:, :, :], sp_b[:, :, :], ACT.Ln, bias=1.0).then_inc(bd_ln, 1)
            act.wait_ge(gc_ready, 1)
            A(gam[:, :], one[1][:, 0:32], ACT.Exp)
            A(neg_gc[:, :], one[1][:, 0:32], ACT.Copy, scale=-1.0).then_inc(gc_read, 1)
            act.wait_ge(gc_made, 1)
            A(kds[:, :], gdiff[:, :], ACT.Exp).then_inc(gc_read, 1)

            act.wait_ge(l2_done, 8)
            with act.Fori(0, TOK_TILES) as t:
                tok, n = ds(t * P, P), Num(t, 2, BLK_A)
                settle(act)
                A(kn[:, :, :], mixb[:, 4:8, tok], ACT.Copy).then_inc(tiles_in, 1)
                A(vn[:, :, :], mixb[:, 0:4, tok], ACT.Copy).then_inc(tiles_in, 1)
                act.wait_ge(gcb_ready, t + 1)
                A(gamb[:, :, :], bank4(0), ACT.Exp).then_inc(gamb_made, 1)
                act.wait_ge(dtmp_made, t + 1)
                settle(act)
                for h in range(4):
                    last = A(decT[:, h, :], dtmp[:, h, :], ACT.Exp, bias=neg_gc[:, ds(t * 4 + h, 1)])
                last.then_inc(dec_made, 1)
                act.wait_ge(tok_ready, t + 1)
                A(vtok[:, :, :], bank4(4), ACT.Copy).then_inc(vtok_made, 1)
                fetch_hi(act, n + 1, n.value * 2)
                act.wait_ge(t0_ready, t + 1)
                A(T[:, :, :], bank4(5), ACT.Copy).then_inc(t0_made, 1)
                for m in range(5):
                    act.wait_ge(n_ready, t * 5 + (m + 1))
                    A(Ns[:, :, :], bank4(0), ACT.Copy).then_inc(n_made, 1)
                act.wait_ge(wk_ready, t + 1)
                A(nwk[:, :, :], bank4(3), ACT.Copy, scale=-1.0).then_inc(nwk_made, 1)
                fetch_hi(act, n + 2, n.value * 2 + 2)
                act.wait_ge(o_ready, t + 1)
                settle(act)
                A(mixb[:, 8:12, tok], bank4(5), ACT.Copy).then_inc(o_made, 1)

            act.wait_ge(state_made, 16)
            act.drain()
            for c in range(4):
                for d in ((0, 1) if c == 0 else (c + 1,) if c < 3 else ()):
                    if d >= 2:
                        act.wait_ge(o_sum, d - 1)
                    A(osq[d % 2][:, :], mixb[:, 8 + d, :], ACT.Square).then_inc(o_sq, 1)
                act.drain()
                act.wait_ge(o_sum, c + 1)
                A(oln[:, :], (pair_a, pair_b)[c % 2][:, :], ACT.Ln, bias=eps_col, scale=1.0 / B_DIM).then_inc(o_ln, 1)
                act.drain()
                if c >= 2:
                    act.wait_ge(o_normed, c - 1)
                A(oinv[c % 2][:, :], oln[:, :], ACT.Exp, scale=-0.5).then_inc(o_inv, 1)
                if c == 0:
                    fetch_hi(act, num(BLK_G + 1), 2 * JOB_G)
            fetch_hi(act, num(BLK_G + 2), 2 * (JOB_G + 1))

            with act.Fori(0, 2) as i:
                for q in range(2):
                    p = i * 2 + q
                    act.wait_ge(vt_ready, p + 1)
                    A(flat(va_tok), pair_b[:, :], ACT.Copy).then_inc(vt_made, 1)
                    for u in range(19):
                        b, base = u % 2, p * 16
                        for c in range(3):
                            if FETCH_STEP[c] == u:
                                n = Num(i, 6, BLK_G + 2 + 3 * q + c)
                                fetch_hi(act, n + 1, n.value * 2)
                        if u < 16:
                            width = P * min(u // 2 + 1, 5)
                            act.wait_ge(max_made, base + (u + 1))
                            if u >= 2:
                                act.wait_ge(prT_ready, base + (u - 1))
                            A(pr[b][:, :width], sc[b][:, :width], ACT.Exp, bias=nmax[:, b:b + 1],
                              accum_out=psum_row[:, u % 4:u % 4 + 1]).then_inc(pr_made, 1)
                        if 1 <= u < 17:
                            width = P * min((u - 1) // 2 + 1, 5)
                            act.wait_ge(prT_ready, base + u)
                            if u >= 3:
                                act.wait_ge(oa_ready, base + (u - 2))
                            A(prT[1 - b][:, :width], pair_b[:, :width], ACT.Copy).then_inc(prT_made, 1)
                        if u >= 4 and u % 2 == 0:
                            tt = (u - 4) // 2
                            act.wait_ge(yT_ready, p * 8 + (tt + 1))
                            settle(act)
                            A(ya_hi[:, p, tt * P:(tt + 1) * P], one[1][:, P:2 * P], ACT.Copy).then_inc(yT_hi, 1)

            fetch_hi(act, num(BLK_G + 15), 2 * (JOB_G + 14))
            act.wait_ge(qkv_loaded, 5 * 48)
            for c in range(3):
                A(z_sb[c][:, :], z_sb[c][:, :], ACT.Silu).then_inc(z_silu, 1)
            act.wait_ge(z_loaded, 16)
            A(z_sb[3][:, :], z_sb[3][:, :], ACT.Silu).then_inc(z_silu, 1)
            act.wait_ge(oa_ready, 64)
            for c in range(4):
                act.wait_ge(yb_made, c + 1)
                A(yb_hi[:, c, :], mixb[:, 8 + c, :], ACT.Copy).then_inc(yb_h, 1)
            fetch_hi(act, num(BLK_M), 2 * (JOB_G + 15))
            act.wait_ge(yb_l, 4)
            for k in range(4):
                act.dma_start(x_sb[:, k, :], x_t[k]).then_inc(x_loaded[k], 16)

            with act.Fori(0, 4) as i:
                for q in range(2):
                    n, j = Num(i, 2, BLK_M + q), i * 2 + q
                    fetch_hi(act, n + 1, i * 8 + (2 * JOB_M + 4 * q))
                    act.wait_ge(gates_loaded[q], i * 32 + 32)
                    for c in range(2):
                        A(gate_sb[q][c][:, :], gate_sb[q][c][:, :], ACT.Sigmoid).then_inc(gate_sig, 1)
                    act.wait_ge(merged_made, j + 1)
                    settle(act)
                    A(mg_hi[:, j, :], prod[0][:, :], ACT.Copy).then_inc(mg_h, 1)
            act.wait_ge(acc_read[1], JOB_O)
            for k in range(4, 8):
                act.dma_start(x_sb[:, k, :], x_t[k]).then_inc(x_loaded[k], 16)

            for j in range(8):
                n = BLK_O + j
                fetch_hi(act, num(n + 1), 2 * (JOB_O + j))
                for half in range(2):
                    residual_hi(act, JOB_O + j, j, half, P_GFFN, 0)
            stat_rstd(act, 2, sumsq2)

            def group(i, reg, gpar, step, last=False):
                n = Num(reg, 6 * step, BLK_F + 6 * i)
                if reg is None:
                    jobs = ffn_jobs(i)[0]
                    before = ffn_jobs(i - 1)[0] if i else [0, 0, 0, JOB_O + 7]
                    down_free = 2 * (ffn_jobs(i - 1)[0][3] + 3) if i > 1 else 2 * JOB_F
                else:
                    jobs = [reg * (12 * step) + v for v in ffn_jobs(i)[0]]
                    before = [None, None, None, reg * (12 * step) + (ffn_jobs(i)[0][0] - 3)]
                    down_free = reg * (24 * step) + 2 * ffn_jobs(i)[0][0]
                for c in range(4):
                    free = before[3] if c == 0 else jobs[c - 1]
                    if c < 3:
                        fetch_hi(act, n + (c + 1), (free + 1) * 2)
                    else:
                        fetch_down_hi(act, n + 4, gpar, down_free)
                        if not last:
                            fetch_hi(act, n + 6, (free + 1) * 2)
                    for half in range(2):
                        if c % 2 == 0:
                            evacuated(act, jobs[c], half)
                            A(tmp[half][:, :], tmp[half][:, :], ACT.Silu).then_inc(f_silu, 1)
                        else:
                            evacuated(act, jobs[c], half)
                            A(hid_hi[gpar][:, c // 2, half_of(half)], tmp[2 + half][:, :], ACT.Copy
                              ).then_inc(f_hi, 1)

            group(0, None, 0, 0)
            with act.Fori(0, 4) as i:
                group(1, i, 1, 2)
                group(2, i, 0, 2)
            group(9, None, 1, 0)
            group(10, None, 0, 0, last=True)
            fetch_down_hi(act, num(BLK_PP), 1, 2 * JOB_T)
            fetch_hi(act, num(BLK_PG), 2 * JOB_T)
            act.wait_ge(p_loaded, 16)
            for k in range(2):
                A(hid_hi[1][:, k, :], p_raw[:, k, :], ACT.Copy).then_inc(p_hi, 1)
            for j in range(8):
                for half in range(2):
                    residual_hi(act, JOB_T + j, j, half, P_GPLE, 16)
            stat_rstd(act, 3, sumsq2)

            for j in range(8):
                if j < 7:
                    fetch_hi(act, num(BLK_PG + j + 1), 2 * (JOB_P + 2 * (j - 1) + 1) if j else 2 * JOB_T)
                for half in range(2):
                    evacuated(act, JOB_P + 2 * j, half)
                    A(tmp[2 + half][:, :], tmp[2 + half][:, :], ACT.Sigmoid).then_inc(pg_sig, 1)
                for half in range(2):
                    act.wait_ge(x4_made, 2 * j + half + 1)
                    squares(act, j, half, 32)
            stat_rstd(act, 4, sumsq2)

        @block.vector
        def _(dve):
            V = nc.vector
            TTs, STT, TS = V.tensor_tensor, V.scalar_tensor_tensor, V.tensor_scalar
            dve.wait_ge(smalls_loaded, 32)
            V.memset(convin[:, 0:4], 0.0)
            for k in range(8):
                dve.wait_ge(norm_hi, k + 1)
                STT(h_lo[:, k, :], x_sb[:, k, :], params[:, P_GMIX + k:P_GMIX + k + 1],
                    h_hi[:, k, :].bitcast(f32), ALU.mult, ALU.subtract).then_inc(norm_lo, 1)
                if k:
                    dve.wait_ge(sq0_added, k)
                dve.wait_ge(sq0_made, k + 1)
                if k == 0:
                    V.tensor_copy(sumsq[:, :], sq[0][:, :]).then_inc(sq0_added, 1)
                else:
                    TTs(sumsq[:, :], sumsq[:, :], sq[k % 2][:, :], ALU.add).then_inc(sq0_added, 1)

            def l2_scale(idx, job):
                dve.wait_ge(l2_inv, idx + 1)
                STT(mixb[:, job, :], mixb[:, job, :], consts[:, ds(C_QKS + job, 1)] if not isinstance(job, int)
                    else consts[:, C_QKS + job:C_QKS + job + 1], inv_l2[:, :], ALU.mult, ALU.mult).then_inc(l2_done, 1)

            def conv_step(n, scale_prev):
                j = n.value
                dve.drain()
                for half in range(2):
                    job_done(dve, j, half)
                    TTs(convin[:, 3 + half * HALF:3 + (half + 1) * HALF], acc[half][:, :], rstd[:, half_of(half)],
                        ALU.mult).then_inc(acc_read[half], 1)
                for w in range(CONV):
                    col = P_CONV + w - CONV + (j * CONV)
                    tap = params[:, col:col + 1] if isinstance(col, int) else params[:, ds(col, 1)]
                    dve.drain()
                    if w == 0:
                        if not (isinstance(j, int) and j < 3):
                            dve.wait_ge(silu_done, (n + -2).value)
                        last = TS(conv[n.parity][:, :], convin[:, 0:S], tap, None, ALU.mult)
                    else:
                        last = STT(conv[n.parity][:, :], convin[:, w:w + S], tap, conv[n.parity][:, :], ALU.mult, ALU.add)
                last.then_inc(conv_done, 1)
                if scale_prev:
                    l2_scale((n + -6).value, (n + -2).value)

            dve.wait_ge(rstd_ready, 1)
            for half in range(2):
                job_done(dve, 0, half)
                TTs(bd_rows[:, half_of(half)], acc[half][0:8, :], rstd[0:8, half_of(half)], ALU.mult
                    ).then_inc(acc_read[half], 1)
            for j in range(1, 7):
                conv_step(num(j), j == 6)
            with dve.Fori(3, 6) as i:
                conv_step(Num(i, 2, 1), True)
                conv_step(Num(i, 2, 2), True)
            dve.drain()
            dve.wait_ge(bd_ready, 1)
            V.tensor_copy(gates8[:, :, :], one[0][:, 0:64].rearrange("p (t c) -> p t c", t=8))
            dve.drain()
            TTs(gates8[:, :, 4:8], gates8[:, :, 4:8],
                params[:, P_DTB:P_DTB + 4].unsqueeze(1).to_broadcast([P, 8, 4]), ALU.add)
            dve.drain()
            g4 = g_log[:, :].rearrange("p (t c) -> p t c", t=8)
            b4 = beta[:, :].rearrange("p (t c) -> p t c", t=8)
            TS(g4, gates8[:, :, 4:8], 0.0, None, ALU.max)
            TS(b4, gates8[:, :, 4:8], -1.0, None, ALU.mult)
            dve.drain()
            TTs(gates8[:, :, 4:8], gates8[:, :, 4:8], b4, ALU.max).then_inc(bd_scaled, 1)
            dve.wait_ge(bd_ln, 1)
            TS(b4, sp_a[:, :, :], 1.0, None, ALU.add)
            TTs(g4, g4, sp_b[:, :, :], ALU.add)
            dve.drain()
            V.reciprocal(beta[:, :], beta[:, :])
            dve.wait_ge(neg_a_made, 1)
            STT(g4, g4, -1.0, neg_a[:, :].unsqueeze(1).to_broadcast([P, 8, 4]), ALU.mult, ALU.mult).then_inc(g_made, 1)
            dve.wait_ge(gc_ready, 1)
            dve.wait_ge(gc_read, 1)
            V.tensor_copy(gdiff[:, :], one[1][:, 32:64])
            dve.drain()
            TTs(gdiff[:, :], gdiff[:, :], one[1][:, 0:32], ALU.subtract).then_inc(gc_made, 1)
            l2_scale(7, 11)
            V.memset(state[:, :, :], 0.0).then_inc(state_init, 1)
            for s in range(2):
                V.memset(stage[s][:, 0:1], 0.0).then_inc(spilled[s], 16)
            dve.wait_ge(gc_read, 2)

            with dve.Fori(0, TOK_TILES) as t:
                tok = ds(t * P, P)
                jobs = [Num(t, 2, JOB_A + c) for c in range(2)]

                def column(a):
                    return a[:, ds(t * 4, 4)].unsqueeze(2).to_broadcast([P, 4, P])

                TTs(gb[:, :, :], heads(ones), column(g_log), ALU.mult).then_inc(gb_made, 1)
                dve.wait_ge(gcb_ready, t + 1)
                dve.wait_ge(gamb_made, t + 1)
                TTs(dtmp[:, :, :], bank4(0), heads(decay_mask), ALU.add).then_inc(dtmp_made, 1)
                TTs(qg[:, :, :], mixb[:, 8:12, tok], gamb[:, :, :], ALU.mult)
                dve.wait_ge(dec_made, t + 1)
                dve.wait_ge(kk_ready, t + 1)
                for h in range(4):
                    last = STT(aT[:, h, :], decT[:, h, :], beta[:, ds(t * 4 + h, 1)], bank4(1)[:, h, :],
                               ALU.mult, ALU.mult)
                last.then_inc(aT_made, 1)
                dve.drain()
                TTs(TT[:, :, :], aT[:, :, :], heads(level[0]), ALU.mult)
                dve.drain()
                TTs(TT[:, :, :], heads(ident), TT[:, :, :], ALU.subtract).then_inc(tt0_made, 1)
                TTs(pT_[:, :, :], bank4(2), decT[:, :, :], ALU.mult)
                dve.wait_ge(tok_ready, t + 1)
                TTs(gk[:, :, :], bank4(3), column(gam), ALU.mult)
                TTs(kdec[:, :, :], bank4(3), column(kds), ALU.mult).then_inc(keys_made, 1)
                dve.wait_ge(t0_made, t + 1)
                for n in range(5):
                    dve.wait_ge(tn_ready, t * 5 + (n + 1))
                    if n < 4:
                        TTs(T[:, :, :], T[:, :, :], bank4(1), ALU.subtract)
                    TTs(TT[:, :, :], TT[:, :, :], bank4(2), ALU.subtract).then_inc(t_updated, 1)
                    for h in range(3):
                        if (HALF_LEVEL[h] - 3) // 2 == n:
                            stage_out(dve, jobs[h // 2], h % 2)
                for c in range(2):
                    r = slice(c * CHUNK, (c + 1) * CHUNK)
                    dve.wait_ge(wv_ready, t * 2 + (c + 1))
                    TTs(w_[r, :, :], bank4(4)[r, :, :],
                        beta[r, ds(t * 4, 4)].unsqueeze(2).to_broadcast([CHUNK, 4, P]), ALU.mult).then_inc(w_made, 1)
                    dve.wait_ge(ds_ready, t * 2 + (c + 1))
                    end = (c + 1) * CHUNK - 1
                    for h in range(4):
                        last = STT(state[:, h, :], state[:, h, :], gamb[:, h, end:end + 1], bank4(0)[:, h, :],
                                   ALU.mult, ALU.add)
                    last.then_inc(state_made, 1)
                stage_out(dve, jobs[1], 1)

            for c in range(4):
                if c % 2:
                    for half in range(2):
                        stage_out(dve, num(JOB_G + c // 2), half)
                dve.wait_ge(o_inv, c + 1)
                last = STT(mixb[:, 8 + c, :], mixb[:, 8 + c, :], params[:, P_ONORM:P_ONORM + 1], oinv[c % 2][:, :],
                           ALU.mult, ALU.mult)
                last.then_inc(o_normed, 1)

            V.memset(rsum[:, :], 0.0).then_inc(norm_o_done, 1)
            with dve.Fori(0, 2) as i:
                for q in range(2):
                    p = i * 2 + q
                    for hh in range(2):
                        dve.wait_ge(bias_loaded[hh], i * 32 + 32)
                    for u in range(19):
                        b, base = u % 2, p * 16
                        if u < 16:
                            width = P * min(u // 2 + 1, 5)
                            dve.wait_ge(sc_ready, base + (u + 1))
                            if u >= 2:
                                dve.wait_ge(pr_made, base + (u - 1))
                            STT(sc[b][:, :width], pair_a[:, :width], A_DIM ** -0.5,
                                biast[q][u % 2][:, WINDOW - width:], ALU.mult, ALU.add).then_inc(sc_read, 1)
                            dve.drain()
                            V.tensor_reduce(nmax[:, b:b + 1], sc[b][:, :width], AX.X, ALU.max, negate=True
                                            ).then_inc(max_made, 1)
                        if 2 <= u < 18:
                            v, vb = u - 2, u % 2
                            tt = v // 2
                            dve.wait_ge(oa_ready, base + (v + 1))
                            V.reciprocal(rsum[:, vb:vb + 1], psum_row[:, v % 4:v % 4 + 1])
                            dve.drain()
                            if tt >= 2:
                                dve.wait_ge(yT_ready, p * 8 + (tt - 1))
                            TS(ytok[tt % 2][:, (v % 2) * 64:(v % 2) * 64 + 64], one[vb][:, 0:64], rsum[:, vb:vb + 1],
                               None, ALU.mult).then_inc(ya_norm, 1)
                        if u >= 4 and u % 2 == 0:
                            tt = (u - 4) // 2
                            dve.wait_ge(yT_hi, p * 8 + (tt + 1))
                            TTs(ya_lo[:, p, tt * P:(tt + 1) * P], one[1][:, P:2 * P],
                                ya_hi[:, p, tt * P:(tt + 1) * P].bitcast(f32), ALU.subtract).then_inc(yT_lo, 1)

                        for h in range(6):
                            if HALF_STEP[h] == u:
                                stage_out(dve, Num(i, 6, JOB_G + 2 + 3 * q + h // 2), h % 2)
                dve.drain()
                V.memset(rsum[:, :], 0.0).then_inc(norm_o_done, 1)

            def gated(c):
                dve.wait_ge(z_silu, c + 1)
                TTs(mixb[:, 8 + c, :], mixb[:, 8 + c, :], z_sb[c][:, :], ALU.mult).then_inc(yb_made, 1)

            def gated_lo(c):
                dve.wait_ge(yb_h, c + 1)
                TTs(yb_lo[:, c, :], mixb[:, 8 + c, :], yb_hi[:, c, :].bitcast(f32), ALU.subtract).then_inc(yb_l, 1)

            gated(0)
            gated(1)
            stage_out(dve, num(JOB_G + 14), 0)
            gated(2)
            gated_lo(0)
            stage_out(dve, num(JOB_G + 14), 1)
            gated(3)
            for c in range(1, 4):
                gated_lo(c)
            for half in range(2):
                stage_out(dve, num(JOB_G + 15), half)

            for s in range(2):
                dve.wait_ge(spilled[s], spills(16))
            with dve.Fori(0, 4) as i:
                for q in range(2):
                    j, job = i * 2 + q, i * 4 + (JOB_M + 2 * q)
                    for c in range(2):
                        dve.drain()
                        dve.wait_ge(gate_sig, i * 4 + (2 * q + c + 1))
                        for half in range(2):
                            cols = half_of(half)
                            job_done(dve, job + c, half)
                            TTs(prod[c][:, cols], acc[half][:, :], gate_sb[q][c][:, cols], ALU.mult
                                ).then_inc(acc_read[half], 1)
                    dve.drain()
                    TTs(prod[0][:, :], prod[0][:, :], prod[1][:, :], ALU.add).then_inc(merged_made, 1)
                    dve.wait_ge(mg_h, j + 1)
                    TTs(mg_lo[:, j, :], prod[0][:, :], mg_hi[:, j, :].bitcast(f32), ALU.subtract).then_inc(mg_l, 1)

            def residual(job, j, half):
                job_done(dve, job, half)
                TTs(x_sb[:, j, half_of(half)], x_sb[:, j, half_of(half)], acc[half][:, :], ALU.add
                    ).then_inc(acc_read[half], 1)

            for j in range(8):
                dve.wait_ge(x_loaded[j], 32)
                for half in range(2):
                    residual(JOB_O + j, j, half)
                dve.drain()
                for half in range(2):
                    residual_lo(dve, j, half, P_GFFN, 8)

            def group(i, reg, gpar, step):
                shift = 12 * step
                jobs = [lin(reg, shift, v) for v in ffn_jobs(i)[0]]
                downs = [lin(reg, shift, v) for v in ffn_jobs(i)[1]]
                for c in range(4):
                    tile_ = c // 2
                    dve.drain()
                    for half in range(2):
                        job_done(dve, jobs[c], half)
                        if c % 2 == 0:
                            TTs(tmp[half][:, :], acc[half][:, :], rstd[:, half_of(half)], ALU.mult
                                ).then_inc(acc_read[half], 1)
                        else:
                            dve.wait_ge(f_scaled, lin(reg, 4 * step, 4 * i + 2 * tile_ + half + 1))
                            TTs(tmp[2 + half][:, :], acc[half][:, :], tmp[half][:, :], ALU.mult
                                ).then_inc(acc_read[half], 1)
                    if c % 2:
                        for half in range(2):
                            dve.wait_ge(f_hi, lin(reg, 4 * step, 4 * i + 2 * tile_ + half + 1))
                            TTs(hid_lo[gpar][:, tile_, half_of(half)], tmp[2 + half][:, :],
                                hid_hi[gpar][:, tile_, half_of(half)].bitcast(f32), ALU.subtract).then_inc(f_lo, 1)
                    for j in (2 * c, 2 * c + 1):
                        if downs:
                            for half in range(2):
                                residual(downs[j], j, half)

            dve.wait_ge(rstd_ready, 2)
            group(0, None, 0, 0)
            with dve.Fori(0, 4) as i:
                group(1, i, 1, 2)
                group(2, i, 0, 2)
            group(9, None, 1, 0)
            group(10, None, 0, 0)
            dve.drain()
            for j in range(8):
                for half in range(2):
                    residual(JOB_T + j, j, half)
                if j == 0:
                    for k in range(2):
                        dve.wait_ge(p_hi, k + 1)
                        TTs(hid_lo[1][:, k, :], p_raw[:, k, :], hid_hi[1][:, k, :].bitcast(f32), ALU.subtract
                            ).then_inc(p_lo, 1)
                dve.drain()
                for half in range(2):
                    residual_lo(dve, j, half, P_GPLE, 24)

            dve.wait_ge(rstd_ready, 3)
            for j in range(8):
                dve.drain()
                for half in range(2):
                    job_done(dve, JOB_P + 2 * j, half)
                    TTs(tmp[2 + half][:, :], acc[half][:, :], rstd[:, half_of(half)], ALU.mult
                        ).then_inc(acc_read[half], 1)
                for half in range(2):
                    job_done(dve, JOB_P + 2 * j + 1, half)
                    dve.wait_ge(pg_sig, 2 * j + half + 1)
                    TTs(tmp[2 + half][:, :], acc[half][:, :], tmp[2 + half][:, :], ALU.mult).then_inc(acc_read[half], 1)
                dve.drain()
                for half in range(2):
                    TTs(x_sb[:, j, half_of(half)], x_sb[:, j, half_of(half)], tmp[2 + half][:, :], ALU.add
                        ).then_inc(x4_made, 1)
            dve.wait_ge(rstd_ready, 4)
            for j in range(8):
                STT(out_sb[:, j, :], x_sb[:, j, :], params[:, P_GFIN + j:P_GFIN + j + 1], rstd[:, :],
                    ALU.mult, ALU.mult).then_inc(out_made, 1)

        @block.tensor
        def _(pe):
            mm, tr = nc.tensor.matmul, nc.tensor.transpose

            def l2_sums(idx):
                pe.wait_ge(l2_sq, idx + 1)
                if not (isinstance(idx, int) and idx == 0):
                    pe.wait_ge(l2_ln, idx)
                for half in range(2):
                    last = mm(pair_b[:, half_of(half)], ones, sqv[:, half_of(half)], start=True, stop=True)
                last.then_inc(l2_sum, 1)

            pe.wait_ge(smalls_loaded, 32)
            project(pe, 0, ring(num(0)), hx, ALL, num(0), lambda n: pe.wait_ge(norm_lo, n + 1))
            pe.wait_ge(sq0_added, 8)
            stat_sum(pe, sumsq)
            for j in range(1, 7):
                project(pe, j, ring(num(j)), hx, ALL, num(j))
                if j == 1:
                    for half in range(2):
                        pe.wait_ge(acc_read[half], 1)
                    for t in range(TOK_TILES):
                        last = tr(one[0][:, t * 8:(t + 1) * 8], bd_rows[:, t * P:(t + 1) * P], ident[0:8, 0:8])
                    last.then_inc(bd_ready, 1)
                if j == 6:
                    l2_sums(0)
            with pe.Fori(3, 6) as i:
                for c in range(2):
                    n = Num(i, 2, 1 + c)
                    project(pe, n.value, ring(n), hx, ALL, n)
                    l2_sums((n + -6).value)
            l2_sums(7)
            pe.wait_ge(g_made, 1)
            mm(one[1][:, 0:32], cum, g_log[:, :], start=True, stop=True)
            mm(one[1][:, 32:64], chunk_ones, g_log[:, :], start=True, stop=True).then_inc(gc_ready, 1)
            pe.wait_ge(state_init, 1)
            pe.wait_ge(gc_made, 1)
            pe.wait_ge(gc_read, 2)
            with pe.Fori(0, TOK_TILES) as t:
                tok, jobs = ds(t * P, P), [Num(t, 2, JOB_A + c) for c in range(2)]
                place = iter(fill_b)
                pe.wait_ge(gb_made, t + 1)
                for h in range(4):
                    last = mm(bank4(0)[:, h, :], gb[:, h, :], cum, start=True, stop=True)
                last.then_inc(gcb_ready, 1)
                fill(pe, jobs, next(place))
                pe.wait_ge(tiles_in, t * 2 + 2)
                for h in range(4):
                    mm(bank4(1)[:, h, :], kn[:, h, :], kn[:, h, :], start=True, stop=True)
                for h in range(4):
                    last = mm(bank4(2)[:, h, :], kn[:, h, :], mixb[:, 8 + h, tok], start=True, stop=True)
                last.then_inc(kk_ready, 1)
                for h in range(4):
                    tr(bank4(3)[:, h, :], kn[:, h, :], ident)
                for h in range(4):
                    last = tr(bank4(4)[:, h, :], vn[:, h, :], ident)
                last.then_inc(tok_ready, 1)
                fill(pe, jobs, next(place))
                pe.wait_ge(tt0_made, t + 1)
                for h in range(4):
                    last = tr(bank4(5)[:, h, :], TT[:, h, :], ident)
                last.then_inc(t0_ready, 1)
                fill(pe, jobs, next(place))
                pe.wait_ge(t0_made, t + 1)
                for n in range(5):
                    if n == 0:
                        pe.wait_ge(dtmp_made, t + 1)
                        pe.wait_ge(keys_made, t + 1)
                    else:
                        pe.wait_ge(t_updated, t * 5 + n)
                    pe.wait_ge(aoff_made, t * 5 + (n + 1))
                    for h in range(4):
                        last = mm(bank4(0)[:, h, :], aoff[n][:, h, :], T[:, h, :], start=True, stop=True)
                    last.then_inc(n_ready, 1)
                    fill(pe, jobs, next(place))
                    pe.wait_ge(n_made, t * 5 + (n + 1))
                    for h in range(4):
                        if n < 4:
                            mm(bank4(1)[:, h, :], TT[:, h, :], Ns[:, h, :], start=True, stop=True)
                        last = mm(bank4(2)[:, h, :], Ns[:, h, :], TT[:, h, :], start=True, stop=True)
                    last.then_inc(tn_ready, 1)
                    fill(pe, jobs, next(place))
                pe.wait_ge(t_updated, t * 5 + 5)
                for h in range(4):
                    last = mm(bank4(3)[:, h, :], gk[:, h, :], TT[:, h, :], start=True, stop=True)
                last.then_inc(wk_ready, 1)
                fill(pe, jobs, next(place))
                pe.wait_ge(nwk_made, t + 1)
                pe.wait_ge(vtok_made, t + 1)
                for c in range(2):
                    r = slice(c * CHUNK, (c + 1) * CHUNK)
                    if c:
                        pe.wait_ge(state_made, t * 2 + c)
                    for h in range(4):
                        mm(bank4(4)[r, h, :], TT[:, h, r], vtok[:, h, :], start=True, stop=False)
                        last = mm(bank4(4)[r, h, :], nwk[:, h, r], state[:, h, :], start=False, stop=True)
                    last.then_inc(wv_ready, 1)
                    fill(pe, jobs, next(place))
                    pe.wait_ge(w_made, t * 2 + (c + 1))
                    for h in range(4):
                        mm(bank4(5)[:, h, r], state[:, h, :], qg[:, h, r], start=True, stop=False)
                        last = mm(bank4(5)[:, h, r], w_[r, h, :], pT_[r, h, r], start=False, stop=True)
                    if c:
                        last.then_inc(o_ready, 1)
                    for h in range(4):
                        last = mm(bank4(0)[:, h, :], kdec[r, h, :], w_[r, h, :], start=True, stop=True)
                    last.then_inc(ds_ready, 1)
                    if c == 0:
                        fill(pe, jobs, next(place))

            jobs = [num(JOB_G), num(JOB_G + 1)]
            pe.wait_ge(o_made, 8)
            pe.wait_ge(state_made, 16)
            for c in range(4):
                fill(pe, jobs, (8 * c, 8 * c + 8))
                pe.wait_ge(o_sq, c + 1)
                if c >= 2:
                    pe.wait_ge(o_ln, c - 1)
                for half in range(2):
                    last = mm((pair_a, pair_b)[c % 2][:, half_of(half)], ones, osq[c % 2][:, half_of(half)],
                              start=True, stop=True)
                last.then_inc(o_sum, 1)
            pe.wait_ge(o_ln, 4)
            with pe.Fori(0, 2) as i:
                for q in range(2):
                    p = i * 2 + q
                    base = p * 16
                    jobs = [Num(i, 6, JOB_G + 2 + 3 * q + c) for c in range(3)]
                    pe.wait_ge(qkv_loaded, p * 48 + 48)
                    for tt in range(8):
                        last = tr(pair_b[:, tt * P:(tt + 1) * P], va[:, tt * P:(tt + 1) * P], ident)
                    last.then_inc(vt_ready, 1)
                    pe.wait_ge(vt_made, p + 1)
                    for u in range(19):
                        if u < 16:
                            tt, r = u // 2, slice(64 * (u % 2), 64 * (u % 2) + 64)
                            tiles = min(tt + 1, 5)
                            k0, width = (tt + 1 - tiles) * P, tiles * P
                            if u:
                                pe.wait_ge(sc_read, base + u)
                            for a in range(0, width, HALF):
                                e = min(width, a + HALF)
                                last = mm(pair_a[:, a:e], qa[q][r, tt * P:(tt + 1) * P], ka[q][r, k0 + a:k0 + e],
                                          start=True, stop=True)
                            last.then_inc(sc_ready, 1)
                        fill(pe, jobs, fill_a[u])
                        if 1 <= u < 17:
                            v = u - 1
                            tiles = min(v // 2 + 1, 5)
                            pe.wait_ge(pr_made, base + u)
                            if v:
                                pe.wait_ge(prT_made, base + v)
                            for kt in range(tiles):
                                last = tr(pair_b[:, kt * P:(kt + 1) * P], pr[v % 2][:, kt * P:(kt + 1) * P], ident)
                            last.then_inc(prT_ready, 1)
                        if u >= 4 and u % 2 == 0:
                            tt = (u - 4) // 2
                            pe.wait_ge(ya_norm, base + (2 * tt + 2))
                            tr(one[1][:, P:2 * P], ytok[tt % 2][:, :], ident).then_inc(yT_ready, 1)
                        if 2 <= u < 18:
                            v = u - 2
                            tt, r = v // 2, slice(64 * (v % 2), 64 * (v % 2) + 64)
                            tiles = min(tt + 1, 5)
                            pe.wait_ge(prT_made, base + (v + 1))
                            if v >= 2 and v % 2:
                                pe.wait_ge(yT_lo, p * 8 + tt)
                            elif v >= 2:
                                pe.wait_ge(ya_norm, base + (v - 1))
                            for kt in range(tiles):
                                last = mm(one[v % 2][:, 0:64], prT[v % 2][:, kt * P:(kt + 1) * P],
                                          va_tok[:, tt + 1 - tiles + kt, r], start=(kt == 0), stop=(kt == tiles - 1))
                            last.then_inc(oa_ready, 1)

            for c in (14, 15):
                n = num(JOB_G + c)
                project(pe, n.value, ring(n), hx, ALL, n)

            pe.wait_ge(yT_lo, 32)
            with pe.Fori(0, 4) as i:
                for q in range(2):
                    n, job = Num(i, 2, BLK_M + q), i * 4 + (JOB_M + 2 * q)
                    project(pe, job, ring(n), (ya_hi, ya_lo), [(k, k) for k in range(4)], n)
                    pe.wait_ge(yb_l, 4)
                    project(pe, job + 1, ring(n), (yb_hi, yb_lo), [(4 + k, k) for k in range(4)])
            for j in range(8):
                project(pe, JOB_O + j, ring(num(BLK_O + j)), mgx, ALL, num(BLK_O + j),
                        (lambda n: pe.wait_ge(mg_l, n + 1)) if j == 0 else None)

            def group(i, reg, gpar, step):
                shift = 12 * step
                jobs = [lin(reg, shift, v) for v in ffn_jobs(i)[0]]
                downs = [lin(reg, shift, v) for v in ffn_jobs(i)[1]]
                n = Num(reg, 6 * step, BLK_F + 6 * i)
                for c in range(4):
                    wait = (lambda k: pe.wait_ge(norm_lo, 8 + 2 * k + 2)) if i == 0 and reg is None and c == 0 else None
                    project(pe, jobs[c], ring(n + c), h2x, ALL, n + c, wait)
                    if wait is not None:
                        pe.wait_ge(sq_added, 16)
                        stat_sum(pe, sumsq2)
                    if downs:
                        if c == 0:
                            pe.wait_ge(f_lo, lin(reg, 4 * step, 4 * i))
                        for j in (2 * c, 2 * c + 1):
                            project(pe, downs[j], down_w(1 - gpar, j), (hid_hi[1 - gpar], hid_lo[1 - gpar]),
                                    [(0, 0), (1, 1)])

            group(0, None, 0, 0)
            with pe.Fori(0, 4) as i:
                group(1, i, 1, 2)
                group(2, i, 0, 2)
            group(9, None, 1, 0)
            group(10, None, 0, 0)
            pe.wait_ge(f_lo, 4 * GROUPS)
            pe.wait_ge(lo_made, BLK_F + 6 * GROUPS)
            for j in range(8):
                project(pe, JOB_T + j, down_w(0, j), (hid_hi[0], hid_lo[0]), [(0, 0), (1, 1)])
            for j in range(8):
                project(pe, JOB_P + 2 * j, ring(num(BLK_PG + j)), h2x, ALL, num(BLK_PG + j),
                        (lambda k: pe.wait_ge(norm_lo, 24 + 2 * k + 2)) if j == 0 else None)
                if j == 0:
                    pe.wait_ge(sq_added, 32)
                    stat_sum(pe, sumsq2)
                    pe.wait_ge(p_lo, 2)
                project(pe, JOB_P + 2 * j + 1, down_w(1, j), (hid_hi[1], hid_lo[1]), [(0, 0), (1, 1)])
            pe.wait_ge(sq_added, 48)
            stat_sum(pe, sumsq2)


def constants():
    c = np.zeros((P, N_CONST), np.float32)
    j, i = np.arange(P)[:, None], np.arange(P)[None, :]
    same = j // CHUNK == i // CHUNK
    c[:, C_IDENT:C_IDENT + P] = j == i
    c[:, C_ONES:C_ONES + P] = 1.0
    c[:, C_CUM:C_CUM + P] = same & (j <= i)
    c[:, C_CHUNK:C_CHUNK + P] = same
    c[:, C_MASK:C_MASK + P] = np.where(same & (j <= i), 0.0, NEG)
    for n, b in enumerate(LEVELS):
        c[:, C_LEVEL + P * n:C_LEVEL + P * (n + 1)] = (j // (2 * b) == i // (2 * b)) & (i % (2 * b) >= b) & (j % (2 * b) < b)
    c[:, C_EPS] = EPS
    c[:, C_QKS:C_QKS + 8] = 1.0
    c[:, C_QKS + 8:C_QKS + 12] = B_DIM ** -0.5
    return c


def kernel(**inputs):
    import concourse.bacc as bacc
    from concourse.bass_utils import run_bass_kernel_spmd

    a = {k: np.asarray(v) for k, v in inputs.items()}
    f = np.float32
    w_in = a["w_in"][0]
    aw, qkv = A_HEADS * A_DIM, B_HEADS * B_DIM

    def col_blocks(w):
        k, n = w.shape[0] // P, w.shape[1] // P
        return w.reshape(k, P, n, P).transpose(2, 1, 0, 3).reshape(n, P, k * P)

    qa, ka, va = (col_blocks(w_in[:, aw * n:aw * (n + 1)]) for n in range(3))
    o = 3 * aw
    qb, kb, vb, z = (col_blocks(w_in[:, o + qkv * n:o + qkv * (n + 1)]) for n in range(4))
    o += 4 * qkv
    wbd = np.zeros((D, P), f)
    wbd[:, :8] = w_in[:, o:o + 8]
    ga, gb = col_blocks(w_in[:, o + 8:o + 8 + D]), col_blocks(w_in[:, o + 8 + D:o + 8 + 2 * D])
    wa, wb = col_blocks(a["w_branch_a"][0]), col_blocks(a["w_branch_b"][0])
    gate, up = col_blocks(a["w_gate_up"][0][:, :D_FF]), col_blocks(a["w_gate_up"][0][:, D_FF:])
    down = a["w_down"][0].reshape(D_FF // P, P, D)
    parts = [col_blocks(wbd), vb, kb, qb, np.stack([qa, ka, va], 1), z,
             np.stack([ga, gb], 1), np.concatenate([wa, wb], 2), col_blocks(a["w_out"][0])]
    for g in range(GROUPS):
        parts += [gate[2 * g], up[2 * g], gate[2 * g + 1], up[2 * g + 1], down[2 * g], down[2 * g + 1]]
    parts += [a["w_ple_proj"][0].reshape(2, P, D), col_blocks(a["w_ple_gate"][0])]
    blocks = np.concatenate([x.reshape(-1, P, D) for x in parts]).astype(f, copy=False)
    assert blocks.shape[0] == N_BLK

    params = np.zeros((P, N_PARAM), f)
    for c, g in ((P_GMIX, a["g_mix"][0]), (P_GFFN, a["g_ffn"][0]), (P_GPLE, a["g_ple"][0]), (P_GFIN, a["g_final"])):
        params[:, c:c + 8] = g.reshape(8, P).T
    cw = a["conv_w"][0].reshape(CONV, 3, B_HEADS, P)[:, ::-1]
    params[:, P_CONV:P_CONV + 12 * CONV] = cw.reshape(CONV, 12, P).transpose(2, 1, 0).reshape(P, 48)
    params[:, P_ONORM] = a["w_onorm"][0]
    params[:, P_ALOG:P_ALOG + 4] = a["a_log"][0][None]
    params[:, P_DTB:P_DTB + 4] = a["dt_bias"][0][None]

    qi, kj = np.arange(P)[:, None], np.arange(WINDOW)[None, :]
    idx = np.clip(WINDOW - P + qi - kj, -REL_CLIP, REL_CLIP) + REL_CLIP
    chunks = kj // CHUNK - qi // CHUNK
    bias = np.where((chunks >= 0) & (chunks <= LOOKBACK), a["rel_bias"][0][:, idx], f(NEG)).astype(f, copy=False)

    x_t = np.ascontiguousarray(a["x"][0].T).reshape(8, P, S)
    p_t = np.ascontiguousarray(a["p"][0, 0].T).reshape(2, P, S)
    arrays = {"x_t": x_t, "p_t": p_t, "blocks": blocks, "consts": constants(), "params": params, "bias": bias}
    nc = bacc.Bacc("TRN2", target_bir_lowering=False, num_devices=1)
    aps = [nc.dram_tensor(n, v.shape, mybir.dt.float32, kind="ExternalInput").ap() for n, v in arrays.items()]
    aps.append(nc.dram_tensor("out_t", (8, P, S), mybir.dt.float32, kind="ExternalOutput").ap())
    aps.append(nc.dram_tensor("spill", (JOB_M - JOB_A, P, S), mybir.dt.float32, kind="Internal").ap())
    hybrid_block(nc, *aps)
    r = run_bass_kernel_spmd(nc, [arrays], core_ids=[0])
    return np.ascontiguousarray(r.results[0]["out_t"].reshape(D, S).T).reshape(1, S, D)
```

```python
import numpy as np
import concourse.bass as bass
from concourse import mybir
from contextlib import ExitStack

S, D, P = 1024, 1024, 128
KT = D // P
HALF = 512
TOK_TILES = S // P
CHUNK = 64
A_HEADS, A_DIM, LOOKBACK, REL_CLIP = 8, 64, 8, 128
PAIRS = A_HEADS // 2
WINDOW = 5 * P
B_HEADS, B_DIM = 4, 128
CONV = 4
D_FF = 2816
GROUPS = D_FF // (2 * P)
EPS = 1e-6
NEG = -1e30

C_IDENT, C_ONES, C_CUM, C_CHUNK, C_MASK, C_LEVEL = 0, 128, 256, 384, 512, 640
LEVELS = (1, 2, 4, 8, 16, 32)
C_EPS = C_LEVEL + 128 * len(LEVELS)
C_QKS = C_EPS + 1
N_CONST = C_QKS + 12
P_GMIX, P_GFFN, P_GPLE, P_GFIN, P_CONV = 0, 8, 16, 24, 32
P_ONORM = P_CONV + 12 * CONV
P_ALOG, P_DTB = P_ONORM + 1, P_ONORM + 5
N_PARAM = P_ONORM + 9

BLK_A, BLK_G, BLK_M = 13, 29, 45
BLK_O = BLK_M + 8
BLK_F = BLK_O + 8
BLK_P = BLK_F + 6 * GROUPS
N_BLK = BLK_P + 2 + 16
JOB_A, JOB_G, JOB_M = BLK_A, BLK_G, BLK_M
JOB_O = JOB_M + 2 * 8
JOB_F = JOB_O + 8
JOB_T = JOB_F + 4 + 12 * (GROUPS - 1)
JOB_P = JOB_T + 8

FILL_B = (1, 3, 2) + (2, 2) * 4 + (1, 2) + (2, 1, 1, 2, 1)
FILL_A = (4, 3, 3, 3, 3, 3, 3, 3, 2, 2, 2, 2, 2, 2, 2, 2, 2, 2, 3)


def ffn_jobs(i):
    if isinstance(i, int) and i == 0:
        return [JOB_F + c for c in range(4)], []
    base = JOB_F + 4 + (i - 1) * 12
    return [base + 3 * c for c in range(4)], [base + 3 * (n // 2) + 1 + n % 2 for n in range(8)]


def ple_block(m):
    return BLK_P + m + (2 if m else 0)


def cuts(counts):
    ends = [sum(counts[:n + 1]) for n in range(len(counts))]
    return list(zip([0] + ends, ends))


def hybrid_block(nc, x_t, p_t, blocks, consts_d, params_d, bias_d, out_t, spill):
    f32, f32r = mybir.dt.float32, mybir.dt.float32r
    ALU, ACT, AX = mybir.AluOpType, mybir.ActivationFunctionType, mybir.AxisListType
    ds = bass.ds

    ctx = ExitStack()
    with ctx:
        BASE = 16512
        K = 1024

        def at(name, shape, dt, offset):
            return nc.alloc_sbuf_tensor_at(name, shape, dt, offset=BASE + offset)

        def sem(name):
            return ctx.enter_context(nc.semaphore(name))

        h_hi = at("h_hi", [P, 8, S], f32r, 0)
        h_lo = at("h_lo", [P, 8, S], f32r, 32 * K)
        mg_hi = at("mg_hi", [P, 8, S], f32r, 0)
        mg_lo = at("mg_lo", [P, 8, S], f32r, 32 * K)
        hid_hi = [at(f"hid_hi{g}", [P, 2, S], f32r, 32 * K * g) for g in range(2)]
        hid_lo = [at(f"hid_lo{g}", [P, 2, S], f32r, 32 * K * g + 8 * K) for g in range(2)]
        dw_hi = [at(f"dw_hi{g}", [P, 2, S], f32r, 32 * K * g + 16 * K) for g in range(2)]
        dw_lo = [at(f"dw_lo{g}", [P, 2, S], f32r, 32 * K * g + 24 * K) for g in range(2)]
        out_sb = at("out_sb", [P, 8, S], f32, 0)
        ya_hi = at("ya_hi", [P, 4, S], f32r, 64 * K)
        ya_lo = at("ya_lo", [P, 4, S], f32r, 80 * K)
        yb_hi = at("yb_hi", [P, 4, S], f32r, 96 * K)
        yb_lo = at("yb_lo", [P, 4, S], f32r, 112 * K)
        h2_hi = at("h2_hi", [P, 8, S], f32r, 64 * K)
        h2_lo = at("h2_lo", [P, 8, S], f32r, 96 * K)
        mixb = at("mixb", [P, 12, S], f32, 96 * K)
        x_sb = at("x_sb", [P, 8, S], f32, 128 * K)
        raw = [at(f"raw{s}", [P, 1024], f32, 160 * K + 4 * K * s) for s in range(2)]
        w_hi = [at(f"w_hi{s}", [P, 8, P], f32r, 168 * K + 8 * K * s) for s in range(2)]
        w_lo = [at(f"w_lo{s}", [P, 8, P], f32r, 172 * K + 8 * K * s) for s in range(2)]
        consts = at("consts", [P, N_CONST], f32, 184 * K)
        params = at("params", [P, N_PARAM], f32, 190 * K)
        rstd = at("rstd", [P, S], f32, 191 * K)
        tmp = [at(f"tmp{n}", [P, HALF], f32, 195 * K + 2 * K * n) for n in range(6)]
        off = [207 * K]

        def tiny(name, n, dt=f32):
            off[0] += 32
            return at(name, [P, n], dt, off[0] - 32)

        nmax = tiny("nmax", 4)
        psum_row = tiny("psum_row", 4)
        rsum = tiny("rsum", 4)
        rate_a = tiny("rate_a", 4)
        assert off[0] <= 212848
        sq = [at(f"sq{n}", [P, S], f32, 64 * K + 4 * K * n) for n in range(2)]
        sumsq = at("sumsq", [P, S], f32, 72 * K)
        sumsq2 = at("sumsq2", [P, S], f32, 203 * K)
        convin = at("convin", [P, S + 4], f32, 76 * K)
        conv = [at(f"conv{n}", [P, S], f32, 81 * K + 4 * K * n) for n in range(2)]
        lnb = at("lnb", [P, S], f32, 89 * K)
        inv_l2 = at("inv_l2", [P, S], f32, 64 * K)
        sqv = [at(f"sqv{n}", [P, S], f32, 68 * K + 4 * K * n) for n in range(2)]
        spots = [144 * K + 2 * K * n for n in range(8)] + [64 * K + 2 * K * n for n in range(16)]
        spot = iter(spots)

        def four(name):
            return at(name, [P, 4, P], f32, next(spot))

        (kn, vn, gb, gamb, dtmp, decT, pT_, aT, qg, gk, kdec, vtok, T, TT, Ns, nwk, w_, *state) = (
            four(n) for n in "kn vn gb gamb dtmp decT pT aT qg gk kdec vtok T TT Ns nwk w state0 state1".split())
        aoff = [four(f"aoff{b}") for b in LEVELS[1:]]
        gates8 = at("gates8", [P, 8, 8], f32, 93 * K)
        sp_a = at("sp_a", [P, 8, 4], f32, 93 * K + 256)
        sp_b = at("sp_b", [P, 8, 4], f32, 93 * K + 384)
        beta = at("beta", [P, 32], f32, 203 * K)
        g_log = at("g_log", [P, 32], f32, 203 * K + 128)
        neg_gc = at("neg_gc", [P, 32], f32, 203 * K + 256)
        gam = at("gam", [P, 32], f32, 203 * K + 384)
        kds = at("kds", [P, 32], f32, 203 * K + 512)
        gdiff = at("gdiff", [P, 32], f32, 203 * K + 640)
        g_end = at("g_end", [P, 2, 4], f32, 203 * K + 768)
        bd_rows = at("bd_rows", [8, S], f32, 195 * K)
        stage = [at(f"stage{n}", [P, S], f32, 195 * K + 4 * K * n) for n in range(2)]
        osq = [at(f"osq{n}", [P, S], f32, 64 * K + 4 * K * n) for n in range(2)]
        oln = [at(f"oln{n}", [P, S], f32, (72, 84)[n] * K) for n in range(2)]
        oinv = [at(f"oinv{n}", [P, S], f32, 76 * K + 4 * K * n) for n in range(2)]
        biast = [[at(f"biast{q}{n}", [P, WINDOW], f32, 96 * K + 2560 * (2 * q + n)) for n in range(2)] for q in range(2)]
        sc = [at(f"sc{n}", [P, WINDOW], f32, 106 * K + 2560 * n) for n in range(2)]
        pr = [at(f"pr{n}", [P, WINDOW], f32, 111 * K + 2560 * n) for n in range(2)]
        prT = [at(f"prT{n}", [P, WINDOW], f32, 116 * K + 2560 * n) for n in range(2)]
        ytok = [at(f"ytok{n}", [P, P], f32, 121 * K + 512 * n) for n in range(2)]
        qa = [at(f"qa{q}", [P, S], f32, o * K) for q, o in enumerate((144, 124))]
        ka = [at(f"ka{q}", [P, S], f32, o * K) for q, o in enumerate((148, 203))]
        va = at("va", [P, S], f32, 152 * K)
        va_tok = at("va_tok", [P, 8, P], f32, 156 * K)
        z_sb = [qa[0], ka[0], va, at("z3", [P, S], f32, 156 * K)]
        gate_sb = [[at(f"gate{q}{n}", [P, S], f32, (144 + 8 * q + 4 * n) * K) for n in range(2)] for q in range(2)]
        prod = [at(f"prod{n}", [P, S], f32, 199 * K - 4 * K * n) for n in range(2)]
        p_raw = at("p_raw", [P, 2, S], f32, 40 * K)

        ident = consts[:, C_IDENT:C_IDENT + P]
        ones = consts[:, C_ONES:C_ONES + P]
        cum = consts[:, C_CUM:C_CUM + P]
        chunk_ones = consts[:, C_CHUNK:C_CHUNK + P]
        decay_mask = consts[:, C_MASK:C_MASK + P]
        level = [consts[:, C_LEVEL + P * n:C_LEVEL + P * (n + 1)] for n in range(len(LEVELS))]
        eps_col = consts[:, C_EPS:C_EPS + 1]

        def heads(a):
            return a.unsqueeze(1).to_broadcast([P, 4, P])

        acc = [ctx.enter_context(nc.psum_tensor(f"acc{n}", [P, HALF], f32)) for n in range(2)]
        pair_a = ctx.enter_context(nc.psum_tensor("pair_a", [P, 1024], f32))
        pair_b = ctx.enter_context(nc.psum_tensor("pair_b", [P, 1024], f32))
        one = [ctx.enter_context(nc.psum_tensor(f"one{n}", [P, HALF], f32)) for n in range(2)]

        def bank(n):
            t = (pair_a, pair_a, pair_b, pair_b, one[0], one[1])[n]
            c = (0, HALF, 0, HALF, 0, 0)[n]
            return t[:, c:c + HALF]

        def bank4(n):
            return bank(n).rearrange("p (h i) -> p h i", h=4)

        def sems(names):
            return [sem(n) for n in names.split()]

        params_loaded, smalls_loaded, hi_made, lo_made, acc_ready = sems(
            "params_loaded smalls_loaded hi_made lo_made acc_ready")
        x_loaded = [sem(f"x_loaded{k}") for k in range(8)]
        raw_loaded = [sem(f"raw_loaded{s}") for s in range(2)]
        acc_read = [sem(f"acc_read{s}") for s in range(2)]
        norm_hi, norm_lo, sq_made, sq_added, stat_ready, rstd_ready = sems(
            "norm_hi norm_lo sq_made sq_added stat_ready rstd_ready")
        sq0_made, sq0_added = sems("sq0_made sq0_added")
        conv_done, silu_done, l2_sq, l2_sum, l2_ln, l2_inv, l2_done = sems(
            "conv_done silu_done l2_sq l2_sum l2_ln l2_inv l2_done")
        bd_rows_made, bd_ready, bd_scaled, bd_ln, rate_made, g_made, gc_ready, gc_read, gc_made = sems(
            "bd_rows_made bd_ready bd_scaled bd_ln rate_made g_made gc_ready gc_read gc_made")
        (tiles_in, gb_made, gcb_ready, kk_ready, tok_ready, gamb_made, dtmp_made, dec_made, aT_made, qg_made, vtok_made,
         keys_made, tt0_made, t0_ready, t0_made, aoff_made, n_ready, n_made, tn_ready, t_updated, tt_ready, tt_updated,
         wk_ready, nwk_made, wv_ready, w_made, o_ready, ds_ready, state_made, o_made) = sems(
            "tiles_in gb_made gcb_ready kk_ready tok_ready gamb_made dtmp_made dec_made aT_made qg_made vtok_made "
            "keys_made tt0_made t0_ready t0_made aoff_made n_ready n_made tn_ready t_updated tt_ready tt_updated "
            "wk_ready nwk_made wv_ready w_made o_ready ds_ready state_made o_made")
        bias_loaded = [sem(f"bias_loaded{q}") for q in range(2)]
        spilled = [sem(f"spilled{s}") for s in range(2)]
        gates_loaded = [sem(f"gates_loaded{s}") for s in range(2)]
        (qkv_loaded, z_loaded, vt_ready, vt_made, sc_ready, sc_read, max_made, pr_made, prT_ready, prT_made, oa_ready,
         ya_norm, yT_ready, yT_hi, yT_lo) = sems(
            "qkv_loaded z_loaded vt_ready vt_made sc_ready sc_read max_made pr_made prT_ready prT_made oa_ready ya_norm "
            "yT_ready yT_hi yT_lo")
        o_sq, o_sum, o_ln, o_inv, o_normed, z_silu, yb_made, yb_h, yb_l = sems(
            "o_sq o_sum o_ln o_inv o_normed z_silu yb_made yb_h yb_l")
        gate_sig, merged_made, mg_h, mg_l = sems("gate_sig merged_made mg_h mg_l")
        f_silu, f_scaled, f_hi, f_lo = sems("f_silu f_scaled f_hi f_lo")
        p_loaded, p_hi, p_lo, pg_sig, x4_made, out_made, out_stored = sems(
            "p_loaded p_hi p_lo pg_sig x4_made out_made out_stored")

        class Num:

            def __init__(self, reg, step, base):
                self.reg, self.step, self.base = reg, step, base

            def __add__(self, n):
                return Num(self.reg, self.step, self.base + n)

            @property
            def parity(self):
                return self.base % 2

            @property
            def value(self):
                return self.base if self.reg is None else self.reg * self.step + self.base

            @property
            def turn(self):
                return self.base // 2 if self.reg is None else self.reg * (self.step // 2) + self.base // 2

        def num(n):
            return Num(None, 0, n)

        def tile_job(t, c):
            return num(JOB_A + 1 + c + 2 * t) if isinstance(t, int) else Num(t, 2, JOB_A + 1 + c)

        def lin(reg, step, base):
            return base if reg is None else reg * step + base

        def flat(t):
            return t[:, :, :].rearrange("p a b -> p (a b)")

        def half_of(h):
            return slice(h * HALF, (h + 1) * HALF)

        def settle(eng):
            eng.wait_ge(smalls_loaded, 16)

        def split_hi(act, n, dst, free):
            act.wait_ge(raw_loaded[n.parity], (n.turn + 1) * 16)
            if free is not None:
                act.wait_ge(acc_ready, free)
            nc.scalar.activation(dst, raw[n.parity][:, :], ACT.Copy).then_inc(hi_made, 1)

        def split_lo(pool, n, dst, hi):
            pool.wait_ge(hi_made, (n + 1).value)
            nc.gpsimd.tensor_tensor(dst, raw[n.parity][:, :], hi.bitcast(f32), ALU.subtract).then_inc(lo_made, 1)

        def fetch_hi(act, n, free):
            split_hi(act, n, flat(w_hi[n.parity]), free)

        def fetch_lo(pool, n):
            split_lo(pool, n, flat(w_lo[n.parity]), flat(w_hi[n.parity]))

        def fetch_down_hi(act, n, g, free):
            for r in range(2):
                split_hi(act, n + r, dw_hi[g][:, r, :], free)

        def fetch_down_lo(pool, n, g):
            for r in range(2):
                split_lo(pool, n + r, dw_lo[g][:, r, :], dw_hi[g][:, r, :])

        def project(pe, job, w, src, ks, block_no=None, source_wait=None, between=None):
            for half in range(2):
                project_half(pe, job, w, src, ks, half, half, block_no if half == 0 else None,
                             source_wait if half == 0 else None)
                if half == 0 and between is not None:
                    between()

        def project_half(pe, job, w, src, ks, bank_no, half, block_no=None, source_wait=None):
            if block_no is not None:
                pe.wait_ge(lo_made, (block_no + 1).value)
            if not (isinstance(job, int) and job == 0):
                pe.wait_ge(acc_read[bank_no], job)
            for n, (kw, kx) in enumerate(ks):
                if source_wait is not None:
                    source_wait(n)
                for a, b in ((0, 0), (0, 1), (1, 0)):
                    last = nc.tensor.matmul(acc[bank_no][:, :], w[a](kw), src[b][:, kx, half_of(half)],
                                            start=(n == 0 and a == b), stop=(n == len(ks) - 1 and a == 1))
            last.then_inc(acc_ready, 1)

        def fill(pe, jobs, cut):
            for s in range(*cut):
                n, half, k = jobs[s // 16], s % 16 // 8, s % 8
                if s % 16 == 0:
                    pe.wait_ge(lo_made, (n + 1).value)
                if k == 0:
                    pe.wait_ge(acc_read[half], n.value)
                for a, b in ((w_hi, h_hi), (w_hi, h_lo), (w_lo, h_hi)):
                    last = nc.tensor.matmul(acc[half][:, :], a[n.parity][:, k, :], b[:, k, half_of(half)],
                                            start=(k == 0 and b is h_hi and a is w_hi), stop=(k == 7 and a is w_lo))
                if k == 7:
                    last.then_inc(acc_ready, 1)

        def spills(jobs):
            return jobs * 16 + 16

        def stage_out(dve, n, half):
            dve.wait_ge(spilled[n.parity], spills((n + -JOB_A).turn))
            job_done(dve, n.value, half)
            nc.vector.tensor_tensor(stage[n.parity][:, half_of(half)], acc[half][:, :], rstd[:, half_of(half)],
                                    ALU.mult).then_inc(acc_read[half], 1)

        def ring(n):
            return (lambda k: w_hi[n.parity][:, k, :]), (lambda k: w_lo[n.parity][:, k, :])

        def down_w(g, j):
            return (lambda r: dw_hi[g][:, r, j * P:(j + 1) * P]), (lambda r: dw_lo[g][:, r, j * P:(j + 1) * P])

        ALL = [(k, k) for k in range(8)]
        hx, h2x, mgx = (h_hi, h_lo), (h2_hi, h2_lo), (mg_hi, mg_lo)

        def job_done(eng, job, half):
            eng.wait_ge(acc_ready, job * 2 + (half + 1))

        def evacuated(eng, job, half):
            eng.wait_ge(acc_read[half], job + 1)

        def stat_sum(pe, ss):
            for half in range(2):
                last = nc.tensor.matmul(pair_a[:, half_of(half)], ones, ss[:, half_of(half)], start=True, stop=True)
            last.then_inc(stat_ready, 1)

        def stat_rstd(act, n, scratch):
            act.wait_ge(stat_ready, n)
            nc.scalar.activation(scratch[:, :], pair_a[:, :], ACT.Ln, bias=eps_col, scale=1.0 / D)
            act.drain()
            nc.scalar.activation(rstd[:, :], scratch[:, :], ACT.Exp, scale=-0.5).then_inc(rstd_ready, 1)

        def residual_hi(act, job, j, half, gcol, count):
            act.wait_ge(acc_read[half], job + 1)
            nc.scalar.activation(h2_hi[:, j, half_of(half)], x_sb[:, j, half_of(half)], ACT.Copy,
                                 scale=params[:, gcol + j:gcol + j + 1]).then_inc(norm_hi, 1)
            squares(act, j, half, count)

        def squares(act, j, half, count):
            c = count + 2 * j + half
            if c >= 4:
                act.wait_ge(sq_added, c - 3)
            nc.scalar.activation(tmp[c % 4][:, :], x_sb[:, j, half_of(half)], ACT.Square).then_inc(sq_made, 1)

        def residual_lo(dve, j, half, gcol, count):
            dve.wait_ge(norm_hi, count + 2 * j + half + 1)
            nc.vector.scalar_tensor_tensor(h2_lo[:, j, half_of(half)], x_sb[:, j, half_of(half)],
                                           params[:, gcol + j:gcol + j + 1],
                                           h2_hi[:, j, half_of(half)].bitcast(f32), ALU.mult, ALU.subtract
                                           ).then_inc(norm_lo, 1)

        def add_squares(pool, j, half, count):
            c = count + 2 * j + half
            pool.wait_ge(sq_made, c + 1)
            if j == 0:
                nc.gpsimd.tensor_copy(sumsq2[:, half_of(half)], tmp[c % 4][:, :]).then_inc(sq_added, 1)
            else:
                pool.wait_ge(sq_added, c - 1)
                nc.gpsimd.tensor_tensor(sumsq2[:, half_of(half)], sumsq2[:, half_of(half)], tmp[c % 4][:, :],
                                        ALU.add).then_inc(sq_added, 1)

        fill_b, fill_a = cuts(FILL_B), cuts(FILL_A)
        FETCH_STEP = [max(0, [e > 16 * c for s, e in fill_a].index(True)) for c in range(3)]
        HALF_STEP = [[e >= 8 * (h + 1) for s, e in fill_a].index(True) for h in range(6)]
        HALF_PLACE = [[e >= 8 * (h + 1) for s, e in fill_b].index(True) for h in range(4)]

        block = ctx.enter_context(nc.Block())

        @block.sync
        def _(sp):
            sp.dma_start(params[:, :], params_d).then_inc(params_loaded, 16)
            for k in range(8):
                sp.dma_start(x_sb[:, k, :], x_t[k]).then_inc(x_loaded[k], 16)
                if k == 0:
                    sp.dma_start(raw[0][:, :], blocks[0]).then_inc(raw_loaded[0], 16)
            sp.dma_start(raw[1][:, :], blocks[1]).then_inc(raw_loaded[1], 16)
            sp.dma_start(consts[:, :], consts_d).then_inc(smalls_loaded, 16)

            def load(i, s):
                sp.wait_ge(lo_made, i * 2 + (s - 1))
                src = blocks[ds(i * 2 + s, 1)].rearrange("a p n -> (a p) n")
                sp.dma_start(raw[s][:, :], src).then_inc(raw_loaded[s], 16)

            def store(n):
                for half in range(2):
                    sp.wait_ge(acc_read[half], (n + 1).value)
                dst = spill[ds((n + -JOB_A).value, 1)].rearrange("a p n -> (a p) n")
                sp.dma_start(dst, stage[n.parity][:, :]).then_inc(spilled[n.parity], 16)

            with sp.Fori(1, (JOB_A + 3) // 2) as i:
                load(i, 0)
                load(i, 1)
            with sp.Fori((JOB_A + 3) // 2, (JOB_M + 3) // 2) as i:
                for s in range(2):
                    load(i, s)
                    store(Num(i, 2, s - 3))
            with sp.Fori((JOB_M + 3) // 2, N_BLK // 2) as i:
                load(i, 0)
                load(i, 1)
            if N_BLK % 2:
                sp.wait_ge(lo_made, N_BLK - 2)
                sp.dma_start(raw[(N_BLK - 1) % 2][:, :], blocks[N_BLK - 1]).then_inc(raw_loaded[(N_BLK - 1) % 2], 16)
            for m in range(16):
                cols = half_of(m // 8)
                sp.wait_ge(out_made, m + 1)
                sp.dma_start(out_t[m % 8, :, cols], out_sb[:, m % 8, cols]).then_inc(out_stored, 16)
            sp.wait_ge(out_stored, 16 * 16)

        @block.gpsimd
        def _(pool):
            g = nc.gpsimd
            fetch_lo(pool, num(0))
            fetch_lo(pool, num(1))
            with pool.Fori(1, 7) as i:
                fetch_lo(pool, Num(i, 2, 0))
                fetch_lo(pool, Num(i, 2, 1))
            fetch_lo(pool, num(BLK_A + 1))
            with pool.Fori(0, TOK_TILES) as t:
                n = Num(t, 2, BLK_A + 1)
                pool.wait_ge(aT_made, t + 1)
                for m in range(5):
                    g.tensor_tensor(aoff[m][:, :, :], aT[:, :, :], heads(level[m + 1]), ALU.mult
                                    ).then_inc(aoff_made, 1)
                fetch_lo(pool, n + 1)
                fetch_lo(pool, n + 2)

            def load(dst, row, ready):
                settle(pool)
                src = spill[row] if isinstance(row, int) else spill[ds(row, 1)].rearrange("a p n -> (a p) n")
                pool.dma_start(dst[:, :], src).then_inc(ready, 16)

            for s in range(2):
                pool.wait_ge(spilled[s], spills(8))
            pool.wait_ge(o_made, 8)
            pool.wait_ge(state_made, 16)

            def load_bias(p):
                if p >= 2:
                    pool.wait_ge(sc_read, 16 * (p - 1))
                for hh in range(2):
                    pool.dma_start(biast[p % 2][hh][:, :], bias_d[2 * p + hh]).then_inc(bias_loaded[p % 2], 16)

            for c, dst in ((2, va), (0, qa[0]), (1, ka[0])):
                load(dst, c, qkv_loaded)
            load_bias(0)
            fetch_lo(pool, num(BLK_G + 2))
            fetch_lo(pool, num(BLK_G + 3))
            for p in range(PAIRS):
                pool.wait_ge(vt_ready, p + 1)
                for c, dst in enumerate((qa[1 - p % 2], ka[1 - p % 2], va)):
                    load(dst, p * 3 + 3 + c, qkv_loaded)
                fetch_lo(pool, num(BLK_G + 4 + 3 * p))
                if p < PAIRS - 1:
                    load_bias(p + 1)
                for c in (1, 2):
                    fetch_lo(pool, num(BLK_G + 4 + 3 * p + c))
            pool.wait_ge(oa_ready, 64)
            load(z_sb[3], 15, z_loaded)
            fetch_lo(pool, num(BLK_M))
            for q in range(2):
                pool.wait_ge(yb_made, 2 * q + 2)
                for c in range(2):
                    load(gate_sb[q][c], 16 + 2 * q + c, gates_loaded[q])
            for s in range(2):
                pool.wait_ge(spilled[s], spills(16))

            def merge(i, ahead):
                for q in range(2):
                    fetch_lo(pool, Num(i, 2, BLK_M + q + 1))
                    if ahead:
                        pool.wait_ge(acc_read[1], i * 4 + (JOB_M + 2 * q + 2))
                        for c in range(2):
                            load(gate_sb[q][c], i * 4 + (20 + 2 * q + c), gates_loaded[q])

            with pool.Fori(0, 3) as i:
                merge(i, True)
            for q in range(2):
                fetch_lo(pool, num(BLK_M + 6 + q + 1))
            for j in range(8):
                fetch_lo(pool, num(BLK_O + j + 1))
                for half in range(2):
                    add_squares(pool, j, half, 0)

            def group(i, reg, gpar, step):
                n = Num(reg, 6 * step, BLK_F + 6 * i)
                for c in range(4):
                    if c < 3:
                        fetch_lo(pool, n + (c + 1))
                    else:
                        fetch_down_lo(pool, n + 4, gpar)
                        fetch_lo(pool, n + 6)
                    if c % 2 == 0:
                        for half in range(2):
                            pool.wait_ge(f_silu, lin(reg, 4 * step, 4 * i + c + half + 1))
                            g.tensor_tensor(tmp[half][:, :], tmp[half][:, :], rstd[:, half_of(half)],
                                            ALU.mult).then_inc(f_scaled, 1)

            group(0, None, 0, 0)
            with pool.Fori(0, 4) as i:
                group(1, i, 1, 2)
                group(2, i, 0, 2)
            group(9, None, 1, 0)
            group(10, None, 0, 0)
            for j in range(8):
                for half in range(2):
                    add_squares(pool, j, half, 16)
            fetch_down_lo(pool, num(BLK_P + 1), 1)
            fetch_lo(pool, num(ple_block(1)))
            for m in range(15):
                if m:
                    fetch_lo(pool, num(ple_block(m + 1)))
                pool.wait_ge(sq_made, 33 + m)
                half = half_of(m // 8)
                if m % 8 == 0:
                    g.tensor_copy(sumsq2[:, half], tmp[m % 2][:, :]).then_inc(sq_added, 1)
                else:
                    pool.wait_ge(sq_added, 32 + m)
                    g.tensor_tensor(sumsq2[:, half], sumsq2[:, half], tmp[m % 2][:, :], ALU.add).then_inc(sq_added, 1)

        @block.scalar
        def _(act):
            A = nc.scalar.activation
            act.wait_ge(params_loaded, 16)
            A(rate_a[:, :], params[:, P_ALOG:P_ALOG + 4], ACT.Exp).then_inc(rate_made, 1)
            for k in range(8):
                act.wait_ge(x_loaded[k], 16)
                A(h_hi[:, k, :], x_sb[:, k, :], ACT.Copy, scale=params[:, P_GMIX + k:P_GMIX + k + 1]
                  ).then_inc(norm_hi, 1)
                if k == 0:
                    fetch_hi(act, num(0), None)
            fetch_hi(act, num(1), None)
            for k in range(8):
                if k >= 2:
                    act.wait_ge(sq0_added, k - 1)
                A(sq[k % 2][:, :], x_sb[:, k, :], ACT.Square).then_inc(sq0_made, 1)
            act.wait_ge(smalls_loaded, 16)
            stat_rstd(act, 1, lnb)

            def l2_inverse(n):
                idx = n.value
                act.wait_ge(l2_sum, idx + 1)
                A(lnb[:, :], (pair_a, pair_b)[n.parity][:, :], ACT.Ln, bias=eps_col).then_inc(l2_ln, 1)
                act.drain()
                if not (isinstance(idx, int) and idx == 0):
                    act.wait_ge(l2_done, idx)
                A(inv_l2[:, :], lnb[:, :], ACT.Exp, scale=-0.5).then_inc(l2_inv, 1)

            def conv_step(n, sq_job, inverse_prev):
                j = n.value
                fetch_hi(act, n + 2, j * 2 + 2)
                if inverse_prev:
                    l2_inverse(n + -7)
                act.wait_ge(conv_done, j)
                settle(act)
                A(mixb[:, (n + -1).value, :], conv[n.parity][:, :], ACT.Silu).then_inc(silu_done, 1)
                if sq_job:
                    act.drain()
                    A(sqv[(n + -5).parity][:, :], mixb[:, (n + -1).value, :], ACT.Square).then_inc(l2_sq, 1)

            fetch_hi(act, num(2), 2)
            for j in range(1, 6):
                conv_step(num(j), j > 4, False)
                if j == 3:
                    act.wait_ge(bd_scaled, 1)
                    A(sp_a[:, :, :], gates8[:, :, 0:4], ACT.Exp, scale=-1.0)
                    A(sp_b[:, :, :], gates8[:, :, 4:8], ACT.Exp, scale=-1.0)
                    act.drain()
                    A(sp_b[:, :, :], sp_b[:, :, :], ACT.Ln, bias=1.0).then_inc(bd_ln, 1)
            fetch_hi(act, num(8), 7 * 2)
            act.wait_ge(conv_done, 6)
            A(mixb[:, 5, :], conv[0][:, :], ACT.Silu).then_inc(silu_done, 1)
            act.drain()
            act.wait_ge(gc_ready, 1)
            A(gam[:, :], one[1][:, 0:32], ACT.Exp)
            A(neg_gc[:, :], one[1][:, 0:32], ACT.Copy, scale=-1.0).then_inc(gc_read, 1)
            act.wait_ge(gc_made, 1)
            A(kds[:, :], gdiff[:, :], ACT.Exp).then_inc(gc_read, 1)
            A(sqv[1][:, :], mixb[:, 5, :], ACT.Square).then_inc(l2_sq, 1)
            with act.Fori(3, 5) as i:
                conv_step(Num(i, 2, 1), True, True)
                conv_step(Num(i, 2, 2), True, True)
            conv_step(num(11), True, True)
            conv_step(num(12), True, True)

            def tile_in(t):
                tok = ds(t * P, P)
                settle(act)
                A(kn[:, :, :], mixb[:, 4:8, tok], ACT.Copy).then_inc(tiles_in, 1)
                A(vn[:, :, :], mixb[:, 0:4, tok], ACT.Copy).then_inc(tiles_in, 1)

            def tile_gamma(t):
                act.wait_ge(gcb_ready, t + 1)
                A(gamb[:, :, :], bank4(3), ACT.Exp).then_inc(gamb_made, 1)

            def tile_decay(t):
                act.wait_ge(dtmp_made, t + 1)
                settle(act)
                for h in range(4):
                    last = A(decT[:, h, :], dtmp[:, h, :], ACT.Exp, bias=neg_gc[:, ds(t * 4 + h, 1)])
                last.then_inc(dec_made, 1)

            act.wait_ge(l2_done, 4)
            tile_gamma(0)
            tile_in(0)
            tile_decay(0)
            act.drain()
            for n, dst in ((6, lnb), (7, conv[1])):
                act.wait_ge(l2_sum, n + 1)
                A(dst[:, :], (pair_a, pair_b)[n % 2][:, :], ACT.Ln, bias=eps_col).then_inc(l2_ln, 1)
            act.drain()
            act.wait_ge(l2_done, 6)
            A(inv_l2[:, :], lnb[:, :], ACT.Exp, scale=-0.5).then_inc(l2_inv, 1)
            A(conv[1][:, :], conv[1][:, :], ACT.Exp, scale=-0.5).then_inc(l2_inv, 1)

            def tile(t, last_tile):
                tok = ds(t * P, P)
                act.wait_ge(tok_ready, t + 1)
                A(vtok[:, :, :], bank4(4), ACT.Copy).then_inc(vtok_made, 1)
                fetch_hi(act, tile_job(t, 1), tile_job(t, 0).value * 2)
                act.wait_ge(t0_ready, t + 1)
                A(T[:, :, :], bank4(5), ACT.Copy).then_inc(t0_made, 1)
                for m in range(5):
                    act.wait_ge(n_ready, t * 5 + (m + 1))
                    A(Ns[:, :, :], bank4(0), ACT.Copy).then_inc(n_made, 1)
                act.wait_ge(wk_ready, t + 1)
                A(nwk[:, :, :], bank4(3), ACT.Copy, scale=-1.0).then_inc(nwk_made, 1)
                fetch_hi(act, tile_job(t, 2), tile_job(t, 1).value * 2)
                if not last_tile:
                    tile_in(t + 1)
                    act.wait_ge(qg_made, t + 1)
                    tile_gamma(t + 1)
                    tile_decay(t + 1)
                act.wait_ge(o_ready, t + 1)
                settle(act)
                A(mixb[:, 8:12, tok], bank4(5), ACT.Copy).then_inc(o_made, 1)

            with act.Fori(0, TOK_TILES - 1) as t:
                tile(t, False)
            tile(TOK_TILES - 1, True)

            act.wait_ge(state_made, 16)
            act.drain()
            fetch_hi(act, num(BLK_G + 2), 2 * (JOB_G + 1))
            for c in (0, 2):
                if c:
                    fetch_hi(act, num(BLK_G + 3), 2 * (JOB_G + 2))
                for d in (0, 1):
                    if c:
                        act.wait_ge(o_sum, d + 1)
                    A(osq[d][:, :], mixb[:, 8 + c + d, :], ACT.Square).then_inc(o_sq, 1)
                for d in (0, 1):
                    act.wait_ge(o_sum, c + d + 1)
                    A(oln[d][:, :], (pair_a, pair_b)[d][:, :], ACT.Ln, bias=eps_col, scale=1.0 / B_DIM).then_inc(o_ln, 1)
                act.drain()
                for d in (0, 1):
                    if c:
                        act.wait_ge(o_normed, d + 1)
                    A(oinv[d][:, :], oln[d][:, :], ACT.Exp, scale=-0.5).then_inc(o_inv, 1)
                act.drain()

            with act.Fori(0, 2) as i:
                for q in range(2):
                    p = i * 2 + q
                    act.wait_ge(vt_ready, p + 1)
                    A(flat(va_tok), pair_b[:, :], ACT.Copy).then_inc(vt_made, 1)
                    for u in range(19):
                        b, base = u % 2, p * 16
                        for c in range(3):
                            if FETCH_STEP[c] == u:
                                n = Num(i, 6, BLK_G + 3 + 3 * q + c)
                                fetch_hi(act, n + 1, n.value * 2)
                        if u < 16:
                            width = P * min(u // 2 + 1, 5)
                            act.wait_ge(max_made, base + (u + 1))
                            if u >= 2:
                                act.wait_ge(prT_ready, base + (u - 1))
                            A(pr[b][:, :width], sc[b][:, :width], ACT.Exp, bias=nmax[:, b:b + 1],
                              accum_out=psum_row[:, u % 4:u % 4 + 1]).then_inc(pr_made, 1)
                        if 1 <= u < 17:
                            width = P * min((u - 1) // 2 + 1, 5)
                            act.wait_ge(prT_ready, base + u)
                            if u >= 3:
                                act.wait_ge(oa_ready, base + (u - 2))
                            A(prT[1 - b][:, :width], pair_b[:, :width], ACT.Copy).then_inc(prT_made, 1)
                        if u >= 4 and u % 2 == 0:
                            tt = (u - 4) // 2
                            act.wait_ge(yT_ready, p * 8 + (tt + 1))
                            settle(act)
                            A(ya_hi[:, p, tt * P:(tt + 1) * P], one[1][:, P:2 * P], ACT.Copy).then_inc(yT_hi, 1)

            fetch_hi(act, num(BLK_M), 2 * (JOB_G + 15))
            act.wait_ge(qkv_loaded, 5 * 48)
            for c in range(3):
                A(z_sb[c][:, :], z_sb[c][:, :], ACT.Silu).then_inc(z_silu, 1)
            act.wait_ge(z_loaded, 16)
            A(z_sb[3][:, :], z_sb[3][:, :], ACT.Silu).then_inc(z_silu, 1)
            act.wait_ge(oa_ready, 64)
            for c in range(4):
                act.wait_ge(yb_made, c + 1)
                A(yb_hi[:, c, :], mixb[:, 8 + c, :], ACT.Copy).then_inc(yb_h, 1)

            def sigmoids(q, count):
                act.wait_ge(gates_loaded[q], count)
                for c in range(2):
                    A(gate_sb[q][c][:, :], gate_sb[q][c][:, :], ACT.Sigmoid).then_inc(gate_sig, 1)

            def merge(i, q, ahead=True):
                j = i * 2 + q
                n = num(BLK_M + j) if isinstance(i, int) else Num(i, 2, BLK_M + q)
                fetch_hi(act, n + 1, i * 8 + (2 * JOB_M + 4 * q))
                if ahead:
                    sigmoids(1 - q, i * 32 + (32 + 32 * q))
                for half in range(2):
                    act.wait_ge(merged_made, j * 2 + (half + 1))
                    settle(act)
                    A(mg_hi[:, j, half_of(half)], prod[0][:, half_of(half)], ACT.Copy).then_inc(mg_h, 1)

            sigmoids(0, 32)
            act.wait_ge(yb_l, 4)
            for k in range(4):
                act.dma_start(x_sb[:, k, :], x_t[k]).then_inc(x_loaded[k], 16)
            with act.Fori(0, 3) as i:
                merge(i, 0)
                merge(i, 1)
            merge(3, 0)
            merge(3, 1, False)
            act.wait_ge(acc_read[1], JOB_O)
            for k in range(4, 8):
                act.dma_start(x_sb[:, k, :], x_t[k]).then_inc(x_loaded[k], 16)

            for j in range(8):
                n = BLK_O + j
                fetch_hi(act, num(n + 1), 2 * (JOB_O + j))
                for half in range(2):
                    residual_hi(act, JOB_O + j, j, half, P_GFFN, 0)
            fetch_hi(act, num(BLK_F + 1), 2 * JOB_F)
            stat_rstd(act, 2, sumsq2)

            def group(i, reg, gpar, step):
                n = Num(reg, 6 * step, BLK_F + 6 * i)
                if reg is None:
                    jobs = ffn_jobs(i)[0]
                    before = ffn_jobs(i - 1)[0] if i else [0, 0, 0, JOB_O + 7]
                    down_free = 2 * (ffn_jobs(i - 1)[0][3] + 3) if i > 1 else 2 * JOB_F
                else:
                    jobs = [reg * (12 * step) + v for v in ffn_jobs(i)[0]]
                    before = [None, None, None, reg * (12 * step) + (ffn_jobs(i)[0][0] - 3)]
                    down_free = reg * (24 * step) + 2 * ffn_jobs(i)[0][0]
                for c in range(4):
                    free = before[3] if c == 0 else jobs[c - 1]
                    if c < 3:
                        if i or c:
                            fetch_hi(act, n + (c + 1), (free + 1) * 2)
                    else:
                        fetch_down_hi(act, n + 4, gpar, down_free)
                        fetch_hi(act, n + 6, (free + 1) * 2)
                    for half in range(2):
                        if c % 2 == 0:
                            evacuated(act, jobs[c], half)
                            A(tmp[half][:, :], tmp[half][:, :], ACT.Silu).then_inc(f_silu, 1)
                        else:
                            evacuated(act, jobs[c], half)
                            A(hid_hi[gpar][:, c // 2, half_of(half)], tmp[2 + half][:, :], ACT.Copy
                              ).then_inc(f_hi, 1)

            group(0, None, 0, 0)
            with act.Fori(0, 4) as i:
                group(1, i, 1, 2)
                group(2, i, 0, 2)
            group(9, None, 1, 0)
            group(10, None, 0, 0)
            act.wait_ge(acc_ready, 2 * JOB_T)
            act.dma_start(p_raw[:, :, :], p_t.rearrange("k p n -> p k n")).then_inc(p_loaded, 16)
            for j in range(8):
                for half in range(2):
                    residual_hi(act, JOB_T + j, j, half, P_GPLE, 16)
            fetch_down_hi(act, num(BLK_P + 1), 1, 2 * JOB_T)
            act.wait_ge(p_loaded, 16)
            for k in range(2):
                A(hid_hi[1][:, k, :], p_raw[:, k, :], ACT.Copy).then_inc(p_hi, 1)
            stat_rstd(act, 3, sumsq2)
            fetch_hi(act, num(ple_block(1)), 2 * JOB_T)

            def final_rstd(half):
                act.wait_ge(stat_ready, 4 + half)
                A(sumsq2[:, half_of(half)], pair_a[:, half_of(half)], ACT.Ln, bias=eps_col, scale=1.0 / D)
                act.drain()
                A(rstd[:, half_of(half)], sumsq2[:, half_of(half)], ACT.Exp, scale=-0.5).then_inc(rstd_ready, 1)

            for m in range(16):
                if 0 < m < 15:
                    fetch_hi(act, num(ple_block(m + 1)), 2 * (JOB_P + m))
                if m == 10:
                    final_rstd(0)
                act.wait_ge(acc_read[0], JOB_P + m + 1)
                A(tmp[2 + m % 2][:, :], tmp[2 + m % 2][:, :], ACT.Sigmoid).then_inc(pg_sig, 1)
                act.wait_ge(x4_made, m + 1)
                act.wait_ge(sq_added, 31 + m)
                A(tmp[m % 2][:, :], x_sb[:, m % 8, half_of(m // 8)], ACT.Square).then_inc(sq_made, 1)
            final_rstd(1)

        @block.vector
        def _(dve):
            V = nc.vector
            TTs, STT, TS = V.tensor_tensor, V.scalar_tensor_tensor, V.tensor_scalar
            dve.wait_ge(params_loaded, 16)
            V.memset(convin[:, 0:4], 0.0)
            for k in range(8):
                dve.wait_ge(norm_hi, k + 1)
                STT(h_lo[:, k, :], x_sb[:, k, :], params[:, P_GMIX + k:P_GMIX + k + 1],
                    h_hi[:, k, :].bitcast(f32), ALU.mult, ALU.subtract).then_inc(norm_lo, 1)
            dve.wait_ge(smalls_loaded, 16)
            for k in range(8):
                if k:
                    dve.wait_ge(sq0_added, k)
                dve.wait_ge(sq0_made, k + 1)
                if k == 0:
                    V.tensor_copy(sumsq[:, :], sq[0][:, :]).then_inc(sq0_added, 1)
                else:
                    TTs(sumsq[:, :], sumsq[:, :], sq[k % 2][:, :], ALU.add).then_inc(sq0_added, 1)
                if k in (2, 7):
                    job_done(dve, 0, k // 7)
                    V.tensor_copy(bd_rows[:, half_of(k // 7)], acc[k // 7][0:8, :]).then_inc(acc_read[k // 7], 1)

            def l2_scale(idx, job, inverse=inv_l2):
                dve.wait_ge(l2_inv, idx + 1)
                STT(mixb[:, job, :], mixb[:, job, :], consts[:, ds(C_QKS + job, 1)] if not isinstance(job, int)
                    else consts[:, C_QKS + job:C_QKS + job + 1], inverse[:, :], ALU.mult, ALU.mult).then_inc(l2_done, 1)

            def conv_step(n, scale_prev):
                j = n.value
                dve.drain()
                for half in range(2):
                    job_done(dve, j, half)
                    TTs(convin[:, 3 + half * HALF:3 + (half + 1) * HALF], acc[half][:, :], rstd[:, half_of(half)],
                        ALU.mult).then_inc(acc_read[half], 1)
                for w in range(CONV):
                    col = P_CONV + w - CONV + (j * CONV)
                    tap = params[:, col:col + 1] if isinstance(col, int) else params[:, ds(col, 1)]
                    dve.drain()
                    if w == 0:
                        if not (isinstance(j, int) and j < 3):
                            dve.wait_ge(silu_done, (n + -2).value)
                        last = TS(conv[n.parity][:, :], convin[:, 0:S], tap, None, ALU.mult)
                    else:
                        last = STT(conv[n.parity][:, :], convin[:, w:w + S], tap, conv[n.parity][:, :], ALU.mult, ALU.add)
                last.then_inc(conv_done, 1)
                if scale_prev:
                    l2_scale((n + -7).value, (n + -3).value)

            dve.drain()
            dve.wait_ge(rstd_ready, 1)
            TTs(bd_rows[:, :], bd_rows[:, :], rstd[0:8, :], ALU.mult).then_inc(bd_rows_made, 1)

            def column(a, t):
                return a[:, ds(t * 4, 4)].unsqueeze(2).to_broadcast([P, 4, P])

            def tile_log(t):
                TTs(gb[:, :, :], heads(ones), column(g_log, t), ALU.mult).then_inc(gb_made, 1)

            def tile_masked(t):
                dve.wait_ge(gcb_ready, t + 1)
                dve.wait_ge(gamb_made, t + 1)
                TTs(dtmp[:, :, :], bank4(3), heads(decay_mask), ALU.add).then_inc(dtmp_made, 1)

            for j in range(1, 7):
                conv_step(num(j), False)
                if j == 2:
                    dve.drain()
                    dve.wait_ge(bd_ready, 1)
                    V.tensor_copy(gates8[:, :, :], one[0][:, 0:64].rearrange("p (t c) -> p t c", t=8))
                    dve.drain()
                    TTs(gates8[:, :, 4:8], gates8[:, :, 4:8],
                        params[:, P_DTB:P_DTB + 4].unsqueeze(1).to_broadcast([P, 8, 4]), ALU.add)
                    dve.drain()
                    g4 = g_log[:, :].rearrange("p (t c) -> p t c", t=8)
                    b4 = beta[:, :].rearrange("p (t c) -> p t c", t=8)
                    TS(g4, gates8[:, :, 4:8], 0.0, None, ALU.max)
                    TS(b4, gates8[:, :, 4:8], -1.0, None, ALU.mult)
                    dve.drain()
                    TTs(gates8[:, :, 4:8], gates8[:, :, 4:8], b4, ALU.max).then_inc(bd_scaled, 1)
                if j == 4:
                    dve.wait_ge(bd_ln, 1)
                    TS(b4, sp_a[:, :, :], 1.0, None, ALU.add)
                    TTs(g4, g4, sp_b[:, :, :], ALU.add)
                    dve.drain()
                    V.reciprocal(beta[:, :], beta[:, :])
                    dve.wait_ge(rate_made, 1)
                    rate = rate_a[:, :].unsqueeze(1).to_broadcast([P, 8, 4])
                    STT(g4, g4, -1.0, rate, ALU.mult, ALU.mult).then_inc(g_made, 1)
            tile_log(0)
            for s in range(2):
                V.memset(stage[s][:, 0:1], 0.0).then_inc(spilled[s], 16)
            dve.wait_ge(gc_ready, 1)
            dve.wait_ge(gc_read, 1)
            V.tensor_copy(gdiff[:, :], one[1][:, 32:64])
            dve.drain()
            TTs(gdiff[:, :], gdiff[:, :], one[1][:, 0:32], ALU.subtract).then_inc(gc_made, 1)
            with dve.Fori(3, 6) as i:
                conv_step(Num(i, 2, 1), True)
                conv_step(Num(i, 2, 2), True)
            tile_masked(0)
            V.memset(state[0][:, :, :], 0.0).then_inc(state_made, 1)
            stage_out(dve, num(JOB_A), 0)
            l2_scale(6, 10)
            l2_scale(7, 11, conv[1])
            stage_out(dve, num(JOB_A), 1)
            dve.wait_ge(gc_read, 2)

            def tile(t, last_tile):
                jobs = [tile_job(t, c) for c in range(2)]
                tok = ds(t * P, P)

                def stage_ended(*places):
                    for h in range(4):
                        if HALF_PLACE[h] in places:
                            stage_out(dve, jobs[h // 2], h % 2)

                dve.drain()
                TTs(qg[:, :, :], mixb[:, 8:12, tok], gamb[:, :, :], ALU.mult)
                V.tensor_copy(g_end[:, :, :], gamb[:, :, CHUNK - 1::CHUNK].rearrange("p h c -> p c h")
                              ).then_inc(qg_made, 1)
                dve.wait_ge(dec_made, t + 1)
                dve.wait_ge(kk_ready, t + 1)
                for h in range(4):
                    last = STT(aT[:, h, :], decT[:, h, :], beta[:, ds(t * 4 + h, 1)], bank4(1)[:, h, :],
                               ALU.mult, ALU.mult)
                last.then_inc(aT_made, 1)
                dve.drain()
                TTs(TT[:, :, :], aT[:, :, :], heads(level[0]), ALU.mult)
                dve.drain()
                TTs(TT[:, :, :], heads(ident), TT[:, :, :], ALU.subtract).then_inc(tt0_made, 1)
                TTs(pT_[:, :, :], bank4(2), decT[:, :, :], ALU.mult)
                dve.wait_ge(tok_ready, t + 1)
                TTs(gk[:, :, :], bank4(3), column(gam, t), ALU.mult)
                TTs(kdec[:, :, :], bank4(3), column(kds, t), ALU.mult).then_inc(keys_made, 1)
                stage_ended(0, 1, 2)
                dve.wait_ge(t0_made, t + 1)
                for n in range(5):
                    dve.wait_ge(tn_ready, t * 5 + (n + 1))
                    TTs(T[:, :, :], T[:, :, :], bank4(1), ALU.subtract).then_inc(t_updated, 1)
                    dve.wait_ge(tt_ready, t * 5 + (n + 1))
                    V.tensor_copy(TT[:, :, :], bank4(2)).then_inc(tt_updated, 1)
                    stage_ended(3 + 2 * n, 4 + 2 * n)
                    if n == 3 and not last_tile:
                        tile_log(t + 1)
                stage_ended(13, 14)
                for c in range(2):
                    r = slice(c * CHUNK, (c + 1) * CHUNK)
                    dve.wait_ge(wv_ready, t * 2 + (c + 1))
                    TTs(w_[r, :, :], bank4(4)[r, :, :],
                        beta[r, ds(t * 4, 4)].unsqueeze(2).to_broadcast([CHUNK, 4, P]), ALU.mult).then_inc(w_made, 1)
                    if c == 1 and last_tile:
                        stage_ended(17)
                        continue
                    dve.wait_ge(ds_ready, t * 2 + (c + 1))
                    for h in range(4):
                        last = STT(state[1 - c][:, h, :], state[c][:, h, :], g_end[:, c, h:h + 1], bank4(0)[:, h, :],
                                   ALU.mult, ALU.add)
                    last.then_inc(state_made, 1)
                    if c == 0 and not last_tile:
                        tile_masked(t + 1)
                    stage_ended(*((15, 16), (17,))[c])

            with dve.Fori(0, TOK_TILES - 1) as t:
                tile(t, False)
            tile(TOK_TILES - 1, True)

            for c in range(4):
                if c in (0, 2):
                    stage_out(dve, num(JOB_G + 1), c // 2)
                dve.wait_ge(o_inv, c + 1)
                STT(mixb[:, 8 + c, :], mixb[:, 8 + c, :], params[:, P_ONORM:P_ONORM + 1], oinv[c % 2][:, :],
                    ALU.mult, ALU.mult).then_inc(o_normed, 1)
            for half in range(2):
                stage_out(dve, num(JOB_G + 2), half)

            with dve.Fori(0, 2) as i:
                for q in range(2):
                    p = i * 2 + q
                    dve.wait_ge(bias_loaded[q], i * 32 + 32)
                    for u in range(19):
                        b, base = u % 2, p * 16
                        if u < 16:
                            width = P * min(u // 2 + 1, 5)
                            dve.wait_ge(sc_ready, base + (u + 1))
                            if u >= 2:
                                dve.wait_ge(pr_made, base + (u - 1))
                            STT(sc[b][:, :width], pair_a[:, :width], A_DIM ** -0.5,
                                biast[q][u % 2][:, WINDOW - width:], ALU.mult, ALU.add).then_inc(sc_read, 1)
                            dve.drain()
                            V.tensor_reduce(nmax[:, b:b + 1], sc[b][:, :width], AX.X, ALU.max, negate=True
                                            ).then_inc(max_made, 1)
                        if 2 <= u < 18:
                            v, vb = u - 2, u % 2
                            tt = v // 2
                            dve.wait_ge(oa_ready, base + (v + 1))
                            V.reciprocal(rsum[:, vb:vb + 1], psum_row[:, v % 4:v % 4 + 1])
                            dve.drain()
                            if tt >= 2:
                                dve.wait_ge(yT_ready, p * 8 + (tt - 1))
                            TS(ytok[tt % 2][:, (v % 2) * 64:(v % 2) * 64 + 64], one[vb][:, 0:64], rsum[:, vb:vb + 1],
                               None, ALU.mult).then_inc(ya_norm, 1)
                        if u >= 4 and u % 2 == 0:
                            tt = (u - 4) // 2
                            dve.wait_ge(yT_hi, p * 8 + (tt + 1))
                            TTs(ya_lo[:, p, tt * P:(tt + 1) * P], one[1][:, P:2 * P],
                                ya_hi[:, p, tt * P:(tt + 1) * P].bitcast(f32), ALU.subtract).then_inc(yT_lo, 1)

                        for h in range(6):
                            if HALF_STEP[h] == u:
                                stage_out(dve, Num(i, 6, JOB_G + 3 + 3 * q + h // 2), h % 2)

            def gated(c):
                dve.wait_ge(z_silu, c + 1)
                TTs(mixb[:, 8 + c, :], mixb[:, 8 + c, :], z_sb[c][:, :], ALU.mult).then_inc(yb_made, 1)

            def gated_lo(c):
                dve.wait_ge(yb_h, c + 1)
                TTs(yb_lo[:, c, :], mixb[:, 8 + c, :], yb_hi[:, c, :].bitcast(f32), ALU.subtract).then_inc(yb_l, 1)

            gated(0)
            gated(1)
            gated(2)
            gated_lo(0)
            stage_out(dve, num(JOB_G + 15), 0)
            gated(3)
            for c in range(1, 4):
                gated_lo(c)
                if c == 1:
                    stage_out(dve, num(JOB_G + 15), 1)

            dve.wait_ge(spilled[1], spills(16))
            with dve.Fori(0, 4) as i:
                for q in range(2):
                    j, job = i * 2 + q, i * 4 + (JOB_M + 2 * q)
                    dve.drain()
                    dve.wait_ge(gate_sig, i * 4 + (2 * q + 1))
                    for half in range(2):
                        job_done(dve, job, half)
                        TTs(prod[0][:, half_of(half)], acc[half][:, :], gate_sb[q][0][:, half_of(half)], ALU.mult
                            ).then_inc(acc_read[half], 1)
                    dve.wait_ge(gate_sig, i * 4 + (2 * q + 2))
                    dve.wait_ge(spilled[0], spills(16))
                    for half in range(2):
                        cols = half_of(half)
                        job_done(dve, job + 1, half)
                        TTs(prod[1][:, cols], acc[half][:, :], gate_sb[q][1][:, cols], ALU.mult
                            ).then_inc(acc_read[half], 1)
                        dve.drain()
                        TTs(prod[0][:, cols], prod[0][:, cols], prod[1][:, cols], ALU.add).then_inc(merged_made, 1)
                    for half in range(2):
                        cols = half_of(half)
                        dve.wait_ge(mg_h, j * 2 + (half + 1))
                        TTs(mg_lo[:, j, cols], prod[0][:, cols], mg_hi[:, j, cols].bitcast(f32), ALU.subtract
                            ).then_inc(mg_l, 1)

            def residual(job, j, half):
                job_done(dve, job, half)
                TTs(x_sb[:, j, half_of(half)], x_sb[:, j, half_of(half)], acc[half][:, :], ALU.add
                    ).then_inc(acc_read[half], 1)

            for j in range(8):
                dve.wait_ge(x_loaded[j], 32)
                for half in range(2):
                    residual(JOB_O + j, j, half)
                dve.drain()
                for half in range(2):
                    residual_lo(dve, j, half, P_GFFN, 8)

            def group(i, reg, gpar, step):
                shift = 12 * step
                jobs = [lin(reg, shift, v) for v in ffn_jobs(i)[0]]
                downs = [lin(reg, shift, v) for v in ffn_jobs(i)[1]]
                for c in range(4):
                    tile_ = c // 2
                    dve.drain()
                    for half in range(2):
                        job_done(dve, jobs[c], half)
                        if c % 2 == 0:
                            TTs(tmp[half][:, :], acc[half][:, :], rstd[:, half_of(half)], ALU.mult
                                ).then_inc(acc_read[half], 1)
                        else:
                            dve.wait_ge(f_scaled, lin(reg, 4 * step, 4 * i + 2 * tile_ + half + 1))
                            TTs(tmp[2 + half][:, :], acc[half][:, :], tmp[half][:, :], ALU.mult
                                ).then_inc(acc_read[half], 1)
                    for half in range(2):
                        if c % 2:
                            dve.wait_ge(f_hi, lin(reg, 4 * step, 4 * i + 2 * tile_ + half + 1))
                            TTs(hid_lo[gpar][:, tile_, half_of(half)], tmp[2 + half][:, :],
                                hid_hi[gpar][:, tile_, half_of(half)].bitcast(f32), ALU.subtract).then_inc(f_lo, 1)
                        if downs:
                            residual(downs[2 * c], 2 * c, half)
                    if downs:
                        for half in range(2):
                            residual(downs[2 * c + 1], 2 * c + 1, half)

            dve.wait_ge(rstd_ready, 2)
            group(0, None, 0, 0)
            with dve.Fori(0, 4) as i:
                group(1, i, 1, 2)
                group(2, i, 0, 2)
            group(9, None, 1, 0)
            group(10, None, 0, 0)
            dve.drain()
            for j in range(9):
                if j < 8:
                    for half in range(2):
                        residual(JOB_T + j, j, half)
                if j:
                    for half in range(2):
                        residual_lo(dve, j - 1, half, P_GPLE, 24)
            for k in range(2):
                dve.wait_ge(p_hi, k + 1)
                TTs(hid_lo[1][:, k, :], p_raw[:, k, :], hid_hi[1][:, k, :].bitcast(f32), ALU.subtract
                    ).then_inc(p_lo, 1)

            def finish(j, half):
                STT(out_sb[:, j, half_of(half)], x_sb[:, j, half_of(half)], params[:, P_GFIN + j:P_GFIN + j + 1],
                    rstd[:, half_of(half)], ALU.mult, ALU.mult).then_inc(out_made, 1)

            dve.wait_ge(rstd_ready, 3)
            for m in range(16):
                j, half = m % 8, m // 8
                dve.drain()
                dve.wait_ge(acc_ready, 2 * (JOB_P + m) + 1)
                TTs(tmp[2 + m % 2][:, :], acc[0][:, :], rstd[:, half_of(half)], ALU.mult).then_inc(acc_read[0], 1)
                if m >= 11:
                    dve.wait_ge(rstd_ready, 4)
                    finish(m - 11, 0)
                dve.wait_ge(acc_ready, 2 * (JOB_P + m) + 2)
                dve.wait_ge(pg_sig, m + 1)
                TTs(tmp[2 + m % 2][:, :], acc[1][:, :], tmp[2 + m % 2][:, :], ALU.mult).then_inc(acc_read[1], 1)
                dve.drain()
                TTs(x_sb[:, j, half_of(half)], x_sb[:, j, half_of(half)], tmp[2 + m % 2][:, :], ALU.add
                    ).then_inc(x4_made, 1)
            for j in range(5, 8):
                finish(j, 0)
            dve.wait_ge(rstd_ready, 5)
            for j in range(8):
                finish(j, 1)

        @block.tensor
        def _(pe):
            mm, tr = nc.tensor.matmul, nc.tensor.transpose

            def l2_sums(n):
                idx = n.value
                pe.wait_ge(l2_sq, idx + 1)
                if not (isinstance(idx, int) and idx < 2):
                    pe.wait_ge(l2_ln, idx + -1)
                for half in range(2):
                    last = mm((pair_a, pair_b)[n.parity][:, half_of(half)], ones, sqv[n.parity][:, half_of(half)],
                              start=True, stop=True)
                last.then_inc(l2_sum, 1)

            def sum_x():
                pe.wait_ge(smalls_loaded, 16)
                pe.wait_ge(sq0_added, 8)
                stat_sum(pe, sumsq)

            project(pe, 0, ring(num(0)), hx, ALL, num(0), lambda n: pe.wait_ge(norm_lo, n + 1))
            for j in range(1, 7):
                project(pe, j, ring(num(j)), hx, ALL, num(j), None, sum_x if j == 1 else None)
                if j == 2:
                    pe.wait_ge(bd_rows_made, 1)
                    for t in range(TOK_TILES):
                        last = tr(one[0][:, t * 8:(t + 1) * 8], bd_rows[:, t * P:(t + 1) * P], ident[0:8, 0:8])
                    last.then_inc(bd_ready, 1)
                if j == 5:
                    pe.wait_ge(g_made, 1)
                    mm(one[1][:, 0:32], cum, g_log[:, :], start=True, stop=True)
                    mm(one[1][:, 32:64], chunk_ones, g_log[:, :], start=True, stop=True).then_inc(gc_ready, 1)
            for n in (num(7), num(8)):
                project(pe, n.value, ring(n), hx, ALL, n, None, lambda: l2_sums(n + -7))
            with pe.Fori(4, 6) as i:
                for c in range(2):
                    n = Num(i, 2, 1 + c)
                    project(pe, n.value, ring(n), hx, ALL, n, None, lambda: l2_sums(n + -7))
            def tile_cumulate(t):
                pe.wait_ge(gb_made, t + 1)
                for h in range(4):
                    last = mm(bank4(3)[:, h, :], gb[:, h, :], cum, start=True, stop=True)
                last.then_inc(gcb_ready, 1)

            n = num(BLK_A)
            fill(pe, [n], (0, 3))
            l2_sums(num(6))
            pe.wait_ge(l2_ln, 6)
            tile_cumulate(0)
            fill(pe, [n], (3, 12))
            pe.wait_ge(dtmp_made, 1)
            l2_sums(num(7))
            fill(pe, [n], (12, 16))
            pe.wait_ge(gc_made, 1)
            pe.wait_ge(gc_read, 2)
            pe.wait_ge(l2_ln, 8)

            def tile(t, last_tile):
                tok, jobs = ds(t * P, P), [tile_job(t, c) for c in range(2)]
                place = iter(fill_b)
                pe.wait_ge(tiles_in, t * 2 + 2)
                for h in range(4):
                    mm(bank4(1)[:, h, :], kn[:, h, :], kn[:, h, :], start=True, stop=True)
                pe.wait_ge(l2_done, 8)
                for h in range(4):
                    last = mm(bank4(2)[:, h, :], kn[:, h, :], mixb[:, 8 + h, tok], start=True, stop=True)
                last.then_inc(kk_ready, 1)
                fill(pe, jobs, next(place))
                pe.wait_ge(dtmp_made, t + 1)
                for h in range(4):
                    tr(bank4(3)[:, h, :], kn[:, h, :], ident)
                for h in range(4):
                    last = tr(bank4(4)[:, h, :], vn[:, h, :], ident)
                last.then_inc(tok_ready, 1)
                fill(pe, jobs, next(place))
                pe.wait_ge(vtok_made, t + 1)
                pe.wait_ge(tt0_made, t + 1)
                for h in range(4):
                    last = tr(bank4(5)[:, h, :], TT[:, h, :], ident)
                last.then_inc(t0_ready, 1)
                fill(pe, jobs, next(place))
                pe.wait_ge(t0_made, t + 1)
                def turn():
                    for h in range(4):
                        last = tr(bank4(2)[:, h, :], T[:, h, :], ident)
                    last.then_inc(tt_ready, 1)

                for n in range(5):
                    if n == 0:
                        pe.wait_ge(state_made, t * 2 + 1)
                        pe.wait_ge(keys_made, t + 1)
                    else:
                        pe.wait_ge(t_updated, t * 5 + n)
                    pe.wait_ge(aoff_made, t * 5 + (n + 1))
                    for h in range(4):
                        last = mm(bank4(0)[:, h, :], aoff[n][:, h, :], T[:, h, :], start=True, stop=True)
                    last.then_inc(n_ready, 1)
                    if n:
                        turn()
                    fill(pe, jobs, next(place))
                    if n:
                        pe.wait_ge(tt_updated, t * 5 + n)
                    pe.wait_ge(n_made, t * 5 + (n + 1))
                    for h in range(4):
                        last = mm(bank4(1)[:, h, :], TT[:, h, :], Ns[:, h, :], start=True, stop=True)
                    last.then_inc(tn_ready, 1)
                    fill(pe, jobs, next(place))
                pe.wait_ge(t_updated, t * 5 + 5)
                turn()
                fill(pe, jobs, next(place))
                pe.wait_ge(tt_updated, t * 5 + 5)
                for h in range(4):
                    last = mm(bank4(3)[:, h, :], gk[:, h, :], TT[:, h, :], start=True, stop=True)
                last.then_inc(wk_ready, 1)
                fill(pe, jobs, next(place))
                pe.wait_ge(nwk_made, t + 1)
                if not last_tile:
                    tile_cumulate(t + 1)
                pe.wait_ge(vtok_made, t + 1)
                for h in range(4):
                    mm(bank4(4)[:, h, :], TT[:, h, :], vtok[:, h, :], start=(h == 0), stop=False)
                for c in range(2):
                    r = slice(c * CHUNK, (c + 1) * CHUNK)
                    if c:
                        pe.wait_ge(state_made, t * 2 + 2)
                    for h in range(4):
                        last = mm(bank4(4)[r, h, :], nwk[:, h, r], state[c][:, h, :], start=False, stop=(h == 3))
                    last.then_inc(wv_ready, 1)
                    if c:
                        for h in range(4):
                            for d in range(2):
                                e = slice(d * CHUNK, (d + 1) * CHUNK)
                                mm(bank4(5)[:, h, e], state[d][:, h, :], qg[:, h, e],
                                   start=(h == 0 and d == 0), stop=False)
                    fill(pe, jobs, next(place))
                    pe.wait_ge(w_made, t * 2 + (c + 1))
                    if c == 0 or not last_tile:
                        for h in range(4):
                            last = mm(bank4(0)[:, h, :], kdec[r, h, :], w_[r, h, :], start=True, stop=True)
                        last.then_inc(ds_ready, 1)
                    if c == 0:
                        fill(pe, jobs, next(place))
                for h in range(4):
                    last = mm(bank4(5)[:, h, :], w_[:, h, :], pT_[:, h, :], start=False, stop=(h == 3))
                last.then_inc(o_ready, 1)

            with pe.Fori(0, TOK_TILES - 1) as t:
                tile(t, False)
            tile(TOK_TILES - 1, True)

            jobs = [num(JOB_G + 1), num(JOB_G + 2)]
            pe.wait_ge(o_made, 8)
            pe.wait_ge(state_made, 16)
            for c in range(4):
                if c % 2 == 0:
                    fill(pe, jobs, (0, 8) if c == 0 else (8, 24))
                pe.wait_ge(o_sq, c + 1)
                if c >= 2:
                    pe.wait_ge(o_ln, c - 1)
                for half in range(2):
                    last = mm((pair_a, pair_b)[c % 2][:, half_of(half)], ones, osq[c % 2][:, half_of(half)],
                              start=True, stop=True)
                last.then_inc(o_sum, 1)
            fill(pe, jobs, (24, 32))
            pe.wait_ge(o_ln, 4)

            with pe.Fori(0, 2) as i:
                for q in range(2):
                    p = i * 2 + q
                    base = p * 16
                    jobs = [Num(i, 6, JOB_G + 3 + 3 * q + c) for c in range(3)]
                    pe.wait_ge(qkv_loaded, p * 48 + 48)
                    for tt in range(8):
                        last = tr(pair_b[:, tt * P:(tt + 1) * P], va[:, tt * P:(tt + 1) * P], ident)
                    last.then_inc(vt_ready, 1)
                    for u in range(19):
                        if u < 16:
                            tt, r = u // 2, slice(64 * (u % 2), 64 * (u % 2) + 64)
                            tiles = min(tt + 1, 5)
                            k0, width = (tt + 1 - tiles) * P, tiles * P
                            if u:
                                pe.wait_ge(sc_read, base + u)
                            for a in range(0, width, HALF):
                                e = min(width, a + HALF)
                                last = mm(pair_a[:, a:e], qa[q][r, tt * P:(tt + 1) * P], ka[q][r, k0 + a:k0 + e],
                                          start=True, stop=True)
                            last.then_inc(sc_ready, 1)
                        fill(pe, jobs, fill_a[u])
                        if 1 <= u < 17:
                            v = u - 1
                            tiles = min(v // 2 + 1, 5)
                            if u == 1:
                                pe.wait_ge(vt_made, p + 1)
                            pe.wait_ge(pr_made, base + u)
                            if v:
                                pe.wait_ge(prT_made, base + v)
                            for kt in range(tiles):
                                last = tr(pair_b[:, kt * P:(kt + 1) * P], pr[v % 2][:, kt * P:(kt + 1) * P], ident)
                            last.then_inc(prT_ready, 1)
                        if u >= 4 and u % 2 == 0:
                            tt = (u - 4) // 2
                            pe.wait_ge(ya_norm, base + (2 * tt + 2))
                            tr(one[1][:, P:2 * P], ytok[tt % 2][:, :], ident).then_inc(yT_ready, 1)
                        if 2 <= u < 18:
                            v = u - 2
                            tt, r = v // 2, slice(64 * (v % 2), 64 * (v % 2) + 64)
                            tiles = min(tt + 1, 5)
                            pe.wait_ge(prT_made, base + (v + 1))
                            if v >= 2 and v % 2:
                                pe.wait_ge(yT_lo, p * 8 + tt)
                            elif v >= 2:
                                pe.wait_ge(ya_norm, base + (v - 1))
                            for kt in range(tiles):
                                last = mm(one[v % 2][:, 0:64], prT[v % 2][:, kt * P:(kt + 1) * P],
                                          va_tok[:, tt + 1 - tiles + kt, r], start=(kt == 0), stop=(kt == tiles - 1))
                            last.then_inc(oa_ready, 1)

            project(pe, JOB_G + 15, ring(num(JOB_G + 15)), hx, ALL, num(JOB_G + 15))

            pe.wait_ge(yT_lo, 32)
            with pe.Fori(0, 4) as i:
                for q in range(2):
                    n, job = Num(i, 2, BLK_M + q), i * 4 + (JOB_M + 2 * q)
                    project(pe, job, ring(n), (ya_hi, ya_lo), [(k, k) for k in range(4)], n)
                    pe.wait_ge(yb_l, 4)
                    project(pe, job + 1, ring(n), (yb_hi, yb_lo), [(4 + k, k) for k in range(4)])
            for j in range(8):
                project(pe, JOB_O + j, ring(num(BLK_O + j)), mgx, ALL, num(BLK_O + j),
                        (lambda n: pe.wait_ge(mg_l, 2 * n + 2)) if j == 0 else None)

            def residual_in(k, count):
                if k == 7:
                    sum_residual(count)
                pe.wait_ge(norm_lo, count - 8 + 2 * k + 2)

            def final_sum(half):
                pe.wait_ge(sq_added, 40 if half == 0 else 47)
                last = mm(pair_a[:, half_of(half)], ones, sumsq2[:, half_of(half)], start=True, stop=(half == 0))
                if half:
                    pe.wait_ge(sq_made, 48)
                    last = mm(pair_a[:, half_of(half)], ones, tmp[1][:, :], start=False, stop=True)
                last.then_inc(stat_ready, 1)

            def sum_residual(count):
                pe.wait_ge(sq_added, count)
                stat_sum(pe, sumsq2)

            def group(i, reg, gpar, step):
                shift = 12 * step
                jobs = [lin(reg, shift, v) for v in ffn_jobs(i)[0]]
                downs = [lin(reg, shift, v) for v in ffn_jobs(i)[1]]
                n = Num(reg, 6 * step, BLK_F + 6 * i)
                for c in range(4):
                    wait = (lambda k: residual_in(k, 16)) if i == 0 and reg is None and c == 0 else None
                    project(pe, jobs[c], ring(n + c), h2x, ALL, n + c, wait)
                    if downs:
                        if c == 0:
                            pe.wait_ge(f_lo, lin(reg, 4 * step, 4 * i))
                        for j in (2 * c, 2 * c + 1):
                            project(pe, downs[j], down_w(1 - gpar, j), (hid_hi[1 - gpar], hid_lo[1 - gpar]),
                                    [(0, 0), (1, 1)])

            group(0, None, 0, 0)
            with pe.Fori(0, 4) as i:
                group(1, i, 1, 2)
                group(2, i, 0, 2)
            group(9, None, 1, 0)
            group(10, None, 0, 0)
            pe.wait_ge(f_lo, 4 * GROUPS)
            pe.wait_ge(lo_made, BLK_F + 6 * GROUPS)
            for j in range(8):
                project(pe, JOB_T + j, down_w(0, j), (hid_hi[0], hid_lo[0]), [(0, 0), (1, 1)])
            for m in range(16):
                half = m // 8
                wait = (lambda k: residual_in(k, 32)) if m == 0 else None
                project_half(pe, JOB_P + m, ring(num(ple_block(m))), h2x, ALL, 0, half, num(ple_block(m)), wait)
                if m == 9:
                    final_sum(0)
                if m == 0:
                    pe.wait_ge(lo_made, BLK_P + 3)
                    pe.wait_ge(p_lo, 2)
                project_half(pe, JOB_P + m, down_w(1, m % 8), (hid_hi[1], hid_lo[1]), [(0, 0), (1, 1)], 1, half)
            final_sum(1)


def constants():
    c = np.zeros((P, N_CONST), np.float32)
    j, i = np.arange(P)[:, None], np.arange(P)[None, :]
    same = j // CHUNK == i // CHUNK
    c[:, C_IDENT:C_IDENT + P] = j == i
    c[:, C_ONES:C_ONES + P] = 1.0
    c[:, C_CUM:C_CUM + P] = same & (j <= i)
    c[:, C_CHUNK:C_CHUNK + P] = same
    c[:, C_MASK:C_MASK + P] = np.where(same & (j <= i), 0.0, NEG)
    for n, b in enumerate(LEVELS):
        c[:, C_LEVEL + P * n:C_LEVEL + P * (n + 1)] = (j // (2 * b) == i // (2 * b)) & (i % (2 * b) >= b) & (j % (2 * b) < b)
    c[:, C_EPS] = EPS
    c[:, C_QKS:C_QKS + 8] = 1.0
    c[:, C_QKS + 8:C_QKS + 12] = B_DIM ** -0.5
    return c


def kernel(**inputs):
    import concourse.bacc as bacc
    from concourse.bass_utils import run_bass_kernel_spmd

    a = {k: np.asarray(v) for k, v in inputs.items()}
    f = np.float32
    w_in = a["w_in"][0]
    aw, qkv = A_HEADS * A_DIM, B_HEADS * B_DIM

    def col_blocks(w):
        k, n = w.shape[0] // P, w.shape[1] // P
        return w.reshape(k, P, n, P).transpose(2, 1, 0, 3).reshape(n, P, k * P)

    qa, ka, va = (col_blocks(w_in[:, aw * n:aw * (n + 1)]) for n in range(3))
    o = 3 * aw
    qb, kb, vb, z = (col_blocks(w_in[:, o + qkv * n:o + qkv * (n + 1)]) for n in range(4))
    o += 4 * qkv
    wbd = np.zeros((D, P), f)
    wbd[:, :8] = w_in[:, o:o + 8]
    ga, gb = col_blocks(w_in[:, o + 8:o + 8 + D]), col_blocks(w_in[:, o + 8 + D:o + 8 + 2 * D])
    wa, wb = col_blocks(a["w_branch_a"][0]), col_blocks(a["w_branch_b"][0])
    gate, up = col_blocks(a["w_gate_up"][0][:, :D_FF]), col_blocks(a["w_gate_up"][0][:, D_FF:])
    down = a["w_down"][0].reshape(D_FF // P, P, D)
    parts = [col_blocks(wbd), vb, kb, qb, np.stack([qa, ka, va], 1), z,
             np.stack([ga, gb], 1), np.concatenate([wa, wb], 2), col_blocks(a["w_out"][0])]
    for g in range(GROUPS):
        parts += [gate[2 * g], up[2 * g], gate[2 * g + 1], up[2 * g + 1], down[2 * g], down[2 * g + 1]]
    ple = col_blocks(a["w_ple_gate"][0])
    parts += [ple[:1], a["w_ple_proj"][0].reshape(2, P, D), ple[1:], ple]
    blocks = np.concatenate([x.reshape(-1, P, D) for x in parts]).astype(f, copy=False)
    assert blocks.shape[0] == N_BLK

    params = np.zeros((P, N_PARAM), f)
    for c, g in ((P_GMIX, a["g_mix"][0]), (P_GFFN, a["g_ffn"][0]), (P_GPLE, a["g_ple"][0]), (P_GFIN, a["g_final"])):
        params[:, c:c + 8] = g.reshape(8, P).T
    cw = a["conv_w"][0].reshape(CONV, 3, B_HEADS, P)[:, ::-1]
    params[:, P_CONV:P_CONV + 12 * CONV] = cw.reshape(CONV, 12, P).transpose(2, 1, 0).reshape(P, 48)
    params[:, P_ONORM] = a["w_onorm"][0]
    params[:, P_ALOG:P_ALOG + 4] = a["a_log"][0][None]
    params[:, P_DTB:P_DTB + 4] = a["dt_bias"][0][None]

    qi, kj = np.arange(P)[:, None], np.arange(WINDOW)[None, :]
    idx = np.clip(WINDOW - P + qi - kj, -REL_CLIP, REL_CLIP) + REL_CLIP
    chunks = kj // CHUNK - qi // CHUNK
    bias = np.where((chunks >= 0) & (chunks <= LOOKBACK), a["rel_bias"][0][:, idx], f(NEG)).astype(f, copy=False)

    x_t = np.ascontiguousarray(a["x"][0].T).reshape(8, P, S)
    p_t = np.ascontiguousarray(a["p"][0, 0].T).reshape(2, P, S)
    arrays = {"x_t": x_t, "p_t": p_t, "blocks": blocks, "consts": constants(), "params": params, "bias": bias}
    nc = bacc.Bacc("TRN2", target_bir_lowering=False, num_devices=1)
    aps = [nc.dram_tensor(n, v.shape, mybir.dt.float32, kind="ExternalInput").ap() for n, v in arrays.items()]
    aps.append(nc.dram_tensor("out_t", (8, P, S), mybir.dt.float32, kind="ExternalOutput").ap())
    aps.append(nc.dram_tensor("spill", (JOB_M - JOB_A, P, S), mybir.dt.float32, kind="Internal").ap())
    hybrid_block(nc, *aps)
    r = run_bass_kernel_spmd(nc, [arrays], core_ids=[0])
    return np.ascontiguousarray(r.results[0]["out_t"].reshape(D, S).T).reshape(1, S, D)
```
